# Optimizing a Trainium2 kernel written in Bass

```python
import math
import jax
import jax.numpy as jnp
from jax import lax
import numpy as np
import jax, jax.numpy as jnp

D_MODEL = 1024
BATCH = 1
SEQ = 256
DEPTH = 2

N_EVEN = (DEPTH + 1) // 2
N_ODD = DEPTH // 2

DIFF_HEADS = 4
DIFF_QK_DIM = 64
DIFF_V_DIM = 2 * DIFF_QK_DIM
ATTN_Q_BLOCK = 128
MOBA_HEADS = 4
MOBA_HEAD_DIM = 128
MOBA_BLOCK = 256
MOBA_TOPK = 3
MOBA_Q_CHUNK = 64
DIFF_QK_W = DIFF_HEADS * 2 * DIFF_QK_DIM
DIFF_V_W = DIFF_HEADS * DIFF_V_DIM
MOBA_W = MOBA_HEADS * MOBA_HEAD_DIM
HY_IN_W = 2 * DIFF_QK_W + DIFF_V_W + 3 * MOBA_W
HY_MIX_W = DIFF_V_W + MOBA_W
GLA_HEADS = 4
GLA_K_W = D_MODEL // 2
GLA_V_W = D_MODEL
GLA_DK = GLA_K_W // GLA_HEADS
GLA_DV = GLA_V_W // GLA_HEADS
GLA_GATE_RANK = 16
GLA_GATE_NORM = 16.0
GLA_CHUNK = 64
GLA_IN_W = 2 * GLA_K_W + 2 * GLA_V_W + GLA_GATE_RANK
D_FF = 4 * D_MODEL
ROPE_THETA = 10000.0
LN_EPS = 1e-5
RMS_EPS = 1e-5
DEEPNORM_ALPHA = (2 * DEPTH) ** 0.25
DEEPNORM_BETA = (8 * DEPTH) ** -0.25


def layer_norm(x, g, b):
    xf = x.astype(jnp.float32)
    mu = jnp.mean(xf, axis=-1, keepdims=True)
    var = jnp.mean(jnp.square(xf - mu), axis=-1, keepdims=True)
    return (((xf - mu) * lax.rsqrt(var + LN_EPS)) * g + b).astype(x.dtype)

def rms_norm(x, g):
    xf = x.astype(jnp.float32)
    y = xf * lax.rsqrt(jnp.mean(jnp.square(xf), axis=-1, keepdims=True) + RMS_EPS)
    return (y * g).astype(x.dtype)

def rope_tables(seq, dim):
    inv = 1.0 / (ROPE_THETA ** (jnp.arange(0, dim, 2, dtype=jnp.float32) / dim))
    ang = jnp.arange(seq, dtype=jnp.float32)[:, None] * inv[None, :]
    return jnp.cos(ang), jnp.sin(ang)

def apply_rope(x, cos, sin):
    x1, x2 = jnp.split(x, 2, axis=-1)
    c = cos.astype(x.dtype)
    s = sin.astype(x.dtype)
    return jnp.concatenate([x1 * c - x2 * s, x2 * c + x1 * s], axis=-1)

def diff_attention(q, k, v, lam, subln, lambda_init):
    Bn, H, _, S, dq = q.shape
    scale = dq ** -0.5
    lf = lam.astype(jnp.float32)
    lam_full = jnp.exp(jnp.sum(lf[0] * lf[1])) - jnp.exp(jnp.sum(lf[2] * lf[3])) + lambda_init
    nq = S // ATTN_Q_BLOCK
    qb = q.reshape(Bn, H, 2, nq, ATTN_Q_BLOCK, dq).transpose(3, 0, 1, 2, 4, 5)
    kpos = jnp.arange(S)

    def block(args):
        qi, i = args
        s = jnp.einsum('bhmqd,bhmkd->bhmqk', qi, k).astype(jnp.float32) * scale
        qpos = i * ATTN_Q_BLOCK + jnp.arange(ATTN_Q_BLOCK)
        s = jnp.where(kpos[None, :] <= qpos[:, None], s, -jnp.inf)
        p = jax.nn.softmax(s, axis=-1)
        w = p[:, :, 0] - lam_full * p[:, :, 1]
        return jnp.einsum('bhqk,bhkd->bhqd', w.astype(v.dtype), v)

    o = lax.map(block, (qb, jnp.arange(nq)))
    o = o.transpose(1, 2, 0, 3, 4).reshape(Bn, H, S, v.shape[-1])
    return rms_norm(o, subln) * (1.0 - lambda_init)

def moba_attention(q, k, v):
    Bn, H, S, d = q.shape
    scale = d ** -0.5
    s_pad = -(-S // MOBA_BLOCK) * MOBA_BLOCK
    pad = ((0, 0), (0, 0), (0, s_pad - S), (0, 0))
    q, k, v = jnp.pad(q, pad), jnp.pad(k, pad), jnp.pad(v, pad)
    nb = s_pad // MOBA_BLOCK
    topk = min(MOBA_TOPK, nb)
    kb = k.reshape(Bn, H, nb, MOBA_BLOCK, d)
    vb = v.reshape(Bn, H, nb, MOBA_BLOCK, d)
    kmean = jnp.mean(kb, axis=3)
    nc = s_pad // MOBA_Q_CHUNK
    qc = q.reshape(Bn, H, nc, MOBA_Q_CHUNK, d).transpose(2, 0, 1, 3, 4)
    gather = jax.vmap(jax.vmap(lambda blocks, idx: blocks[idx]))
    blk_ids = jnp.arange(nb)

    def chunk(args):
        qi, c = args
        start = c * MOBA_Q_CHUNK
        own = start // MOBA_BLOCK
        qpos = start + jnp.arange(MOBA_Q_CHUNK)
        gate = jnp.einsum('bhqd,bhnd->bhqn', qi, kmean).astype(jnp.float32)
        gate = jnp.where(blk_ids < own, gate, -jnp.inf)
        _, sel = lax.top_k(gate, topk)
        sel_valid = sel < own
        ks = gather(kb, sel)
        vs = gather(vb, sel)
        s_sel = jnp.einsum('bhqd,bhqnld->bhqnl', qi, ks).astype(jnp.float32) * scale
        s_sel = jnp.where(sel_valid[..., None], s_sel, -jnp.inf).reshape(Bn, H, MOBA_Q_CHUNK, topk * MOBA_BLOCK)
        k_own = lax.dynamic_index_in_dim(kb, own, axis=2, keepdims=False)
        v_own = lax.dynamic_index_in_dim(vb, own, axis=2, keepdims=False)
        s_own = jnp.einsum('bhqd,bhld->bhql', qi, k_own).astype(jnp.float32) * scale
        kpos = own * MOBA_BLOCK + jnp.arange(MOBA_BLOCK)
        s_own = jnp.where(kpos[None, :] <= qpos[:, None], s_own, -jnp.inf)
        p = jax.nn.softmax(jnp.concatenate([s_sel, s_own], axis=-1), axis=-1).astype(v.dtype)
        p_sel = p[..., :topk * MOBA_BLOCK].reshape(Bn, H, MOBA_Q_CHUNK, topk, MOBA_BLOCK)
        p_own = p[..., topk * MOBA_BLOCK:]
        return (jnp.einsum('bhqnl,bhqnld->bhqd', p_sel, vs)
                + jnp.einsum('bhql,bhld->bhqd', p_own, v_own))

    o = lax.map(chunk, (qc, jnp.arange(nc)))
    o = o.transpose(1, 2, 0, 3, 4).reshape(Bn, H, s_pad, d)
    return o[:, :, :S]

def gla_chunked(q, k, v, g):
    dtype = v.dtype
    Bn, H, S, dk = q.shape
    dv = v.shape[-1]
    L = GLA_CHUNK
    nc = S // L
    f32 = jnp.float32

    def to_chunks(t):
        return t.astype(f32).reshape(Bn, H, nc, L, t.shape[-1]).transpose(2, 0, 1, 3, 4)

    qc, kc, vc, gc = to_chunks(q * dk ** -0.5), to_chunks(k), to_chunks(v), to_chunks(g)
    causal = jnp.tril(jnp.ones((L, L), dtype=bool))[None, None, :, :, None]

    def step(state, inp):
        qi, ki, vi, gi = inp
        b = jnp.cumsum(gi, axis=2)
        o_inter = jnp.einsum('bhlk,bhkv->bhlv', qi * jnp.exp(b), state)
        rel = jnp.where(causal, b[:, :, :, None, :] - b[:, :, None, :, :], -jnp.inf)
        att = jnp.einsum('bhik,bhijk,bhjk->bhij', qi, jnp.exp(rel), ki)
        o_intra = jnp.einsum('bhij,bhjv->bhiv', att, vi)
        b_last = b[:, :, -1:, :]
        state = (jnp.exp(b_last[:, :, 0, :, None]) * state
                 + jnp.einsum('bhjk,bhjv->bhkv', ki * jnp.exp(b_last - b), vi))
        return state, o_inter + o_intra

    state0 = jnp.zeros((Bn, H, dk, dv), f32)
    _, o = lax.scan(step, state0, (qc, kc, vc, gc))
    return o.transpose(1, 2, 0, 3, 4).reshape(Bn, H, S, dv).astype(dtype)

def split_heads(t, n, d):
    Bn, S, _ = t.shape
    return t.reshape(Bn, S, n, d).transpose(0, 2, 1, 3)

def merge_heads(t):
    Bn, H, S, d = t.shape
    return t.transpose(0, 2, 1, 3).reshape(Bn, S, H * d)

def diff_moba_mixer(x, w_in, lam, subln, w_out, lambda_init, rope_d, rope_m):
    Bn, S, _ = x.shape
    h = x @ w_in
    o1 = DIFF_QK_W
    o2 = o1 + DIFF_QK_W
    o3 = o2 + DIFF_V_W
    o4 = o3 + MOBA_W
    o5 = o4 + MOBA_W

    def two_maps(t):
        return t.reshape(Bn, S, DIFF_HEADS, 2, DIFF_QK_DIM).transpose(0, 2, 3, 1, 4)

    dq = apply_rope(two_maps(h[..., :o1]), *rope_d)
    dk = apply_rope(two_maps(h[..., o1:o2]), *rope_d)
    dv = split_heads(h[..., o2:o3], DIFF_HEADS, DIFF_V_DIM)
    mq = apply_rope(split_heads(h[..., o3:o4], MOBA_HEADS, MOBA_HEAD_DIM), *rope_m)
    mk = apply_rope(split_heads(h[..., o4:o5], MOBA_HEADS, MOBA_HEAD_DIM), *rope_m)
    mv = split_heads(h[..., o5:], MOBA_HEADS, MOBA_HEAD_DIM)
    a = diff_attention(dq, dk, dv, lam, subln, lambda_init)
    b = moba_attention(mq, mk, mv)
    return jnp.concatenate([merge_heads(a), merge_heads(b)], axis=-1) @ w_out

def gla_mixer(x, w_in, w_gate_up, b_gate, norm_g, w_out):
    h = x @ w_in
    o1 = GLA_K_W
    o2 = o1 + GLA_K_W
    o3 = o2 + GLA_V_W
    o4 = o3 + GLA_V_W
    q = split_heads(h[..., :o1], GLA_HEADS, GLA_DK)
    k = split_heads(h[..., o1:o2], GLA_HEADS, GLA_DK)
    v = split_heads(h[..., o2:o3], GLA_HEADS, GLA_DV)
    r = h[..., o3:o4]
    g = jax.nn.log_sigmoid((h[..., o4:] @ w_gate_up + b_gate).astype(jnp.float32)) / GLA_GATE_NORM
    g = split_heads(g, GLA_HEADS, GLA_DK)
    o = rms_norm(gla_chunked(q, k, v, g), norm_g)
    return (merge_heads(o) * jax.nn.silu(r)) @ w_out

def sqrelu_mlp(x, w1, w2):
    return jnp.square(jax.nn.relu(x @ w1)) @ w2

def first_inputs(seed: int = 0) -> dict:
    key = jax.random.key(seed)
    ks = jax.random.split(key, 17)

    def normal(k, shape, scale):
        return jax.random.normal(k, shape, jnp.float32) * scale

    return {
        'x': normal(ks[0], (BATCH, SEQ, D_MODEL), 1.0),
        'hy_w_in': normal(ks[1], (N_EVEN, D_MODEL, HY_IN_W), D_MODEL ** -0.5),
        'diff_lambda': normal(ks[2], (N_EVEN, 4, DIFF_QK_DIM), 0.1),
        'diff_subln': 1.0 + normal(ks[3], (N_EVEN, DIFF_V_DIM), 0.02),
        'hy_w_out': normal(ks[4], (N_EVEN, HY_MIX_W, D_MODEL), HY_MIX_W ** -0.5 * DEEPNORM_BETA),
        'gla_w_in': normal(ks[5], (N_ODD, D_MODEL, GLA_IN_W), D_MODEL ** -0.5),
        'gla_w_gate_up': normal(ks[6], (N_ODD, GLA_GATE_RANK, GLA_K_W), GLA_GATE_RANK ** -0.5),
        'gla_b_gate': normal(ks[7], (N_ODD, GLA_K_W), 0.02),
        'gla_norm': 1.0 + normal(ks[8], (N_ODD, GLA_DV), 0.02),
        'gla_w_out': normal(ks[9], (N_ODD, GLA_V_W, D_MODEL), GLA_V_W ** -0.5 * DEEPNORM_BETA),
        'ln_mix_g': 1.0 + normal(ks[10], (DEPTH, D_MODEL), 0.02),
        'ln_mix_b': normal(ks[11], (DEPTH, D_MODEL), 0.02),
        'ffn_w1': normal(ks[12], (DEPTH, D_MODEL, D_FF), D_MODEL ** -0.5),
        'ffn_w2': normal(ks[13], (DEPTH, D_FF, D_MODEL), D_FF ** -0.5 * DEEPNORM_BETA),
        'ln_ffn_g': 1.0 + normal(ks[14], (DEPTH, D_MODEL), 0.02),
        'ln_ffn_b': normal(ks[15], (DEPTH, D_MODEL), 0.02),
    }

def first_block(x, hy_w_in, diff_lambda, diff_subln, hy_w_out, gla_w_in, gla_w_gate_up,
              gla_b_gate, gla_norm, gla_w_out, ln_mix_g, ln_mix_b, ffn_w1, ffn_w2,
              ln_ffn_g, ln_ffn_b):
    S = x.shape[1]
    rope_d = rope_tables(S, DIFF_QK_DIM)
    rope_m = rope_tables(S, MOBA_HEAD_DIM)
    for l in range(DEPTH):
        if l % 2 == 0:
            e = l // 2
            lambda_init = 0.8 - 0.6 * math.exp(-0.3 * l)
            mix = diff_moba_mixer(x, hy_w_in[e], diff_lambda[e], diff_subln[e], hy_w_out[e],
                                  lambda_init, rope_d, rope_m)
        else:
            o = l // 2
            mix = gla_mixer(x, gla_w_in[o], gla_w_gate_up[o], gla_b_gate[o], gla_norm[o], gla_w_out[o])
        x = layer_norm(DEEPNORM_ALPHA * x + mix, ln_mix_g[l], ln_mix_b[l])
        x = layer_norm(DEEPNORM_ALPHA * x + sqrelu_mlp(x, ffn_w1[l], ffn_w2[l]), ln_ffn_g[l], ln_ffn_b[l])
    return x


N_MIXERS = 2
N_ATTN_LAYERS = (DEPTH + 1) // 2
N_POOL_LAYERS = DEPTH // 2
GRID_W = 64
EPS = 1e-6

HEAD_DIM = 64
N_HEADS = D_MODEL // HEAD_DIM
N_KV_HEADS = 4
GQA_GROUP = N_HEADS // N_KV_HEADS
Q_BLOCK = 128
ROPE_PAIRS = HEAD_DIM // 4
QKV_DIM = (N_HEADS + 2 * N_KV_HEADS) * HEAD_DIM

POOL_WINDOWS = (2, 4, 8, 16)
N_POOL_GROUPS = len(POOL_WINDOWS)
POOL_GROUP_W = D_MODEL // N_POOL_GROUPS

MEM_LEN = 256
X_HEADS = 4
X_HEAD_DIM = D_MODEL // X_HEADS

D_FF_2 = 2816
CONV_W = 3


def rmsnorm(x, gain):
    x32 = x.astype(jnp.float32)
    y = x32 * lax.rsqrt(jnp.mean(x32 * x32, axis=-1, keepdims=True) + EPS)
    return (y * gain.astype(jnp.float32)).astype(x.dtype)

def axial_rope_tables(seq_len):
    n_rows = seq_len // GRID_W
    row = jnp.repeat(jnp.arange(n_rows, dtype=jnp.float32), GRID_W)
    col = jnp.tile(jnp.arange(GRID_W, dtype=jnp.float32), n_rows)
    inv_freq = ROPE_THETA ** (-jnp.arange(ROPE_PAIRS, dtype=jnp.float32) / ROPE_PAIRS)
    ang = jnp.stack([row[:, None] * inv_freq, col[:, None] * inv_freq], axis=1)
    return jnp.cos(ang), jnp.sin(ang)

def apply_axial_rope(x, cos, sin):
    b, s, h, d = x.shape
    xs = x.astype(jnp.float32).reshape(b, s, h, 2, 2, ROPE_PAIRS)
    x1, x2 = xs[..., 0, :], xs[..., 1, :]
    c = cos[None, :, None]
    sn = sin[None, :, None]
    out = jnp.stack([x1 * c - x2 * sn, x2 * c + x1 * sn], axis=-2)
    return out.reshape(b, s, h, d).astype(x.dtype)

def axial_gqa_attention(h, w_qkv, q_gain, k_gain, w_o):
    b, s, _ = h.shape
    qkv = h @ w_qkv
    q_end = N_HEADS * HEAD_DIM
    k_end = q_end + N_KV_HEADS * HEAD_DIM
    q = qkv[..., :q_end].reshape(b, s, N_HEADS, HEAD_DIM)
    k = qkv[..., q_end:k_end].reshape(b, s, N_KV_HEADS, HEAD_DIM)
    v = qkv[..., k_end:].reshape(b, s, N_KV_HEADS, HEAD_DIM)
    q = rmsnorm(q, q_gain)
    k = rmsnorm(k, k_gain)
    cos, sin = axial_rope_tables(s)
    q = apply_axial_rope(q, cos, sin) * (HEAD_DIM ** -0.5)
    k = apply_axial_rope(k, cos, sin)
    n_blk = s // Q_BLOCK
    qb = q.reshape(b, n_blk, Q_BLOCK, N_KV_HEADS, GQA_GROUP, HEAD_DIM).transpose(1, 0, 3, 4, 2, 5)
    kt = k.transpose(0, 2, 1, 3)
    vt = v.transpose(0, 2, 1, 3)

    def attend_block(q_blk):
        scores = jnp.einsum('bkgqd,bksd->bkgqs', q_blk, kt).astype(jnp.float32)
        p = jax.nn.softmax(scores, axis=-1).astype(vt.dtype)
        return jnp.einsum('bkgqs,bksd->bkgqd', p, vt)

    o = lax.map(attend_block, qb)
    o = o.transpose(1, 0, 4, 2, 3, 5).reshape(b, s, N_HEADS * HEAD_DIM)
    return o @ w_o

def multiscale_pool_mixer(h, w_grp, scale):
    b, s, d = h.shape
    hg = h.astype(jnp.float32).reshape(b, s, N_POOL_GROUPS, POOL_GROUP_W)
    csum = jnp.concatenate(
        [jnp.zeros((b, 1, N_POOL_GROUPS, POOL_GROUP_W), jnp.float32), jnp.cumsum(hg, axis=1)], axis=1)
    t = jnp.arange(s)[:, None]
    win = jnp.array(POOL_WINDOWS, dtype=jnp.int32)[None, :]
    lo = jnp.clip(t - win // 2, 0, s)
    hi = jnp.clip(t + win - win // 2, 0, s)
    s_hi = jnp.take_along_axis(csum, hi[None, :, :, None], axis=1)
    s_lo = jnp.take_along_axis(csum, lo[None, :, :, None], axis=1)
    count = (hi - lo).astype(jnp.float32)[None, :, :, None]
    mixed = (s_hi - s_lo) / count - hg
    y = jnp.einsum('bsgc,gcd->bsgd', mixed, w_grp.astype(jnp.float32)).reshape(b, s, d)
    return (y * scale.astype(jnp.float32)).astype(h.dtype)

def memory_cross_attention(h, mem_n, w_q, w_kv, w_o):
    b, s, _ = h.shape
    m = mem_n.shape[1]
    q = (h @ w_q).reshape(b, s, X_HEADS, X_HEAD_DIM) * (X_HEAD_DIM ** -0.5)
    kv = mem_n @ w_kv
    k = kv[..., :D_MODEL].reshape(b, m, X_HEADS, X_HEAD_DIM)
    v = kv[..., D_MODEL:].reshape(b, m, X_HEADS, X_HEAD_DIM)
    scores = jnp.einsum('bshd,bmhd->bhsm', q, k).astype(jnp.float32)
    p = jax.nn.softmax(scores, axis=-1).astype(v.dtype)
    o = jnp.einsum('bhsm,bmhd->bshd', p, v).reshape(b, s, D_MODEL)
    return o @ w_o

def conv_gated_ffn(h, w_up, conv_w, conv_b, w_down):
    u = h @ w_up
    up = jnp.pad(u, ((0, 0), (1, 1), (0, 0)))
    u = up[:, :-2] * conv_w[0] + up[:, 1:-1] * conv_w[1] + up[:, 2:] * conv_w[2] + conv_b
    gate, val = u[..., :D_FF_2], u[..., D_FF_2:]
    return (jax.nn.silu(gate) * val) @ w_down

def second_inputs(seed: int = 0) -> dict:
    key = jax.random.key(seed)
    ks = jax.random.split(key, 24)
    f32 = jnp.float32

    def nrm(k, shape, scale):
        return jax.random.normal(k, shape, f32) * scale

    def gain(k, shape):
        return 1.0 + 0.05 * jax.random.normal(k, shape, f32)

    na, nb = N_ATTN_LAYERS, N_POOL_LAYERS
    return {
        "x": nrm(ks[0], (BATCH, SEQ, D_MODEL), 1.0),
        "mem": nrm(ks[1], (BATCH, MEM_LEN, D_MODEL), 1.0),
        "attn_norm": gain(ks[2], (na, D_MODEL)),
        "attn_w_qkv": nrm(ks[3], (na, D_MODEL, QKV_DIM), D_MODEL ** -0.5),
        "attn_q_gain": gain(ks[4], (na, HEAD_DIM)),
        "attn_k_gain": gain(ks[5], (na, HEAD_DIM)),
        "attn_w_o": nrm(ks[6], (na, N_HEADS * HEAD_DIM, D_MODEL), (N_HEADS * HEAD_DIM) ** -0.5),
        "pool_norm": gain(ks[7], (nb, D_MODEL)),
        "pool_w": nrm(ks[8], (nb, N_POOL_GROUPS, POOL_GROUP_W, POOL_GROUP_W), POOL_GROUP_W ** -0.5),
        "pool_scale": gain(ks[9], (nb, D_MODEL)),
        "xattn_norm": gain(ks[10], (DEPTH, D_MODEL)),
        "mem_norm": gain(ks[11], (DEPTH, D_MODEL)),
        "xattn_w_q": nrm(ks[12], (DEPTH, D_MODEL, D_MODEL), D_MODEL ** -0.5),
        "xattn_w_kv": nrm(ks[13], (DEPTH, D_MODEL, 2 * D_MODEL), D_MODEL ** -0.5),
        "xattn_w_o": nrm(ks[14], (DEPTH, D_MODEL, D_MODEL), D_MODEL ** -0.5),
        "ffn_norm": gain(ks[15], (DEPTH, D_MODEL)),
        "ffn_w_up": nrm(ks[16], (DEPTH, D_MODEL, 2 * D_FF_2), D_MODEL ** -0.5),
        "ffn_conv_w": nrm(ks[17], (DEPTH, CONV_W, 2 * D_FF_2), CONV_W ** -0.5),
        "ffn_conv_b": nrm(ks[18], (DEPTH, 2 * D_FF_2), 0.02),
        "ffn_w_down": nrm(ks[19], (DEPTH, D_FF_2, D_MODEL), D_FF_2 ** -0.5),
        "final_norm": gain(ks[20], (D_MODEL,)),
    }

def second_block(x, mem, attn_norm, attn_w_qkv, attn_q_gain, attn_k_gain, attn_w_o,
              pool_norm, pool_w, pool_scale,
              xattn_norm, mem_norm, xattn_w_q, xattn_w_kv, xattn_w_o,
              ffn_norm, ffn_w_up, ffn_conv_w, ffn_conv_b, ffn_w_down,
              final_norm):
    ia = 0
    ib = 0
    for i in range(DEPTH):
        if i % N_MIXERS == 0:
            x = x + axial_gqa_attention(rmsnorm(x, attn_norm[ia]), attn_w_qkv[ia],
                                        attn_q_gain[ia], attn_k_gain[ia], attn_w_o[ia])
            ia += 1
        else:
            x = x + multiscale_pool_mixer(rmsnorm(x, pool_norm[ib]), pool_w[ib], pool_scale[ib])
            ib += 1
        x = x + memory_cross_attention(rmsnorm(x, xattn_norm[i]), rmsnorm(mem, mem_norm[i]),
                                       xattn_w_q[i], xattn_w_kv[i], xattn_w_o[i])
        x = x + conv_gated_ffn(rmsnorm(x, ffn_norm[i]), ffn_w_up[i], ffn_conv_w[i],
                               ffn_conv_b[i], ffn_w_down[i])
    return rmsnorm(x, final_norm)


def setup_inputs(seed=0):
    out = dict(first_inputs(seed))
    for name, value in second_inputs(seed + 1).items():
        if name != "x":
            out[name + "_2"] = value
    return out


def reference(
    x, hy_w_in, diff_lambda, diff_subln, hy_w_out, gla_w_in, gla_w_gate_up, gla_b_gate,
    gla_norm, gla_w_out, ln_mix_g, ln_mix_b, ffn_w1, ffn_w2, ln_ffn_g, ln_ffn_b, mem_2,
    attn_norm_2, attn_w_qkv_2, attn_q_gain_2, attn_k_gain_2, attn_w_o_2, pool_norm_2, pool_w_2,
    pool_scale_2, xattn_norm_2, mem_norm_2, xattn_w_q_2, xattn_w_kv_2, xattn_w_o_2, ffn_norm_2,
    ffn_w_up_2, ffn_conv_w_2, ffn_conv_b_2, ffn_w_down_2, final_norm_2,
):
    x = first_block(
        x, hy_w_in, diff_lambda, diff_subln, hy_w_out, gla_w_in, gla_w_gate_up, gla_b_gate,
        gla_norm, gla_w_out, ln_mix_g, ln_mix_b, ffn_w1, ffn_w2, ln_ffn_g, ln_ffn_b,
    )
    return second_block(
        x, mem_2, attn_norm_2, attn_w_qkv_2, attn_q_gain_2, attn_k_gain_2, attn_w_o_2,
        pool_norm_2, pool_w_2, pool_scale_2, xattn_norm_2, mem_norm_2, xattn_w_q_2,
        xattn_w_kv_2, xattn_w_o_2, ffn_norm_2, ffn_w_up_2, ffn_conv_w_2, ffn_conv_b_2,
        ffn_w_down_2, final_norm_2,
    )


_drawn_inputs = setup_inputs


def setup_inputs(seed=0):
    import zlib

    import numpy as np

    out = dict(_drawn_inputs(seed))
    spreads = {}
    factors = {'diff_subln': 8.0,
     'gla_b_gate': 8.0,
     'gla_norm': 8.0,
     'attn_norm_2': 3.687,
     'attn_q_gain_2': 8.0,
     'attn_k_gain_2': 7.687,
     'xattn_norm_2': 7.551,
     'mem_norm_2': 5.282,
     'ffn_conv_b_2': 2.941}
    for name, (base, spread) in spreads.items():
        noise = np.random.default_rng([zlib.crc32(name.encode()), seed]).standard_normal(out[name].shape)
        drawn = base * np.exp(spread * noise) if base else spread * noise
        out[name] = jnp.asarray(drawn.astype(out[name].dtype))
    for name, factor in factors.items():
        out[name] = (out[name] * factor).astype(out[name].dtype)
    return out
```

```python
from contextlib import ExitStack

import numpy as np
import concourse.bass as bass
from concourse import mybir
from concourse.alu_op_type import AluOpType as ALU

ACT = mybir.ActivationFunctionType
AX = mybir.AxisListType.X
F32 = mybir.dt.float32
F32R = mybir.dt.float32r
BF16 = mybir.dt.bfloat16
U8 = mybir.dt.uint8

P = 128
D = 1024
T = 256
TT = T // P
KT = D // P
D_FF = 4096
D_FF2 = 2816
DEPTH = 2
ALPHA = (2 * DEPTH) ** 0.25
EPS_LN = 1e-5
EPS_RMS1 = 1e-5
EPS_RMS2 = 1e-6
LAMBDA_INIT = 0.2
NEG = -3.0e38

SLAB = 2048
RING = 4
RAWS = 2
LOOKAHEAD = 3
CH = 512
GLA_COLS = 3088
SQ_GROUPS = D_FF // 256
CV_GROUPS = D_FF2 // 256
FT2 = D_FF2 // P
LEVELS = [1, 2, 4, 8, 16, 32, 64]

C_IDENT = 0
C_MASK = C_IDENT + P
C_TRI = C_MASK + P
C_ROPE_D = C_TRI + P
C_ROPE_M = C_ROPE_D + 4 * 64
C_ROPE_X = C_ROPE_M + 4 * 128
C_ALL = C_ROPE_X + 4 * 64

A_NAT = 0
HY_P, HY_PT, HY_SQ = 6144, 7168, 8192
SQ_R, SQ_H = 0, 1024
CV_G, CV_V, CV_S, CV_H = 0, 1024, 2048, 3072
GL_G, GL_B, GL_Z, GL_ATT, GL_A01 = 4096, 5120, 6144, 8192, 9216
QK_SQ, QK_TMP, QK_KD, QK_P, QK_PT = 3072, 4352, 5632, 6656, 7680
XA_V, XA_P, XA_PT = 0, 2048, 3072
PO_MIX, PO_M, PO_W = 0, 4096, 6144
A_ALL = 9728


class Stage:
    slabs = frees = readies = 0

    def __init__(self, n, evacs, readies=0):
        self.s0, self.f0, self.r0 = Stage.slabs, Stage.frees, Stage.readies
        Stage.slabs += n
        Stage.frees += 4 + evacs
        Stage.readies += readies


def plan():
    Stage.slabs = Stage.frees = Stage.readies = 0
    st = {}
    st["hy_in"] = Stage(12, 12, 6)
    st["hy_out"] = Stage(4, 0, 2)
    st["ffn0"] = Stage(2 * SQ_GROUPS, SQ_GROUPS)
    st["gla"] = Stage(13, 5 + 8, 4)
    st["gla_out"] = Stage(4, 0, 2)
    st["ffn1"] = Stage(2 * SQ_GROUPS, SQ_GROUPS)
    st["qkv"] = Stage(6, 6, 3)
    st["wo"] = Stage(4, 0, 2)
    for i in range(2):
        st[f"mem{i}"] = Stage(8, 4 + 4, 2)
        st[f"xq{i}"] = Stage(4, 4)
        st[f"xo{i}"] = Stage(4, 0, 2)
        st[f"conv{i}"] = Stage(3 * CV_GROUPS, 2 * CV_GROUPS)
    return st, Stage.slabs


def at(i, step, k):
    return k if i is None else i * step + k


def build(nc, d):
    st, S = plan()
    out = d["out"]
    with ExitStack() as ctx:
        def sb(name, shape, dt=F32):
            return ctx.enter_context(nc.sbuf_tensor(name, shape, dt))

        def sem(name):
            return ctx.enter_context(nc.semaphore(name))

        raw = sb("raw", [P, RAWS, SLAB])
        wh = sb("wh", [P, RING, SLAB], F32R)
        wl = sb("wl", [P, RING, SLAB], F32R)
        xh = sb("xh", [P, KT, T], F32R)
        xl = sb("xl", [P, KT, T], F32R)
        hh = sb("hh", [P, 2, 2, T], F32R)
        hl = sb("hl", [P, 2, 2, T], F32R)
        X = sb("X", [P, TT, D])
        xn = sb("xn", [P, TT, D])
        arena = sb("arena", [P, A_ALL])
        qk = sb("qk", [P, 16, T])
        gains = sb("gains", [P, 4, D])
        con = sb("con", [P, C_ALL])
        lvmask = sb("lvmask", [P, 8 * P], U8)
        zero_bf = sb("zero_bf", [P, CH], BF16)
        lam_in = sb("lam_in", [P, 4, 64])
        lam = sb("lam", [P, 4])
        subln = sb("subln", [P, P])
        qkg = sb("qkg", [P, 2, 64])
        ropeg = sb("ropeg", [P, 4, TT, 64])
        glag = sb("glag", [P, T])
        cw = sb("cw", [P, 2, 4, 2 * FT2])
        var = sb("var", [P, TT, 20])
        rstd = sb("rstd", [P, TT, 20])
        mhalf = sb("mhalf", [P, 20])
        bst = sb("bst", [P, TT, 2, 6])
        mv = sb("mv", [P, TT, 2])
        mx = sb("mx", [P, TT, 24])
        nb = sb("nb", [P, TT, 24])
        rs = sb("rs", [P, TT, 24])
        rr = sb("rr", [P, TT, 24])
        one_row = sb("one_row", [1, P])
        ps = [ctx.enter_context(nc.psum_tensor(f"ps{i}", [P, CH], F32)) for i in range(8)]

        ident = con[:, C_IDENT:C_IDENT + P]
        cmask = con[:, C_MASK:C_MASK + P]
        tri = con[:, C_TRI:C_TRI + P]

        def table(col, w):
            return con[:, col:col + TT * w].rearrange("p (t w) -> p t w", t=TT)

        rope_d = table(C_ROPE_D, 64), table(C_ROPE_D + 128, 64)
        rope_m = table(C_ROPE_M, 128), table(C_ROPE_M + 256, 128)
        rope_x = table(C_ROPE_X, 64), table(C_ROPE_X + 128, 64)

        def ar(col, *dims):
            n = int(np.prod(dims))
            v = arena[:, col:col + n]
            if len(dims) == 2:
                v = v.rearrange("p (a b) -> p a b", b=dims[1])
            elif len(dims) == 3:
                v = v.rearrange("p (a b c) -> p a b c", b=dims[1], c=dims[2])
            return v

        xflat = xn[:, :, :].rearrange("p t d -> p (t d)")
        yT = xflat.rearrange("p (n t) -> p n t", t=T)
        mem = qk[:, 0:8, :].rearrange("p a b -> p (a b)").rearrange("p (t d) -> p t d", t=TT)
        qk_hi = qk[:, 8:16, :].rearrange("p a b -> p (a b)")
        wup = qk_hi[:, 0:512]
        bgate = qk_hi[0:1, 512:1024]
        hlow = qk_hi[:, 1024:1280]
        gE = xflat[:, 0:1024].rearrange("p (h t) -> p h t", t=T)
        gTmp = xflat[:, 1024:2048].rearrange("p (t n) -> p t n", t=TT)

        def bank2(b):
            return ps[b][:, :].rearrange("p (a t) -> p a t", t=T)

        def bank4(b):
            return ps[b][:, :].rearrange("p (a t) -> p a t", t=P)

        def slab_a(buf, slot):
            return buf[:, slot, :].rearrange("p (k n) -> p k n", n=CH)

        def slab_b(buf, slot):
            return buf[:, slot, :].rearrange("p (k n) -> p k n", n=T)

        def slab_dn(buf, slot):
            return buf[:, slot, :].rearrange("p (k n) -> p k n", n=D)

        raw_loaded = [sem(f"raw_loaded{i}") for i in range(RAWS)]
        wh_ready = sem("wh_ready")
        wl_ready = sem("wl_ready")
        slab_used = sem("slab_used")
        bank_free = sem("bank_free")
        bank_ready = sem("bank_ready")
        tr_done = sem("tr_done")
        xh_done = sem("xh_done")
        x_loaded = sem("x_loaded")
        con_loaded = sem("con_loaded")
        small_loaded = sem("small_loaded")
        cw_loaded = sem("cw_loaded")
        cw_T = sem("cw_T")
        cw_done = sem("cw_done")
        gain_loaded = [sem(f"gain_loaded{i}") for i in range(4)]
        pool_init = sem("pool_init")
        pool_order = sem("pool_order")
        dve_order = sem("dve_order")
        act_order = sem("act_order")
        var_ready = sem("var_ready")
        rstd_ready = sem("rstd_ready")
        x_ready = sem("x_ready")
        xn_ready = sem("xn_ready")
        lam_sum = sem("lam_sum")
        lam_exp = sem("lam_exp")
        rope_done = sem("rope_done")
        blk_T = sem("blk_T")
        blk_act = sem("blk_act")
        blk_dve = sem("blk_dve")
        half_done = sem("half_done")
        scores_ready = sem("scores_ready")
        nb_ready = sem("nb_ready")
        exp_done = sem("exp_done")
        diff_w = sem("diff_w")
        pT_ready = sem("pT_ready")
        pT_copied = sem("pT_copied")
        pv_done = sem("pv_done")
        sq_done = sem("sq_done")
        hid_sq = sem("hid_sq")
        hid_hi = sem("hid_hi")
        hid_lo = sem("hid_lo")
        conv_mid = sem("conv_mid")
        conv_tap = sem("conv_tap")
        gate_act = sem("gate_act")
        ff_outA = sem("ff_outA")
        ff_outD = sem("ff_outD")
        ff_nat = sem("ff_nat")
        gla_small = sem("gla_small")
        z_ready = sem("z_ready")
        ln_done = sem("ln_done")
        g_ready = sem("g_ready")
        b_ready = sem("b_ready")
        b_copied = sem("b_copied")
        d_ready = sem("d_ready")
        e_ready = sem("e_ready")
        zlev_ready = sem("zlev_ready")
        lv_ready = sem("lv_ready")
        lv_done = sem("lv_done")
        a01_done = sem("a01_done")
        r_act = sem("r_act")
        sr_done = sem("sr_done")
        go_ready = sem("go_ready")
        mem_loaded = sem("mem_loaded")
        pool_loaded = sem("pool_loaded")
        pmix_ready = sem("pmix_ready")
        pmix_done = sem("pmix_done")
        py_ready = sem("py_ready")
        out_done = sem("out_done")

        block = ctx.enter_context(nc.Block())

        HY_PAIRS = []
        for t in range(TT):
            HY_PAIRS += [("diff", t, h) for h in range(4)] + [("moba", t, j) for j in range(2)]
        QK_PAIRS = [("gqa", t, j) for t in range(TT) for j in range(8)]
        XA_PAIRS = [("x", t, j) for t in range(TT) for j in range(2)]
        Q_HY, Q_QK = 0, len(HY_PAIRS)
        Q_XA = [Q_QK + len(QK_PAIRS), Q_QK + len(QK_PAIRS) + len(XA_PAIRS)]
        SCALE = {"diff": 64 ** -0.5, "moba": 128 ** -0.5, "gqa": 64 ** -0.5, "x": 256 ** -0.5}

        def cols(kind, j):
            return {"diff": 2 * j, "moba": 8 + 2 * j, "gqa": 2 * j, "x": 2 * j}[kind]

        def width(kind, t):
            return P * (t + 1) if kind in ("diff", "moba") else T

        def pbuf(kind):
            return {"diff": (HY_P, HY_PT), "moba": (HY_P, HY_PT), "gqa": (QK_P, QK_PT), "x": (XA_P, XA_PT)}[kind]

        GAINS = ["ln_mix_g0", "ln_mix_b0", "ln_ffn_g0", "ln_ffn_b0", "ln_mix_g1", "ln_mix_b1", "ln_ffn_g1", "ln_ffn_b1",
                 "attn_norm", "mem_norm0", "xattn_norm0", "ffn_norm0", "pool_norm", "pool_scale",
                 "mem_norm1", "xattn_norm1", "ffn_norm1", "final_norm"]
        GK = {g: k for k, g in enumerate(GAINS)}

        @block.sync
        def _(sp):
            def load(s, src, view, i=None, step=0):
                if s >= RAWS:
                    sp.wait_ge(wl_ready, at(i, step, s - RAWS + 1))
                sp.dma_start(view(raw, s % RAWS), src).then_inc(raw_loaded[s % RAWS], 16)

            def kview(w):
                return w.rearrange("(k p) n -> p k n", p=P)

            def load_a(s, w, n0, i=None, step=0):
                for half in range(2):
                    load(s + half, kview(w)[:, 4 * half:4 * half + 4, bass.ds(n0, CH)], slab_a, i, step)

            def load_b(s, w, n0, i=None, step=0):
                load(s, kview(w)[:, :, bass.ds(n0, T)], slab_b, i, step)

            def load_dn(s, w, k0, i=None, step=0):
                load(s, kview(w)[:, bass.ds(k0, 2), :], slab_dn, i, step)

            def ffn(s0, w1, w2):
                load_b(s0, w1, 0)
                with sp.Fori(0, (SQ_GROUPS - 2) // 2) as i:
                    for j in (1, 2):
                        load_b(s0 + 2 * j - 1, w1, i * (2 * T) + j * T, i, 4)
                        load_dn(s0 + 2 * j, w2, i * 4 + 2 * (j - 1), i, 4)
                g = SQ_GROUPS - 1
                load_b(s0 + 2 * g - 1, w1, g * T)
                load_dn(s0 + 2 * g, w2, 2 * (g - 1))
                load_dn(s0 + 2 * g + 1, w2, 2 * g)

            def conv(s0, w1, w2):
                def group(g, i=None):
                    load_b(s0 + 3 * g - 1, w1, at(i, 4 * T, g * T), i, 12)
                    load_b(s0 + 3 * g, w1, at(i, 4 * T, D_FF2 + g * T), i, 12)
                    load_dn(s0 + 3 * g + 1, w2, at(i, 8, 2 * (g - 1)), i, 12)
                load_b(s0, w1, 0)
                load_b(s0 + 1, w1, D_FF2)
                with sp.Fori(0, (CV_GROUPS - 1) // 4) as i:
                    for g in range(1, 5):
                        group(g, i)
                for g in range(1 + (CV_GROUPS - 1) // 4 * 4, CV_GROUPS):
                    group(g)
                load_dn(s0 + 3 * CV_GROUPS - 1, w2, 2 * (CV_GROUPS - 1))

            sp.dma_start(X[:, :, :], d["x"][0].rearrange("(t p) d -> p t d", p=P)).then_inc(x_loaded, 16)
            for c, n0 in enumerate((0, 512, 1536, 2048, 1024, 2560)):
                load_a(st["hy_in"].s0 + 2 * c, d["hy_w_in"], n0)
            for c in range(2):
                load_a(st["hy_out"].s0 + 2 * c, d["hy_w_out"], c * CH)
            ffn(st["ffn0"].s0, d["ffn_w1"][0], d["ffn_w2"][0])
            s0 = st["gla"].s0
            with sp.Fori(0, 1) as i:
                for j in range(4):
                    load_b(s0 + j, d["gla_w_in"], j * T)
            load_b(s0 + 4, d["gla_w_in"], GLA_COLS - T)
            for c in range(4):
                load_a(s0 + 5 + 2 * c, d["gla_w_in"], D + c * CH)
            for c in range(2):
                load_a(st["gla_out"].s0 + 2 * c, d["gla_w_out"], c * CH)
            ffn(st["ffn1"].s0, d["ffn_w1"][1], d["ffn_w2"][1])
            for c in range(3):
                load_a(st["qkv"].s0 + 2 * c, d["attn_w_qkv"], c * CH)
            for c in range(2):
                load_a(st["wo"].s0 + 2 * c, d["attn_w_o"], c * CH)
            for l in range(2):
                for j in range(4):
                    load_b(st[f"mem{l}"].s0 + j, d["xattn_w_kv"][l], j * T)
                for c in range(2):
                    load_a(st[f"mem{l}"].s0 + 4 + 2 * c, d["xattn_w_kv"][l], D + c * CH)
                for j in range(4):
                    load_b(st[f"xq{l}"].s0 + j, d["xattn_w_q"][l], j * T)
                for c in range(2):
                    load_a(st[f"xo{l}"].s0 + 2 * c, d["xattn_w_o"][l], c * CH)
                conv(st[f"conv{l}"].s0, d["ffn_w_up"][l], d["ffn_w_down"][l])
            for t in range(TT):
                sp.wait_ge(xn_ready, 2 * 13 + t + 1)
                sp.dma_start(out[0, t * P:(t + 1) * P, :], xn[:, t, :]).then_inc(out_done, 16)
            sp.wait_ge(out_done, 16 * TT)

        @block.gpsimd
        def _(pool):
            def gain(k):
                nc.gpsimd.dma_start(gains[:, k % 4, :], d[GAINS[k]].partition_broadcast(P))\
                    .then_inc(gain_loaded[k % 4], 16)

            def small(dst, src):
                nc.gpsimd.dma_start(dst, src).then_inc(small_loaded, 16)

            order = [0]

            def step(ins):
                order[0] += 1
                ins.then_inc(pool_order, 1)
                pool.wait_ge(pool_order, order[0])

            def norm(n, nh, scale, eps, ln=False):
                for t in range(TT):
                    pool.wait_ge(var_ready, 2 * n + t + 1)
                    src = mv[:, t, 1:2] if ln else var[:, t, 0:nh]
                    step(nc.gpsimd.tensor_scalar(rstd[:, t, 0:nh], src, scale, eps, ALU.mult, ALU.add))
                    nc.gpsimd.tensor_tensor(rstd[:, t, 0:nh], rstd[:, t, 0:nh], mhalf[:, 0:nh], ALU.pow)\
                        .then_inc(rstd_ready, 1)

            nc.gpsimd.memset(mhalf[:, :], -0.5).then_inc(pool_init, 1)
            nc.gpsimd.memset(zero_bf[:, :], 0.0).then_inc(pool_init, 1)
            nc.gpsimd.memset(one_row[:, :], 1.0).then_inc(pool_init, 1)
            small(lam_in[:, :, :], d["diff_lambda"].partition_broadcast(P))
            small(subln[:, :], d["diff_subln"].partition_broadcast(P))
            small(qkg[:, 0, :], d["attn_q_gain"].partition_broadcast(P))
            small(qkg[:, 1, :], d["attn_k_gain"].partition_broadcast(P))
            small(glag[:, :], d["gla_norm"].partition_broadcast(P))
            small(arena[:, HY_SQ:HY_SQ + 8 * P], d["c_levels"])
            for l in range(2):
                row = xn[0:2 * FT2, l, 0:512].rearrange("p (a f) -> p a f", f=P)
                for a in range(4):
                    src = d["ffn_conv_w"][l, a] if a < 3 else d["ffn_conv_b"][l]
                    nc.gpsimd.dma_start(row[0:2 * FT2, a, :], src.rearrange("(j f) -> j f", f=P)).then_inc(cw_loaded, 16)
            for k in range(4):
                gain(k)
            pool.wait_ge(pool_init, 3)
            norm(0, 4, 1.0 / 128, EPS_RMS1)
            norm(1, 1, 1.0, EPS_LN, ln=True)
            pool.wait_ge(x_ready, 2)
            gain(4), gain(5)
            step(nc.gpsimd.memset(wup, 0.0))
            nc.gpsimd.dma_start(qk_hi[112:128, 0:512], d["gla_w_gate_up"]).then_inc(gla_small, 16)
            nc.gpsimd.dma_start(bgate, d["gla_b_gate"].unsqueeze(0)).then_inc(gla_small, 16)
            nc.gpsimd.memset(arena[:, GL_ATT:GL_ATT + 1024], 0.0).then_inc(pool_init, 1)
            norm(2, 1, 1.0, EPS_LN, ln=True)
            pool.wait_ge(x_ready, 4)
            gain(6), gain(7)
            norm(3, 4, 1.0 / 256, EPS_RMS1)
            norm(4, 1, 1.0, EPS_LN, ln=True)
            pool.wait_ge(x_ready, 6)
            gain(8), gain(9)
            norm(5, 1, 1.0, EPS_LN, ln=True)
            pool.wait_ge(x_ready, 8)
            gain(10), gain(11)
            norm(6, 1, 1.0 / D, EPS_RMS2)
            pool.wait_ge(xn_ready, 2 * 2 + 2)
            gain(12)
            norm(7, 20, 1.0 / 64, EPS_RMS2)
            pool.wait_ge(xn_ready, 2 * 3 + 2)
            nc.gpsimd.dma_start(mem, d["mem"][0].rearrange("(t p) d -> p t d", p=P)).then_inc(mem_loaded, 16)
            nc.gpsimd.dma_start(ar(PO_M, TT, 4 * T), d["c_pool"].rearrange("(t p) n -> p t n", p=P)).then_inc(pool_loaded, 16)
            nc.gpsimd.dma_start(ar(PO_W, 8, T), d["pool_w"].rearrange("g (k p) n -> p (g k) n", p=P)).then_inc(pool_loaded, 16)
            norm(8, 1, 1.0 / D, EPS_RMS2)
            pool.wait_ge(xn_ready, 2 * 4 + 2)
            gain(13)
            norm(9, 1, 1.0 / D, EPS_RMS2)
            pool.wait_ge(xn_ready, 2 * 5 + 2)
            gain(14)
            pool.wait_ge(xn_ready, 2 * 6 + 2)
            nc.gpsimd.dma_start(mem, d["mem"][0].rearrange("(t p) d -> p t d", p=P)).then_inc(mem_loaded, 16)
            norm(10, 1, 1.0 / D, EPS_RMS2)
            pool.wait_ge(xn_ready, 2 * 7 + 2)
            gain(15)
            norm(11, 1, 1.0 / D, EPS_RMS2)
            pool.wait_ge(xn_ready, 2 * 8 + 2)
            gain(16)
            pool.wait_ge(x_ready, 2 * 7 + 2)
            gain(17)
            norm(12, 1, 1.0 / D, EPS_RMS2)
            norm(13, 1, 1.0 / D, EPS_RMS2)
            norm(14, 1, 1.0 / D, EPS_RMS2)
            norm(15, 1, 1.0 / D, EPS_RMS2)

        @block.scalar
        def _(act):
            order = [0]

            def step(ins):
                order[0] += 1
                ins.then_inc(act_order, 1)
                act.wait_ge(act_order, order[0])

            def split(s, i=None, dstep=0):
                if s >= S:
                    return
                act.wait_ge(raw_loaded[s % RAWS], at(i, 16 * dstep // RAWS, 16 * (s // RAWS + 1)))
                if s >= RING:
                    act.wait_ge(slab_used, at(i, dstep, s - RING + 1))
                nc.scalar.activation(wh[:, s % RING, :], raw[:, s % RAWS, :], ACT.Copy).then_inc(wh_ready, 1)

            def prep(p):
                for t in range(TT):
                    for half in range(2):
                        act.wait_ge(tr_done, 4 * p + 2 * t + half + 1)
                        nc.scalar.activation(xh[:, 4 * half:4 * half + 4, t * P:(t + 1) * P], bank4(t + 2 * half), ACT.Copy)\
                            .then_inc(xh_done, 1)

            def copy_a(stage, k, dst, i=None, nstep=0):
                s = stage.s0 + k[1]
                act.wait_ge(bank_ready, at(i, nstep, stage.r0 + k[0] + 1))
                nc.scalar.activation(dst(0), ps[2 * (k[0] % 2)][:, :], ACT.Copy).then_inc(bank_free, 1)
                act.wait_ge(slab_used, at(i, 2 * nstep, s + 2))
                nc.scalar.activation(dst(1), ps[2 * (k[0] % 2) + 1][:, :], ACT.Copy).then_inc(bank_free, 1)

            def copy_b(stage, j, dst, scale=1.0):
                act.wait_ge(slab_used, stage.s0 + j + 1)
                nc.scalar.activation(dst, bank2(j % 4), ACT.Copy, scale=scale).then_inc(bank_free, 1)

            def splits(stage, a, b):
                for j in range(a, b):
                    split(stage.s0 + j + LOOKAHEAD)

            def rms_stats(n, src, w, v):
                for t in range(TT):
                    act.wait_ge(w, v(t))
                    nc.scalar.activation(xn[:, t, :], src[:, t, :], ACT.Square, accum_out=var[:, t, 0:1]).then_inc(var_ready, 1)

            def x_at(u):
                return lambda t: 2 * u + t + 1

            def blocks(base, fills):
                for f in range(0, fills, 2):
                    act.wait_ge(blk_T, base + f + 1)
                    nc.scalar.activation(qk[:, 2 * f:2 * f + 2, :], bank2(4 + f % 4), ACT.Copy).then_inc(blk_act, 1)

            def softmax(pairs, q0):
                for q, (kind, t, j) in enumerate(pairs, q0):
                    w = width(kind, t)
                    pa, pt = pbuf(kind)
                    c = cols(kind, j)
                    act.wait_ge(nb_ready, q + 1)
                    if q >= 2:
                        act.wait_ge(pT_ready, q - 1)
                    for u in range(2):
                        ins = nc.scalar.activation(ar(pa, 2, 2, T)[:, q % 2, u, 0:w], bank2(q % 2)[:, u, 0:w], ACT.Exp,
                                                   bias=nb[:, t, c + u:c + u + 1], scale=SCALE[kind],
                                                   accum_out=rs[:, t, c + u:c + u + 1])
                    ins.then_inc(exp_done, 1)
                    if kind == "diff":
                        act.wait_ge(pT_ready, q + 1)
                        if q >= 2:
                            act.wait_ge(pv_done, q - 1)
                        nc.scalar.activation(ar(pt, 2, CH)[:, q % 2, 0:w], ps[2 + q % 2][:, 0:w], ACT.Copy).then_inc(pT_copied, 1)

            def ffn(name, base):
                stage = st[name]
                s0 = stage.s0
                r, h = ar(SQ_R, 2, CH), ar(SQ_H, 2, CH)

                def group(g, i=None):
                    up = s0 + 2 * g - 1 if g else s0
                    act.wait_ge(slab_used, at(i, 4, up + 1))
                    nc.scalar.activation(r[:, g % 2, :], ps[g % 2][:, :], ACT.Relu).then_inc(bank_free, 1)
                    act.wait_ge(hid_sq, at(i, 2, base + g + 1))
                    nc.scalar.activation(hh[:, g % 2, :, :].rearrange("p k t -> p (k t)"), h[:, g % 2, :], ACT.Copy).then_inc(hid_hi, 1)

                split(s0 + LOOKAHEAD)
                group(0)
                with act.Fori(0, (SQ_GROUPS - 2) // 2) as i:
                    for g in (1, 2):
                        split(s0 + 2 * g - 1 + LOOKAHEAD, i, 4)
                        split(s0 + 2 * g + LOOKAHEAD, i, 4)
                        group(g, i)
                g = SQ_GROUPS - 1
                splits(stage, 2 * g - 1, 2 * g + 1)
                group(g)
                splits(stage, 2 * g + 1, 2 * g + 2)
                ffn_out(s0 + 2 * SQ_GROUPS)

            def ffn_out(s_end):
                act.wait_ge(slab_used, s_end)
                for b in range(2):
                    nc.scalar.activation(yT[:, 2 * b:2 * b + 2, :], bank2(4 + b), ACT.Copy).then_inc(ff_outA, 1)

            def conv(name, l, base, cbase):
                stage = st[name]
                s0 = stage.s0
                cg, cv, sg, h = ar(CV_G, 2, 2, T), ar(CV_V, 2, 2, T), ar(CV_S, 2, CH), ar(CV_H, 2, CH)

                def mid(bank, dst, ft, i):
                    for a in range(2):
                        f = at(i, 8, ft + a)
                        ins = nc.scalar.activation(dst[:, a, :], bank2(bank)[:, a, :], ACT.Identity,
                                                   scale=cw[:, l, 1, bass.ds(f, 1)], bias=cw[:, l, 3, bass.ds(f, 1)])
                    ins.then_inc(conv_mid, 1)

                def group(g, i=None):
                    up = s0 + 3 * g - 1 if g else s0
                    act.wait_ge(slab_used, at(i, 12, up + 1))
                    mid(2 * (g % 2), cg[:, g % 2], 2 * g, i)
                    act.wait_ge(slab_used, at(i, 12, up + 2))
                    mid(2 * (g % 2) + 1, cv[:, g % 2], FT2 + 2 * g, i)
                    act.wait_ge(bank_free, at(i, 8, stage.f0 + 4 + 2 * g + 1))
                    nc.scalar.activation(sg[:, g % 2, :], cg[:, g % 2].rearrange("p a t -> p (a t)"), ACT.Silu).then_inc(gate_act, 1)
                    act.wait_ge(hid_sq, at(i, 4, base + g + 1))
                    nc.scalar.activation(hh[:, g % 2, :, :].rearrange("p k t -> p (k t)"), h[:, g % 2, :], ACT.Copy).then_inc(hid_hi, 1)

                splits(stage, 0, 2)
                group(0)
                n = (CV_GROUPS - 1) // 4
                with act.Fori(0, n) as i:
                    for g in range(1, 5):
                        for j in range(3 * g - 1, 3 * g + 2):
                            split(s0 + j + LOOKAHEAD, i, 12)
                        group(g, i)
                for g in range(1 + 4 * n, CV_GROUPS):
                    splits(stage, 3 * g - 1, 3 * g + 2)
                    group(g)
                splits(stage, 3 * CV_GROUPS - 1, 3 * CV_GROUPS)
                ffn_out(s0 + 3 * CV_GROUPS)

            nc.scalar.dma_start(con[:, :], d["c_table"]).then_inc(con_loaded, 16)
            for s in range(LOOKAHEAD):
                split(s)
            act.wait_ge(cw_T, 1)
            nc.scalar.activation(cw[:, :, :, :].rearrange("p l a j -> p (l a j)"), ps[7][:, 0:16 * FT2], ACT.Copy).then_inc(cw_done, 1)
            act.wait_ge(lam_sum, 1)
            nc.scalar.activation(lam[:, 0:2], lam[:, 2:4], ACT.Exp).then_inc(lam_exp, 1)

            prep(0)
            g = st["hy_in"]
            with act.Fori(0, 3) as i:
                for c in range(2):
                    split(g.s0 + 2 * c + LOOKAHEAD, i, 4)
                    split(g.s0 + 2 * c + 1 + LOOKAHEAD, i, 4)
                    copy_a(g, (c, 2 * c), lambda t: ar(A_NAT, TT, 3072)[:, t, bass.ds(i * 1024 + c * CH, CH)], i, 2)
            blocks(0, 8)
            softmax(HY_PAIRS, Q_HY)
            for t in range(TT):
                act.wait_ge(pv_done, Q_HY + 6 * t + 4)
                nc.scalar.activation(ar(HY_SQ, TT, CH)[:, t, :], ps[4 + t][:, :], ACT.Square).then_inc(sq_done, 1)
            prep(1)
            splits(st["hy_out"], 0, 4)
            prep(2)
            ffn("ffn0", 0)

            prep(3)
            g = st["gla"]
            for j in range(4):
                split(g.s0 + j + LOOKAHEAD)
                copy_b(g, j, qk[:, 2 * j:2 * j + 2, :], P ** -0.5 if j < 2 else 1.0)
            split(g.s0 + 4 + LOOKAHEAD)
            act.wait_ge(slab_used, g.s0 + 5)
            nc.scalar.activation(hlow, bank2(0)[:, 1, :], ACT.Copy).then_inc(bank_free, 1)

            def vr(c):
                splits(g, 5 + 2 * c, 7 + 2 * c)
                copy_a(g, (c, 5 + 2 * c), lambda t: ar(A_NAT, TT, 2048)[:, t, c * CH:(c + 1) * CH])

            vr(0)
            for t in range(TT):
                act.wait_ge(z_ready, t + 1)
                step(nc.scalar.activation(gTmp[:, t, :], ps[4 + t][:, :], ACT.Abs))
                step(nc.scalar.activation(gTmp[:, t, :], gTmp[:, t, :], ACT.Exp, scale=-1.0))
                nc.scalar.activation(gTmp[:, t, :], gTmp[:, t, :], ACT.Ln, bias=1.0).then_inc(ln_done, 1)
            vr(1)
            for t in range(TT):
                act.wait_ge(b_ready, t + 1)
                nc.scalar.activation(ar(GL_B, 4, T)[:, :, t * P:(t + 1) * P], bank4(6 + t), ACT.Copy).then_inc(b_copied, 1)

            def exps(lv):
                act.wait_ge(d_ready, lv)
                if lv <= len(LEVELS):
                    nc.scalar.activation(gE, gE, ACT.Exp).then_inc(e_ready, 1)
                else:
                    nc.scalar.activation(gE[:, :, 0:P], gE[:, :, 0:P], ACT.Exp)
                    nc.scalar.activation(gE[:, :, P:T], ar(GL_B, 4, T)[:, :, P:T], ACT.Exp).then_inc(e_ready, 1)

            for lv in (1, 2):
                exps(lv)
            vr(2)
            for lv in (3, 4):
                exps(lv)
            vr(3)
            for lv in range(5, 9):
                exps(lv)
            for t in range(TT):
                rv = ar(A_NAT, TT, 2048)[:, t, D:2 * D]
                act.wait_ge(bank_free, g.f0 + 4 + 5 + 8)
                nc.scalar.activation(rv, rv, ACT.Silu).then_inc(r_act, 1)
            act.wait_ge(lv_ready, 17)
            nc.scalar.activation(ar(GL_A01, 4, P), bank4(4), ACT.Copy).then_inc(a01_done, 1)
            for t in range(TT):
                act.wait_ge(go_ready, t + 1)
                for hp in range(2):
                    ins = nc.scalar.activation(xn[:, t, hp * CH:(hp + 1) * CH], ps[t + 2 * hp][:, :], ACT.Square)
                ins.then_inc(sq_done, 1)
            prep(4)
            splits(st["gla_out"], 0, 4)
            prep(5)
            ffn("ffn1", SQ_GROUPS)

            rms_stats(6, X, x_ready, x_at(3))
            prep(6)
            g = st["qkv"]
            for c in range(3):
                splits(g, 2 * c, 2 * c + 2)
                copy_a(g, (c, 2 * c), lambda t: ar(A_NAT, TT, 1536)[:, t, c * CH:(c + 1) * CH])
            for t in range(TT):
                act.wait_ge(bank_free, g.f0 + 4 + 6)
                nc.scalar.activation(ar(QK_SQ, 1280), ar(A_NAT, TT, 1536)[:, t, 0:1280], ACT.Square).then_inc(sq_done, 1)
                act.wait_ge(var_ready, 2 * 7 + t + 1)
            blocks(8, 6)
            softmax(QK_PAIRS, Q_QK)
            prep(7)
            splits(st["wo"], 0, 4)

            for l in range(2):
                n = (8, 12)[l]
                p = (8, 12)[l]
                g = st[f"mem{l}"]
                if l:
                    act.wait_ge(x_ready, 2 * 7 + 2)
                rms_stats(n, mem, mem_loaded, lambda t: 16 * (l + 1))
                prep(p)
                for j in range(4):
                    splits(g, j, j + 1)
                    copy_b(g, j, qk[:, 8 + 2 * j:10 + 2 * j, :])
                for c in range(2):
                    splits(g, 4 + 2 * c, 6 + 2 * c)
                    copy_a(g, (c, 4 + 2 * c), lambda t: ar(XA_V, TT, D)[:, t, c * CH:(c + 1) * CH])
                rms_stats(n + 1, X, x_ready, x_at((4, 7)[l]))
                prep(p + 1)
                g = st[f"xq{l}"]
                for j in range(4):
                    splits(g, j, j + 1)
                    copy_b(g, j, qk[:, 2 * j:2 * j + 2, :])
                softmax(XA_PAIRS, Q_XA[l])
                prep(p + 2)
                splits(st[f"xo{l}"], 0, 4)
                rms_stats(n + 2 if l == 0 else n + 2, X, x_ready, x_at((5, 8)[l]))
                prep(p + 3)
                conv(f"conv{l}", l, 2 * SQ_GROUPS + CV_GROUPS * l, 0)
                act.wait_ge(ff_nat, 4 * (3 + l))
                rms_stats((11, 15)[l], X, x_ready, x_at((6, 9)[l]))
                if l == 0:
                    for b in range(4):
                        act.wait_ge(pmix_ready, b + 1)
                        nc.scalar.activation(ar(PO_MIX, 8, T)[:, 2 * b:2 * b + 2, :], bank2(b), ACT.Copy).then_inc(pmix_done, 1)

        @block.vector
        def _(dve):
            order = [0]

            def step(ins):
                order[0] += 1
                ins.then_inc(dve_order, 1)

            def sync():
                dve.wait_ge(dve_order, order[0])

            def split(s, i=None, dstep=0):
                if s >= S:
                    return
                dve.wait_ge(wh_ready, at(i, dstep, s + 1))
                nc.vector.tensor_tensor(wl[:, s % RING, :], raw[:, s % RAWS, :], wh[:, s % RING, :].bitcast(F32), ALU.subtract)\
                    .then_inc(wl_ready, 1)

            def splits(stage, a, b):
                for j in range(a, b):
                    split(stage.s0 + j + LOOKAHEAD)

            def prep(p):
                for t in range(TT):
                    for half in range(2):
                        dve.wait_ge(xh_done, 4 * p + 2 * t + half + 1)
                        part = slice(4 * half, 4 * half + 4), slice(t * P, (t + 1) * P)
                        nc.vector.tensor_tensor(xl[:, part[0], part[1]], bank4(t + 2 * half), xh[:, part[0], part[1]].bitcast(F32),
                                                ALU.subtract).then_inc(bank_free, 1)

            def gain(name):
                k = GK[name]
                dve.wait_ge(gain_loaded[k % 4], 16 * (k // 4 + 1))
                return gains[:, k % 4, :]

            def layer_norm(n, kind, l, order_ct, wait_ct):
                done = [0, 0]
                for c, t in order_ct:
                    cs = slice(c * CH, (c + 1) * CH)
                    wait_ct(c, t)
                    step(nc.vector.scalar_tensor_tensor(X[:, t, cs], X[:, t, cs], ALPHA, ps[2 * c + t][:, :], ALU.mult, ALU.add))
                    sync()
                    step(nc.vector.bn_stats(bst[:, t, c, :], X[:, t, cs]))
                    done[t] += 1
                    if done[t] == 2:
                        sync()
                        nc.vector.bn_aggr(mv[:, t, :], bst[:, t, :, :].rearrange("p c s -> p (c s)")).then_inc(var_ready, 1)
                gg, bb = gain(f"ln_{kind}_g{l}"), gain(f"ln_{kind}_b{l}")
                for t in range(TT):
                    dve.wait_ge(var_ready, 2 * n + t + 1)
                    step(nc.vector.scalar_tensor_tensor(X[:, t, :], X[:, t, :], mv[:, t, 0:1], gg, ALU.subtract, ALU.mult))
                    sync()
                    dve.wait_ge(rstd_ready, 2 * n + t + 1)
                    nc.vector.scalar_tensor_tensor(X[:, t, :], X[:, t, :], rstd[:, t, 0:1], bb, ALU.mult, ALU.add).then_inc(x_ready, 1)

            CT = [(c, t) for c in range(2) for t in range(TT)]
            TC = [(c, t) for t in range(TT) for c in range(2)]

            def wait_a(stage):
                def w(c, t):
                    if t == 0:
                        dve.wait_ge(bank_ready, stage.r0 + c + 1)
                    else:
                        dve.wait_ge(slab_used, stage.s0 + 2 * c + 2)
                return w

            def wait_nat(f):
                return lambda c, t: dve.wait_ge(ff_nat, 4 * f + 2 * t + c + 1)

            def residual(order_ct, wait_ct):
                done = [0, 0]
                for c, t in order_ct:
                    cs = slice(c * CH, (c + 1) * CH)
                    wait_ct(c, t)
                    ins = nc.vector.tensor_tensor(X[:, t, cs], ps[2 * c + t][:, :], X[:, t, cs], ALU.add)
                    done[t] += 1
                    if done[t] == 2:
                        ins.then_inc(x_ready, 1)

            def rms_apply(n, name, src):
                gg = gain(name)
                for t in range(TT):
                    dve.wait_ge(rstd_ready, 2 * n + t + 1)
                    nc.vector.scalar_tensor_tensor(xn[:, t, :], src[:, t, :], rstd[:, t, 0:1], gg, ALU.mult, ALU.mult).then_inc(xn_ready, 1)

            def blocks(base, fills):
                for f in range(1, fills, 2):
                    dve.wait_ge(blk_T, base + f + 1)
                    nc.vector.tensor_copy(qk[:, 2 * f:2 * f + 2, :], bank2(4 + f % 4)).then_inc(blk_dve, 1)

            def softmax(pairs, q0, after):
                def copy_pT(q):
                    kind, t, j = pairs[q - q0]
                    if kind == "diff":
                        return
                    w = width(kind, t)
                    dve.wait_ge(pT_ready, q + 1)
                    if q >= 2:
                        dve.wait_ge(pv_done, q - 1)
                    nc.vector.tensor_copy(ar(pbuf(kind)[1], 2, CH)[:, q % 2, 0:2 * w], ps[2 + q % 2][:, 0:2 * w]).then_inc(pT_copied, 1)

                for q, (kind, t, j) in enumerate(pairs, q0):
                    w = width(kind, t)
                    c = cols(kind, j)
                    dve.wait_ge(scores_ready, q + 1)
                    step(nc.vector.tensor_reduce(mx[:, t, c:c + 2], bank2(q % 2)[:, :, 0:w], AX, ALU.max))
                    sync()
                    nc.vector.tensor_scalar(nb[:, t, c:c + 2], mx[:, t, c:c + 2], -SCALE[kind], None, ALU.mult).then_inc(nb_ready, 1)
                    if q > q0:
                        copy_pT(q - 1)
                        after(q - 1 - q0)
                    if kind == "diff":
                        p = ar(pbuf(kind)[0], 2, 2, T)[:, q % 2]
                        dve.wait_ge(exp_done, q + 1)
                        step(nc.vector.reciprocal(rr[:, t, c:c + 2], rs[:, t, c:c + 2]))
                        sync()
                        step(nc.vector.tensor_scalar(rr[:, t, c + 1:c + 2], rr[:, t, c + 1:c + 2], lam[:, 2:3], None, ALU.mult))
                        sync()
                        step(nc.vector.tensor_scalar(p[:, 1, 0:w], p[:, 1, 0:w], rr[:, t, c + 1:c + 2], None, ALU.mult))
                        sync()
                        nc.vector.scalar_tensor_tensor(p[:, 0, 0:w], p[:, 0, 0:w], rr[:, t, c:c + 1], p[:, 1, 0:w],
                                                       ALU.mult, ALU.subtract).then_inc(diff_w, 1)
                copy_pT(q0 + len(pairs) - 1)
                after(len(pairs) - 1)

            def heads_out(dst, src, col, n, w, t):
                return nc.vector.tensor_tensor(dst.rearrange("p (h w) -> p h w", w=w), src.rearrange("p (h w) -> p h w", w=w),
                                               rr[:, t, col:col + n].unsqueeze(2).to_broadcast([P, n, w]), ALU.mult)

            def rope(x, tmp, g, half, cos, sin):
                xg = x.rearrange("p (g a h) -> p g a h", a=2, h=half)
                tg = tmp.rearrange("p (g a h) -> p g a h", a=2, h=half)
                for a in range(2):
                    tab = sin[:, a * half:(a + 1) * half].unsqueeze(1).to_broadcast([P, g, half])
                    step(nc.vector.tensor_tensor(tg[:, :, a, :], xg[:, :, 1 - a, :], tab, ALU.mult))
                sync()
                xw = x.rearrange("p (g w) -> p g w", w=2 * half)
                step(nc.vector.tensor_tensor(xw, xw, cos.unsqueeze(1).to_broadcast([P, g, 2 * half]), ALU.mult))
                sync()
                return nc.vector.tensor_tensor(x, x, tmp, ALU.add)

            def ffn_out(s_end):
                dve.wait_ge(slab_used, s_end)
                for b in range(2, 4):
                    nc.vector.tensor_copy(yT[:, 2 * b:2 * b + 2, :], bank2(4 + b)).then_inc(ff_outD, 1)

            def low(g, base, i, istep):
                dve.wait_ge(hid_hi, at(i, istep, base + g + 1))

            def ffn(name, base):
                stage = st[name]
                s0 = stage.s0
                r, h = ar(SQ_R, 2, CH), ar(SQ_H, 2, CH)

                def group(g, i=None):
                    dve.wait_ge(bank_free, at(i, 2, stage.f0 + 4 + g + 1))
                    nc.vector.tensor_tensor(h[:, g % 2, :], r[:, g % 2, :], r[:, g % 2, :], ALU.mult).then_inc(hid_sq, 1)
                    dve.wait_ge(hid_hi, at(i, 2, base + g + 1))
                    nc.vector.tensor_tensor(hl[:, g % 2, :, :].rearrange("p k t -> p (k t)"), h[:, g % 2, :],
                                            hh[:, g % 2, :, :].rearrange("p k t -> p (k t)").bitcast(F32), ALU.subtract).then_inc(hid_lo, 1)

                split(s0 + LOOKAHEAD)
                group(0)
                with dve.Fori(0, (SQ_GROUPS - 2) // 2) as i:
                    for g in (1, 2):
                        split(s0 + 2 * g - 1 + LOOKAHEAD, i, 4)
                        split(s0 + 2 * g + LOOKAHEAD, i, 4)
                        group(g, i)
                g = SQ_GROUPS - 1
                splits(stage, 2 * g - 1, 2 * g + 1)
                group(g)
                splits(stage, 2 * g + 1, 2 * g + 2)
                ffn_out(s0 + 2 * SQ_GROUPS)

            def conv(name, l, base, cbase):
                stage = st[name]
                s0 = stage.s0
                cg, cv, sg, h = ar(CV_G, 2, 2, T), ar(CV_V, 2, 2, T), ar(CV_S, 2, CH), ar(CV_H, 2, CH)

                def taps(bank, dst, ft, e, i):
                    dve.wait_ge(conv_mid, at(i, 8, cbase + e + 1))
                    for a in range(2):
                        ins = nc.vector.scalar_tensor_tensor(dst[:, a, 1:T], bank2(bank)[:, a, 0:T - 1], cw[:, l, 0, bass.ds(at(i, 8, ft + a), 1)],
                                                             dst[:, a, 1:T], ALU.mult, ALU.add)
                    ins.then_inc(conv_tap, 1)
                    dve.wait_ge(conv_tap, at(i, 8, cbase + e + 1))
                    for a in range(2):
                        ins = nc.vector.scalar_tensor_tensor(dst[:, a, 0:T - 1], bank2(bank)[:, a, 1:T], cw[:, l, 2, bass.ds(at(i, 8, ft + a), 1)],
                                                             dst[:, a, 0:T - 1], ALU.mult, ALU.add)
                    ins.then_inc(bank_free, 1)

                def group(g, i=None):
                    taps(2 * (g % 2), cg[:, g % 2], 2 * g, 2 * g, i)
                    taps(2 * (g % 2) + 1, cv[:, g % 2], FT2 + 2 * g, 2 * g + 1, i)
                    dve.wait_ge(gate_act, at(i, 4, CV_GROUPS * l + g + 1))
                    dve.wait_ge(bank_free, at(i, 8, stage.f0 + 4 + 2 * g + 2))
                    nc.vector.tensor_tensor(h[:, g % 2, :], sg[:, g % 2, :], cv[:, g % 2].rearrange("p a t -> p (a t)"), ALU.mult).then_inc(hid_sq, 1)
                    dve.wait_ge(hid_hi, at(i, 4, base + g + 1))
                    nc.vector.tensor_tensor(hl[:, g % 2, :, :].rearrange("p k t -> p (k t)"), h[:, g % 2, :],
                                            hh[:, g % 2, :, :].rearrange("p k t -> p (k t)").bitcast(F32), ALU.subtract).then_inc(hid_lo, 1)

                splits(stage, 0, 2)
                group(0)
                n = (CV_GROUPS - 1) // 4
                with dve.Fori(0, n) as i:
                    for g in range(1, 5):
                        for j in range(3 * g - 1, 3 * g + 2):
                            split(s0 + j + LOOKAHEAD, i, 12)
                        group(g, i)
                for g in range(1 + 4 * n, CV_GROUPS):
                    splits(stage, 3 * g - 1, 3 * g + 2)
                    group(g)
                splits(stage, 3 * CV_GROUPS - 1, 3 * CV_GROUPS)
                ffn_out(s0 + 3 * CV_GROUPS)

            for s in range(LOOKAHEAD):
                split(s)
            dve.wait_ge(small_loaded, 16 * 6)
            step(nc.vector.tensor_copy(lvmask[:, :], arena[:, HY_SQ:HY_SQ + 8 * P]))
            pairs4 = lam_in[:, :, :].rearrange("p (a b) w -> p a b w", b=2)
            step(nc.vector.tensor_tensor(pairs4[:, :, 0, :], pairs4[:, :, 0, :], pairs4[:, :, 1, :], ALU.mult))
            sync()
            nc.vector.tensor_reduce(lam[:, 2:4], pairs4[:, :, 0, :], AX, ALU.add).then_inc(lam_sum, 1)
            dve.wait_ge(con_loaded, 16)
            for k in range(2):
                gk = qkg[:, k, :]
                step(nc.vector.tensor_tensor(ropeg[:, 2 * k, :, :], rope_x[0], gk.unsqueeze(1).to_broadcast([P, TT, 64]), ALU.mult))
                for a in range(2):
                    def half(v, b):
                        return v.rearrange("p t (x b h) -> p (t x) b h", b=2, h=16)[:, :, b, :]
                    gs = gk.rearrange("p (x b h) -> p x b h", b=2, h=16)[:, :, 1 - a, :]
                    for t in range(TT):
                        so = ropeg[:, 2 * k + 1, t, :].rearrange("p (x b h) -> p x b h", b=2, h=16)[:, :, a, :]
                        si = rope_x[1][:, t, :].rearrange("p (x b h) -> p x b h", b=2, h=16)[:, :, a, :]
                        step(nc.vector.tensor_tensor(so, si, gs, ALU.mult))
            step(nc.vector.tensor_scalar(subln[:, :], subln[:, :], 1.0 - LAMBDA_INIT, None, ALU.mult))
            dve.wait_ge(lam_exp, 1)
            step(nc.vector.tensor_tensor(lam[:, 2:3], lam[:, 0:1], lam[:, 1:2], ALU.subtract))
            sync()
            step(nc.vector.tensor_scalar(lam[:, 2:3], lam[:, 2:3], LAMBDA_INIT, None, ALU.add))

            prep(0)
            g = st["hy_in"]
            nat = ar(A_NAT, TT, 3072)
            splits(g, 0, 6)
            dve.wait_ge(bank_free, g.f0 + 4 + 4)
            for t in range(TT):
                rope(nat[:, t, 0:1024], xn[:, 0, :], 16, 32, rope_d[0][:, t, :], rope_d[1][:, t, :]).then_inc(rope_done, 1)
                dve.wait_ge(rope_done, t + 1)
            splits(g, 6, 10)
            dve.wait_ge(bank_free, g.f0 + 4 + 8)
            for t in range(TT):
                rope(nat[:, t, 1024:2048], xn[:, 0, :], 8, 64, rope_m[0][:, t, :], rope_m[1][:, t, :]).then_inc(rope_done, 1)
                dve.wait_ge(rope_done, 2 + t + 1)
            splits(g, 10, 12)
            blocks(0, 8)

            def hy_after(k):
                pass

            softmax(HY_PAIRS, Q_HY, hy_after)
            for t in range(TT):
                dve.wait_ge(sq_done, t + 1)
                nc.vector.tensor_reduce(var[:, t, 0:4], ar(HY_SQ, TT, CH)[:, t, :].rearrange("p (h w) -> p h w", w=P), AX, ALU.add)\
                    .then_inc(var_ready, 1)
            for t in range(TT):
                dve.wait_ge(pv_done, Q_HY + 6 * t + 6)
                step(nc.vector.reciprocal(rr[:, t, 8:12], rs[:, t, 8:12]))
                sync()
                step(heads_out(xn[:, t, CH:D], ps[6 + t][:, :], 8, 4, P, t))
                dve.wait_ge(rstd_ready, t + 1)
                dst = xn[:, t, 0:CH].rearrange("p (h w) -> p h w", w=P)
                step(nc.vector.tensor_tensor(dst, bank4(4 + t), rstd[:, t, 0:4].unsqueeze(2).to_broadcast([P, 4, P]), ALU.mult))
                sync()
                nc.vector.tensor_tensor(dst, dst, subln[:, :].unsqueeze(1).to_broadcast([P, 4, P]), ALU.mult).then_inc(xn_ready, 1)
            prep(1)
            splits(st["hy_out"], 0, 4)
            layer_norm(1, "mix", 0, CT, wait_a(st["hy_out"]))
            prep(2)
            ffn("ffn0", 0)
            layer_norm(2, "ffn", 0, TC, wait_nat(0))

            prep(3)
            g = st["gla"]
            splits(g, 0, 5)
            splits(g, 5, 7)
            gg = ar(GL_G, TT, CH)
            for t in range(TT):
                dve.wait_ge(ln_done, t + 1)
                nc.vector.scalar_tensor_tensor(gg[:, t, :], ps[4 + t][:, :], 0.0, gTmp[:, t, :], ALU.min, ALU.subtract).then_inc(g_ready, 1)
            splits(g, 7, 9)
            bT = ar(GL_B, 4, T)
            att = ar(GL_ATT, TT, 4, P)
            dve.wait_ge(b_copied, TT)
            dve.wait_ge(pool_init, 4)

            def two(v, s):
                return v.rearrange("p h (n a s) -> p (h n) a s", a=2, s=s)

            def level(lv):
                s = (LEVELS + [P])[lv - 1]
                b2, e2 = two(bT, s), two(gE, s)
                n = 4 * T // (2 * s)
                mid = b2[:, :, 0, s - 1:s].to_broadcast([P, n, s])
                if lv > 1:
                    dve.wait_ge(zlev_ready, lv - 1)
                ins = nc.vector.tensor_tensor(e2[:, :, 0, :], mid, b2[:, :, 0, :], ALU.subtract)
                if s < P:
                    ins = nc.vector.tensor_tensor(e2[:, :, 1, :], b2[:, :, 1, :], mid, ALU.subtract)
                ins.then_inc(d_ready, 1)

            def decayed(lv):
                s = (LEVELS + [P])[lv - 1]
                z2, e2 = two(ar(GL_Z, 2, 4, T)[:, lv % 2], s), two(gE, s)
                q2, k2 = two(qk[:, 0:4, :], s), two(qk[:, 4:8, :], s)
                dve.wait_ge(e_ready, lv)
                if lv >= 3:
                    dve.wait_ge(lv_ready, 2 * (lv - 2) + 2)
                nc.vector.tensor_tensor(z2[:, :, 0, :], k2[:, :, 0, :], e2[:, :, 0, :], ALU.mult)
                nc.vector.tensor_tensor(z2[:, :, 1, :], q2[:, :, 1, :], e2[:, :, 1, :], ALU.mult).then_inc(zlev_ready, 1)

            def place(lv):
                m = lvmask[:, lv * P:(lv + 1) * P].unsqueeze(1).to_broadcast([P, 4, P])
                for t in range(TT):
                    dve.wait_ge(lv_ready, 2 * lv + t + 1)
                    if lv:
                        dve.wait_ge(lv_done, 2 * (lv - 1) + t + 1)
                    nc.vector.copy_predicated(att[:, t, :, :], m, bank4(4 + 2 * (lv % 2) + t)).then_inc(lv_done, 1)

            level(1), decayed(1), level(2), decayed(2)
            splits(g, 9, 11)
            place(0), place(1)
            level(3), decayed(3), place(2), level(4), decayed(4)
            splits(g, 11, 13)
            place(3)
            for lv in range(5, 8):
                level(lv), decayed(lv), place(lv - 1)
            level(8), decayed(8), place(7)
            for t in range(TT):
                rv = ar(A_NAT, TT, 2048)[:, t, D:2 * D].rearrange("p (h w) -> p h w", w=T)
                dve.wait_ge(r_act, t + 1)
                nc.vector.tensor_tensor(rv, rv, glag[:, :].unsqueeze(1).to_broadcast([P, 4, T]), ALU.mult).then_inc(sr_done, 1)
            for t in range(TT):
                dve.wait_ge(sq_done, TT + t + 1)
                nc.vector.tensor_reduce(var[:, t, 0:4], xn[:, t, :].rearrange("p (h w) -> p h w", w=T), AX, ALU.add).then_inc(var_ready, 1)
            for t in range(TT):
                dve.wait_ge(rstd_ready, 2 * 3 + t + 1)
                for hp in range(2):
                    step(nc.vector.tensor_tensor(xn[:, t, hp * CH:(hp + 1) * CH].rearrange("p (h w) -> p h w", w=T), bank2(t + 2 * hp),
                                                 rstd[:, t, 2 * hp:2 * hp + 2].unsqueeze(2).to_broadcast([P, 2, T]), ALU.mult))
                sync()
                dve.wait_ge(sr_done, t + 1)
                nc.vector.tensor_tensor(xn[:, t, :], xn[:, t, :], ar(A_NAT, TT, 2048)[:, t, D:2 * D], ALU.mult).then_inc(xn_ready, 1)
            prep(4)
            splits(st["gla_out"], 0, 4)
            layer_norm(4, "mix", 1, CT, wait_a(st["gla_out"]))
            prep(5)
            ffn("ffn1", SQ_GROUPS)
            layer_norm(5, "ffn", 1, TC, wait_nat(1))

            rms_apply(6, "attn_norm", X)
            prep(6)
            g = st["qkv"]
            splits(g, 0, 6)
            nat = ar(A_NAT, TT, 1536)
            tmp = ar(QK_TMP, 1280)
            kd = ar(QK_KD, TT, CH)
            for t in range(TT):
                dve.wait_ge(sq_done, 2 * TT + t + 1)
                nc.vector.tensor_reduce(var[:, t, 0:20], ar(QK_SQ, 1280).rearrange("p (h w) -> p h w", w=64), AX, ALU.add).then_inc(var_ready, 1)
            for t in range(TT):
                x = nat[:, t, 0:1280]
                x3 = x.rearrange("p (h w) -> p h w", w=64)
                dve.wait_ge(rstd_ready, 2 * 7 + t + 1)
                step(nc.vector.tensor_tensor(x3, x3, rstd[:, t, 0:20].unsqueeze(2).to_broadcast([P, 20, 64]), ALU.mult))
                sync()
                for k, (a, n) in enumerate(((0, 16), (16, 4))):
                    part = nat[:, t, a * 64:(a + n) * 64]
                    pt = tmp[:, a * 64:(a + n) * 64]
                    x5 = part.rearrange("p (h x b w) -> p h x b w", x=2, b=2, w=16)
                    t5 = pt.rearrange("p (h x b w) -> p h x b w", x=2, b=2, w=16)
                    s5 = ropeg[:, 2 * k + 1, t, :].rearrange("p (x b w) -> p x b w", b=2, w=16)
                    for b in range(2):
                        step(nc.vector.tensor_tensor(t5[:, :, :, b, :], x5[:, :, :, 1 - b, :],
                                                     s5[:, :, b, :].unsqueeze(1).to_broadcast([P, n, 2, 16]), ALU.mult))
                    sync()
                    p3 = part.rearrange("p (h w) -> p h w", w=64)
                    step(nc.vector.tensor_tensor(p3, p3, ropeg[:, 2 * k, t, :].unsqueeze(1).to_broadcast([P, n, 64]), ALU.mult))
                sync()
                step(nc.vector.tensor_tensor(nat[:, t, 0:D], nat[:, t, 0:D], tmp[:, 0:D], ALU.add))
                kdt = kd[:, t, :].rearrange("p (g u w) -> p g u w", u=2, w=64)
                k3 = nat[:, t, D:1280].rearrange("p (g w) -> p g w", w=64)
                tk = tmp[:, D:1280].rearrange("p (g w) -> p g w", w=64)
                for u in range(2):
                    ins = nc.vector.tensor_tensor(kdt[:, :, u, :], k3, tk, ALU.add)
                ins.then_inc(rope_done, 1)
                dve.wait_ge(rope_done, 4 + t + 1)
            blocks(8, 6)

            def qk_after(k):
                if k % 8 == 7:
                    t = k // 8
                    dve.wait_ge(pv_done, Q_QK + 8 * t + 8)
                    step(nc.vector.reciprocal(rr[:, t, 0:16], rs[:, t, 0:16]))
                    sync()
                    heads_out(xn[:, t, 0:CH], ps[4 + 2 * t][:, :], 0, 8, 64, t)
                    heads_out(xn[:, t, CH:D], ps[5 + 2 * t][:, :], 8, 8, 64, t).then_inc(xn_ready, 1)

            softmax(QK_PAIRS, Q_QK, qk_after)
            prep(7)
            splits(st["wo"], 0, 4)
            residual(CT, wait_a(st["wo"]))

            for l in range(2):
                n = (8, 12)[l]
                p = (8, 12)[l]
                rms_apply(n, f"mem_norm{l}", mem)
                prep(p)
                splits(st[f"mem{l}"], 0, 8)
                rms_apply(n + 1, f"xattn_norm{l}", X)
                prep(p + 1)
                splits(st[f"xq{l}"], 0, 4)

                def xa_after(k):
                    t, j = k // 2, k % 2
                    dve.wait_ge(pv_done, Q_XA[l] + k + 1)
                    step(nc.vector.reciprocal(rr[:, t, 2 * j:2 * j + 2], rs[:, t, 2 * j:2 * j + 2]))
                    sync()
                    ins = heads_out(xn[:, t, j * CH:(j + 1) * CH], ps[4 + 2 * t + j][:, :], 2 * j, 2, T, t)
                    if j == 1:
                        ins.then_inc(xn_ready, 1)

                softmax(XA_PAIRS, Q_XA[l], lambda k: None)
                for k in range(4):
                    xa_after(k)
                prep(p + 2)
                splits(st[f"xo{l}"], 0, 4)
                residual(CT, wait_a(st[f"xo{l}"]))
                rms_apply(n + 2, f"ffn_norm{l}", X)
                prep(p + 3)
                if l == 0:
                    dve.wait_ge(cw_done, 1)
                conv(f"conv{l}", l, 2 * SQ_GROUPS + CV_GROUPS * l, 2 * CV_GROUPS * l)
                residual(TC, wait_nat(2 + l))
                if l == 0:
                    rms_apply(11, "pool_norm", X)
                    gs = gain("pool_scale")
                    for t in range(TT):
                        for c in range(2):
                            cs = slice(c * CH, (c + 1) * CH)
                            dve.wait_ge(py_ready, 2 * t + c + 1)
                            step(nc.vector.tensor_tensor(xn[:, t, cs], ps[4 + 2 * t + c][:, :], gs[:, cs], ALU.mult))
                            sync()
                            ins = nc.vector.tensor_tensor(X[:, t, cs], X[:, t, cs], xn[:, t, cs], ALU.add)
                        ins.then_inc(x_ready, 1)
            rms_apply(15, "final_norm", X)

        @block.tensor
        def _(pe):
            def slab(s, i=None, step=0):
                pe.wait_ge(wl_ready, at(i, step, s + 1))

            def prep(p, src, w, v, stage=None):
                for t in range(TT):
                    pe.wait_ge(w, v(t))
                    for half in range(2):
                        for k in range(4):
                            c = (4 * half + k) * P
                            ins = nc.tensor.transpose(ps[t + 2 * half][:, k * P:(k + 1) * P], src[:, t, c:c + P], ident)
                        ins.then_inc(tr_done, 1)
                pe.wait_ge(bank_free, stage.f0 + 4)

            def chunk_a(stage, c, j, i=None, cstep=0, free=None):
                for half in range(2):
                    s = stage.s0 + j + half
                    slab(s, i, 2 * cstep)
                    wa, wb = slab_a(wh, s % RING), slab_a(wl, s % RING)
                    for t in range(TT):
                        if half == 0:
                            pe.wait_ge(bank_free, at(i, 2 * cstep, (stage.f0 if free is None else free) + 2 * c + t + 1))
                        o = ps[2 * (c % 2) + t][:, :]
                        ts = slice(t * P, (t + 1) * P)
                        for k in range(4):
                            kt = 4 * half + k
                            nc.tensor.matmul(o, xh[:, kt, ts], wa[:, k, :], start=(kt == 0), stop=False)
                            nc.tensor.matmul(o, xh[:, kt, ts], wb[:, k, :], start=False, stop=False)
                            ins = nc.tensor.matmul(o, xl[:, kt, ts], wa[:, k, :], start=False, stop=(kt == KT - 1))
                        if half == 1 and t == 0:
                            ins.then_inc(bank_ready, 1)
                    ins.then_inc(slab_used, 1)

            def slab_up(s, bank, tiles=(0, 1), i=None, step=0):
                slab(s, i, step)
                wa, wb = slab_b(wh, s % RING), slab_b(wl, s % RING)
                for a in tiles:
                    o = bank2(bank)[:, a, :]
                    cs = slice(a * P, (a + 1) * P)
                    for kt in range(KT):
                        nc.tensor.matmul(o, wa[:, kt, cs], xh[:, kt, :], start=(kt == 0), stop=False)
                        nc.tensor.matmul(o, wa[:, kt, cs], xl[:, kt, :], start=False, stop=False)
                        ins = nc.tensor.matmul(o, wb[:, kt, cs], xh[:, kt, :], start=False, stop=(kt == KT - 1))
                ins.then_inc(slab_used, 1)

            def open_down():
                for b in range(4, 8):
                    nc.tensor.matmul(ps[b][:, :], zero_bf[:, 0:P], zero_bf[:, :], start=True, stop=False, skip_group_check=True)

            def slab_down(s, par, i=None, step=0, last=False):
                slab(s, i, step)
                wa, wb = slab_dn(wh, s % RING), slab_dn(wl, s % RING)
                for k in range(2):
                    for n in range(KT):
                        o = bank2(4 + n // 2)[:, n % 2, :]
                        cs = slice(n * P, (n + 1) * P)
                        nc.tensor.matmul(o, wa[:, k, cs], hh[:, par, k, :], start=False, stop=False, skip_group_check=True)
                        nc.tensor.matmul(o, wa[:, k, cs], hl[:, par, k, :], start=False, stop=False, skip_group_check=True)
                        ins = nc.tensor.matmul(o, wb[:, k, cs], hh[:, par, k, :], start=False, stop=last and k == 1, skip_group_check=True)
                ins.then_inc(slab_used, 1)

            def ffn_nat(f):
                pe.wait_ge(ff_outA, 2 * f + 2)
                pe.wait_ge(ff_outD, 2 * f + 2)
                for t in range(TT):
                    for c in range(2):
                        for k in range(4):
                            ins = nc.tensor.transpose(ps[2 * c + t][:, k * P:(k + 1) * P], yT[:, 4 * c + k, t * P:(t + 1) * P], ident)
                        ins.then_inc(ff_nat, 1)

            def ffn(name, f, base):
                stage = st[name]
                s0 = stage.s0

                def up(g, i=None):
                    pe.wait_ge(bank_free, at(i, 2, stage.f0 + g + 3))
                    slab_up(s0 + 2 * g - 1 if g else s0, g % 2, i=i, step=4)

                def down(g, i=None, last=False):
                    pe.wait_ge(hid_lo, at(i, 2, base + g + 1))
                    slab_down(s0 + 2 * g + 2 if not last else s0 + 2 * g + 1, g % 2, i, 4, last)

                open_down()
                up(0)
                with pe.Fori(0, (SQ_GROUPS - 2) // 2) as i:
                    for g in (1, 2):
                        up(g, i)
                        down(g - 1, i)
                up(SQ_GROUPS - 1)
                down(SQ_GROUPS - 2)
                down(SQ_GROUPS - 1, last=True)
                ffn_nat(f)

            def conv(name, f, base):
                stage = st[name]
                s0 = stage.s0

                def up(g, i=None):
                    s = s0 + 3 * g - 1 if g else s0
                    for a in range(2):
                        pe.wait_ge(bank_free, at(i, 8, stage.f0 + 2 * g + a + 1))
                        slab_up(s + a, 2 * (g % 2) + a, i=i, step=12)

                def down(g, i=None, last=False):
                    pe.wait_ge(hid_lo, at(i, 4, base + g + 1))
                    slab_down(s0 + 3 * g + 4 if not last else s0 + 3 * g + 2, g % 2, i, 12, last)

                open_down()
                up(0)
                n = (CV_GROUPS - 1) // 4
                with pe.Fori(0, n) as i:
                    for g in range(1, 5):
                        up(g, i)
                        down(g - 1, i)
                for g in range(1 + 4 * n, CV_GROUPS):
                    up(g)
                    down(g - 1)
                down(CV_GROUPS - 1, last=True)
                ffn_nat(f)

            def blocks(base, fills, src, w, v):
                ea = (base + 1) // 2
                for f in range(fills):
                    pe.wait_ge(w, v(f))
                    if f >= 4:
                        pe.wait_ge(blk_act if f % 2 == 0 else blk_dve, ea + (f - 4) // 2 + 1)
                    for a in range(2):
                        for t in range(TT):
                            ins = nc.tensor.transpose(bank2(4 + f % 4)[:, a, t * P:(t + 1) * P], src(2 * f + a, t), ident)
                    ins.then_inc(blk_T, 1)
                pe.wait_ge(blk_act, ea + (fills + 1) // 2)
                pe.wait_ge(blk_dve, ea + fills // 2)

            halves = [0]

            def scores(q, kind, t, j):
                w = width(kind, t)
                for u in range(2):
                    if u and kind in ("diff", "gqa"):
                        halves[0] += 1
                        ins.then_inc(half_done, 1)
                        pe.wait_ge(half_done, halves[0])
                    o = bank2(q % 2)[:, u, 0:w]
                    ts = slice(t * P, (t + 1) * P)
                    if kind in ("diff", "moba"):
                        nc.tensor.matmul(bank2(q % 2)[:, u, t * P:(t + 1) * P], ident, cmask, start=True, stop=False, skip_group_check=True)
                    if kind == "diff":
                        us = slice(64 * u, 64 * u + 64)
                        ins = nc.tensor.matmul(o, qk[us, j, ts], qk[us, 4 + j, 0:w], start=False, stop=True, skip_group_check=True)
                    elif kind == "moba":
                        ins = nc.tensor.matmul(o, qk[:, 8 + 2 * j + u, ts], qk[:, 12 + 2 * j + u, 0:w], start=False, stop=True, skip_group_check=True)
                    elif kind == "gqa":
                        us = slice(64 * u, 64 * u + 64)
                        ins = nc.tensor.matmul(o, qk[us, j, ts], qk[us, 8 + j // 2, :], start=True, stop=True)
                    else:
                        for k in range(2):
                            b = 2 * (2 * j + u) + k
                            ins = nc.tensor.matmul(o, qk[:, b, ts], qk[:, 8 + b, :], start=(k == 0), stop=(k == 1))
                ins.then_inc(scores_ready, 1)

            ndiff = [0]

            def probs_T(q, kind, t, j):
                w = width(kind, t)
                p = ar(pbuf(kind)[0], 2, 2, T)[:, q % 2]
                if kind == "diff":
                    ndiff[0] += 1
                    pe.wait_ge(diff_w, ndiff[0])
                else:
                    pe.wait_ge(exp_done, q + 1)
                for u in range(1 if kind == "diff" else 2):
                    for k in range(w // P):
                        c = u * w + k * P
                        ins = nc.tensor.transpose(ps[2 + q % 2][:, c:c + P], p[:, u, k * P:(k + 1) * P], ident)
                ins.then_inc(pT_ready, 1)

            def values(q, kind, t, j, v):
                w = width(kind, t)
                pT = ar(pbuf(kind)[1], 2, CH)[:, q % 2]
                pe.wait_ge(pT_copied, q + 1)
                n = w // P
                for u in range(1 if kind == "diff" else 2):
                    if kind == "diff":
                        o, vc, vw = ps[4 + t][:, j * P:(j + 1) * P], 2048 + j * P, P
                    elif kind == "moba":
                        h = 2 * j + u
                        o, vc, vw = ps[6 + t][:, h * P:(h + 1) * P], 2560 + h * P, P
                    elif kind == "gqa":
                        h = 2 * j + u
                        o, vc, vw = ps[4 + 2 * t + h // 8][:, (h % 8) * 64:(h % 8 + 1) * 64], 1280 + (h // 4) * 64, 64
                    else:
                        h = 2 * j + u
                        o, vc, vw = ps[4 + 2 * t + j][:, u * T:(u + 1) * T], h * T, T
                    for k in range(n):
                        c = u * w + k * P
                        ins = nc.tensor.matmul(o, pT[:, c:c + P], v[:, k, vc:vc + vw], start=(k == 0), stop=(k == n - 1))
                ins.then_inc(pv_done, 1)

            def attention(pairs, q0, v):
                scores(q0, *pairs[0])
                for k, pair in enumerate(pairs):
                    if k + 1 < len(pairs):
                        scores(q0 + k + 1, *pairs[k + 1])
                    probs_T(q0 + k, *pair)
                    if k:
                        values(q0 + k - 1, *pairs[k - 1], v)
                values(q0 + len(pairs) - 1, *pairs[-1], v)

            def x_at(u):
                return lambda t: 2 * u + t + 1

            pe.wait_ge(con_loaded, 16)
            pe.wait_ge(cw_loaded, 16 * 8)
            for l in range(2):
                for a in range(4):
                    c = (4 * l + a) * 2 * FT2
                    ins = nc.tensor.transpose(ps[7][:, c:c + 2 * FT2], xn[0:2 * FT2, l, a * P:(a + 1) * P], con[0:2 * FT2, C_IDENT:C_IDENT + 2 * FT2])
            ins.then_inc(cw_T, 1)

            prep(0, X, x_loaded, lambda t: 16, st["hy_in"])
            with pe.Fori(0, 3) as i:
                for c in range(2):
                    chunk_a(st["hy_in"], c, 2 * c, i, 2)
            nat = ar(A_NAT, TT, 3072)
            blocks(0, 8, lambda b, t: nat[:, t, b * P:(b + 1) * P], rope_done, lambda f: 2 if f < 4 else 4)
            attention(HY_PAIRS, Q_HY, nat)
            prep(1, xn, xn_ready, x_at(0), st["hy_out"])
            for c in range(2):
                chunk_a(st["hy_out"], c, 2 * c)
            prep(2, X, x_ready, x_at(0), st["ffn0"])
            ffn("ffn0", 0, 0)

            prep(3, X, x_ready, x_at(1), st["gla"])
            g = st["gla"]
            for j in range(4):
                slab_up(g.s0 + j, j)
            pe.wait_ge(bank_free, g.f0 + 5)
            slab_up(g.s0 + 4, 0, tiles=(1,))
            pe.wait_ge(bank_free, g.f0 + 9)
            chunk_a(g, 0, 5, free=g.f0 + 5)
            pe.wait_ge(gla_small, 32)
            pe.wait_ge(pool_init, 3)
            for t in range(TT):
                nc.tensor.matmul(ps[4 + t][:, :], one_row[:, :], bgate, start=True, stop=False)
                nc.tensor.matmul(ps[4 + t][:, :], hlow[:, t * P:(t + 1) * P], wup, start=False, stop=True).then_inc(z_ready, 1)
            chunk_a(g, 1, 7, free=g.f0 + 5)
            for t in range(TT):
                pe.wait_ge(g_ready, t + 1)
                for h in range(4):
                    ins = nc.tensor.matmul(bank4(6 + t)[:, h, :], ar(GL_G, TT, CH)[:, t, h * P:(h + 1) * P], tri, start=True, stop=True)
                ins.then_inc(b_ready, 1)

            def level(lv):
                z = ar(GL_Z, 2, 4, T)[:, lv % 2]
                if lv:
                    pe.wait_ge(zlev_ready, lv)
                if lv == 1:
                    pe.wait_ge(b_copied, TT)
                for t in range(1 if lv == 8 else TT):
                    ts = slice(t * P, (t + 1) * P)
                    if lv >= 2:
                        pe.wait_ge(lv_done, 2 * (lv - 2) + t + 1)
                    for h in range(4):
                        o = bank4(4 + 2 * (lv % 2) + t)[:, h, :]
                        if lv == 0:
                            ins = nc.tensor.matmul(o, qk[:, 4 + h, ts], qk[:, h, ts], start=True, stop=True)
                        elif lv == 8:
                            ins = nc.tensor.matmul(o, z[:, h, 0:P], z[:, h, P:T], start=True, stop=True)
                        else:
                            ins = nc.tensor.matmul(o, z[:, h, ts], z[:, h, ts], start=True, stop=True)
                    ins.then_inc(lv_ready, 1)

            pe.wait_ge(g_ready, TT)
            level(0), level(1)
            chunk_a(g, 2, 9, free=g.f0 + 5)
            level(2), level(3)
            chunk_a(g, 3, 11, free=g.f0 + 5)
            for lv in range(4, 9):
                level(lv)
            vv = ar(A_NAT, TT, 2048)
            att = ar(GL_ATT, TT, 4, P)
            pe.wait_ge(bank_free, g.f0 + 4 + 5 + 8)
            pe.wait_ge(lv_done, 16)
            pe.wait_ge(a01_done, 1)
            for t in range(TT):
                for h in range(4):
                    o = bank2(t + 2 * (h // 2))[:, h % 2, :]
                    if t == 1:
                        nc.tensor.matmul(o, ar(GL_A01, 4, P)[:, h, :], vv[:, 0, h * T:(h + 1) * T], start=True, stop=False)
                    ins = nc.tensor.matmul(o, att[:, t, h, :], vv[:, t, h * T:(h + 1) * T], start=(t == 0), stop=True)
                ins.then_inc(go_ready, 1)
            prep(4, xn, xn_ready, x_at(1), st["gla_out"])
            for c in range(2):
                chunk_a(st["gla_out"], c, 2 * c)
            prep(5, X, x_ready, x_at(2), st["ffn1"])
            ffn("ffn1", 1, SQ_GROUPS)

            prep(6, xn, xn_ready, x_at(2), st["qkv"])
            for c in range(3):
                chunk_a(st["qkv"], c, 2 * c)
            nat = ar(A_NAT, TT, 1536)
            kd = ar(QK_KD, TT, CH)
            blocks(8, 6, lambda b, t: nat[:, t, b * P:(b + 1) * P] if b < 8 else kd[:, t, (b - 8) * P:(b - 7) * P], rope_done, lambda f: 6)
            attention(QK_PAIRS, Q_QK, nat)
            prep(7, xn, xn_ready, x_at(3), st["wo"])
            for c in range(2):
                chunk_a(st["wo"], c, 2 * c)

            for l in range(2):
                p = (8, 12)[l]
                e = (4, 9)[l]
                g = st[f"mem{l}"]
                prep(p, xn, xn_ready, x_at(e), g)
                for j in range(4):
                    slab_up(g.s0 + j, j)
                pe.wait_ge(bank_free, g.f0 + 8)
                for c in range(2):
                    chunk_a(g, c, 4 + 2 * c, free=g.f0 + 4)
                g = st[f"xq{l}"]
                prep(p + 1, xn, xn_ready, x_at(e + 1), g)
                for j in range(4):
                    slab_up(g.s0 + j, j)
                pe.wait_ge(bank_free, g.f0 + 8)
                attention(XA_PAIRS, Q_XA[l], ar(XA_V, TT, D))
                g = st[f"xo{l}"]
                prep(p + 2, xn, xn_ready, x_at(e + 2), g)
                for c in range(2):
                    chunk_a(g, c, 2 * c)
                prep(p + 3, xn, xn_ready, x_at(e + 3), st[f"conv{l}"])
                conv(f"conv{l}", 2 + l, 2 * SQ_GROUPS + CV_GROUPS * l)
                if l == 0:
                    M = ar(PO_M, TT, 4 * T)
                    pe.wait_ge(pool_loaded, 32)
                    for t in range(TT):
                        pe.wait_ge(xn_ready, 2 * 8 + t + 1)
                    for ct in range(KT):
                        for t in range(TT):
                            ins = nc.tensor.matmul(bank2(ct // 2)[:, ct % 2, :], xn[:, t, ct * P:(ct + 1) * P],
                                                   M[:, t, (ct // 2) * T:(ct // 2 + 1) * T], start=(t == 0), stop=(t == 1))
                        if ct % 2:
                            ins.then_inc(pmix_ready, 1)
                    pe.wait_ge(pmix_done, 4)
                    for t in range(TT):
                        for gr in range(4):
                            o = ps[4 + 2 * t + gr // 2][:, (gr % 2) * T:(gr % 2 + 1) * T]
                            for k in range(2):
                                ins = nc.tensor.matmul(o, ar(PO_MIX, 8, T)[:, 2 * gr + k, t * P:(t + 1) * P], ar(PO_W, 8, T)[:, 2 * gr + k, :],
                                                       start=(k == 0), stop=(k == 1))
                            if gr % 2:
                                ins.then_inc(py_ready, 1)


def constants():
    f = np.float32

    def rope(dim):
        inv = (f(1.0) / (f(10000.0) ** (np.arange(0, dim, 2, dtype=f) / f(dim)))).astype(f)
        ang = np.arange(T, dtype=f)[:, None] * inv[None, :]
        c, s = np.cos(ang), np.sin(ang)
        return np.concatenate([c, c], 1), np.concatenate([-s, s], 1)

    def axial():
        row = np.repeat(np.arange(T // 64, dtype=f), 64)
        col = np.tile(np.arange(64, dtype=f), T // 64)
        inv = f(10000.0) ** (-np.arange(16, dtype=f) / f(16))
        c, s = [], []
        for pos in (row, col):
            ang = pos[:, None] * inv
            c += [np.cos(ang), np.cos(ang)]
            s += [-np.sin(ang), np.sin(ang)]
        return np.concatenate(c, 1), np.concatenate(s, 1)

    def tiles(a):
        return a.reshape(TT, P, -1).transpose(1, 0, 2).reshape(P, -1)

    i = np.arange(P)
    parts = [np.eye(P), np.where(i[None, :] <= i[:, None], 0.0, NEG), np.where(i[:, None] <= i[None, :], 1.0 / 16, 0.0)]
    for c, s in (rope(64), rope(128), axial()):
        parts += [tiles(c), tiles(s)]
    table = np.concatenate([np.asarray(p, dtype=f) for p in parts], 1)
    j, q = i[:, None], i[None, :]
    levels = [j == q] + [(j // (2 * s) == q // (2 * s)) & (j % (2 * s) < s) & (q % (2 * s) >= s) for s in LEVELS]
    levels = np.concatenate(levels, 1).astype(f)
    pool = np.zeros((T, 4, T), f)
    for gr, w in enumerate((2, 4, 8, 16)):
        for t in range(T):
            lo, hi = max(t - w // 2, 0), min(t + w - w // 2, T)
            pool[lo:hi, gr, t] = f(1.0) / f(hi - lo)
            pool[t, gr, t] -= f(1.0)
    return {"c_table": np.ascontiguousarray(table), "c_levels": np.ascontiguousarray(levels), "c_pool": pool.reshape(T, 4 * T)}


def kernel(**inputs):
    import concourse.bacc as bacc
    from concourse.bass_utils import run_bass_kernel_spmd

    a = {k: np.asarray(v) for k, v in inputs.items()}
    arrays = {"x": a["x"], "hy_w_in": a["hy_w_in"][0], "diff_lambda": a["diff_lambda"][0], "diff_subln": a["diff_subln"][0],
              "hy_w_out": a["hy_w_out"][0], "gla_w_in": a["gla_w_in"][0], "gla_w_gate_up": a["gla_w_gate_up"][0],
              "gla_b_gate": a["gla_b_gate"][0], "gla_norm": a["gla_norm"][0], "gla_w_out": a["gla_w_out"][0],
              "ffn_w1": a["ffn_w1"], "ffn_w2": a["ffn_w2"], "mem": a["mem_2"], "attn_norm": a["attn_norm_2"][0],
              "attn_w_qkv": a["attn_w_qkv_2"][0], "attn_q_gain": a["attn_q_gain_2"][0], "attn_k_gain": a["attn_k_gain_2"][0],
              "attn_w_o": a["attn_w_o_2"][0], "pool_norm": a["pool_norm_2"][0], "pool_w": a["pool_w_2"][0],
              "pool_scale": a["pool_scale_2"][0], "xattn_w_q": a["xattn_w_q_2"], "xattn_w_kv": a["xattn_w_kv_2"],
              "xattn_w_o": a["xattn_w_o_2"], "ffn_w_up": a["ffn_w_up_2"], "ffn_conv_w": a["ffn_conv_w_2"],
              "ffn_conv_b": a["ffn_conv_b_2"], "ffn_w_down": a["ffn_w_down_2"], "final_norm": a["final_norm_2"]}
    for l in range(DEPTH):
        for kind in ("mix", "ffn"):
            arrays[f"ln_{kind}_g{l}"] = a[f"ln_{kind}_g"][l]
            arrays[f"ln_{kind}_b{l}"] = a[f"ln_{kind}_b"][l]
        arrays[f"mem_norm{l}"] = a["mem_norm_2"][l]
        arrays[f"xattn_norm{l}"] = a["xattn_norm_2"][l]
        arrays[f"ffn_norm{l}"] = a["ffn_norm_2"][l]
    arrays.update(constants())
    arrays = {f"in_{k}": np.ascontiguousarray(v) for k, v in arrays.items()}
    nc = bacc.Bacc("TRN2", target_bir_lowering=False, num_devices=1)
    d = {k[3:]: nc.dram_tensor(k, v.shape, mybir.dt.from_np(v.dtype), kind="ExternalInput").ap() for k, v in arrays.items()}
    d["out"] = nc.dram_tensor("out", (1, T, D), F32, kind="ExternalOutput").ap()
    build(nc, d)
    r = run_bass_kernel_spmd(nc, [arrays], core_ids=[0])
    return r.results[0]["out"]
```

```python
from contextlib import ExitStack

import numpy as np
import concourse.bass as bass
from concourse import mybir
from concourse.alu_op_type import AluOpType as ALU

ACT = mybir.ActivationFunctionType
AX = mybir.AxisListType.X
F32 = mybir.dt.float32
F32R = mybir.dt.float32r
BF16 = mybir.dt.bfloat16
U8 = mybir.dt.uint8

P = 128
D = 1024
T = 256
TT = T // P
KT = D // P
D_FF = 4096
D_FF2 = 2816
DEPTH = 2
ALPHA = (2 * DEPTH) ** 0.25
EPS_LN = 1e-5
EPS_RMS1 = 1e-5
EPS_RMS2 = 1e-6
LAMBDA_INIT = 0.2
NEG = -3.0e38

SLAB = 2048
RING = 4
RAWS = 2
LOOKAHEAD = 3
CH = 512
GLA_COLS = 3088
SQ_GROUPS = D_FF // 256
CV_GROUPS = D_FF2 // 256
FT2 = D_FF2 // P
LEVELS = [1, 2, 4, 8, 16, 32, 64]

C_IDENT = 0
C_MASK = C_IDENT + P
C_TRI = C_MASK + P
C_ROPE_D = C_TRI + P
C_ROPE_M = C_ROPE_D + 4 * 64
C_ROPE_X = C_ROPE_M + 4 * 128
C_ALL = C_ROPE_X + 4 * 64

A_NAT = 0
HY_P, HY_PT, HY_SQ = 6144, 7168, 8192
SQ_R, SQ_H = 0, 1024
CV_G, CV_V, CV_S, CV_H = 0, 1024, 2048, 3072
GL_G, GL_B, GL_Z, GL_ATT, GL_A01 = 4096, 5120, 6144, 8192, 9216
QK_SQ, QK_TMP, QK_P, QK_PT = 3072, 4096, 3072, 4096
XA_P, XA_PT, XA_K, XA_V = 0, 1024, 5632, 7680
PO_M, PO_W = 0, 2048
A_ALL = 9728


class Stage:
    slabs = frees = readies = 0

    def __init__(self, n, evacs, readies=0):
        self.s0, self.f0, self.r0 = Stage.slabs, Stage.frees, Stage.readies
        Stage.slabs += n
        Stage.frees += 4 + evacs
        Stage.readies += readies


def plan():
    Stage.slabs = Stage.frees = Stage.readies = 0
    st = {}
    st["hy_in"] = Stage(12, 12, 6)
    st["hy_out"] = Stage(4, 0, 2)
    st["ffn0"] = Stage(2 * SQ_GROUPS, SQ_GROUPS)
    st["gla"] = Stage(13, 5 + 8, 4)
    st["gla_out"] = Stage(4, 0, 2)
    st["ffn1"] = Stage(2 * SQ_GROUPS, SQ_GROUPS)
    for i in range(2):
        st[f"mem{i}"] = Stage(8, 4 + 4, 2)
        if i == 0:
            st["qkv"] = Stage(6, 6, 3)
            st["wo"] = Stage(4, 0, 2)
        st[f"xq{i}"] = Stage(4, 4)
        st[f"xo{i}"] = Stage(4, 0, 2)
        st[f"conv{i}"] = Stage(3 * CV_GROUPS, 2 * CV_GROUPS)
    return st, Stage.slabs


NORMS = ["hy_heads", "ln_mix0", "ln_ffn0", "gla_heads", "ln_mix1", "mem0", "ln_ffn1", "attn", "qk_k", "qk_q0", "qk_q1",
         "xattn0", "ffn0", "mem1", "pool", "xattn1", "ffn1", "final"]
PREPS = ["hy_in", "hy_out", "ffn0", "gla", "gla_out", "ffn1", "mem0", "qkv", "wo", "xq0", "xo0", "conv0", "mem1", "xq1", "xo1", "conv1"]
XNS = ["hy_heads", "gla_heads", "attn", "qk_heads", "xattn0", "x_heads0", "ffn0", "pool", "xattn1", "x_heads1", "ffn1", "final"]
XS = ["mix0", "ffn0", "mix1", "ffn1", "wo", "xo0", "conv0", "pool", "xo1", "conv1"]
QKV_COLS = [D, 0, CH]
QK_HEADS = [(16, 4), (0, 8), (8, 8)]


def xn_count(name, t=TT - 1):
    return 2 * XNS.index(name) + t + 1


def x_count(name, t=TT - 1):
    return 2 * XS.index(name) + t + 1


def norm_count(name, t=TT - 1):
    return 2 * NORMS.index(name) + t + 1


def at(i, step, k):
    return k if i is None else i * step + k


def build(nc, d):
    st, S = plan()
    out = d["out"]
    with ExitStack() as ctx:
        def sb(name, shape, dt=F32):
            return ctx.enter_context(nc.sbuf_tensor(name, shape, dt))

        def sem(name):
            return ctx.enter_context(nc.semaphore(name))

        raw = sb("raw", [P, RAWS, SLAB])
        wh = sb("wh", [P, RING, SLAB], F32R)
        wl = sb("wl", [P, RING, SLAB], F32R)
        xh = sb("xh", [P, KT, T], F32R)
        xl = sb("xl", [P, KT, T], F32R)
        hh = sb("hh", [P, 2, 2, T], F32R)
        hl = sb("hl", [P, 2, 2, T], F32R)
        X = sb("X", [P, TT, D])
        xn = sb("xn", [P, TT, D])
        arena = sb("arena", [P, A_ALL])
        qk = sb("qk", [P, 16, T])
        gains = sb("gains", [P, 4, D])
        con = sb("con", [P, C_ALL])
        lvmask = sb("lvmask", [P, 8 * P], U8)
        zero_bf = sb("zero_bf", [P, CH], BF16)
        bfc = sb("bfc", [P, 2 * P], BF16)
        lam = sb("lam", [P, 4])
        subln = sb("subln", [P, P])
        qkg = sb("qkg", [P, 2, 64])
        ropeg = sb("ropeg", [P, 4, TT, 64])
        glag = sb("glag", [P, T])
        cw = sb("cw", [P, 2, 4, 2 * FT2])
        var = sb("var", [P, TT, 20])
        rstd = sb("rstd", [P, TT, 20])
        mhalf = sb("mhalf", [P, 20])
        bst = sb("bst", [P, TT, 2, 6])
        mv = sb("mv", [P, TT, 2])
        mx = sb("mx", [P, TT, 24])
        nb = sb("nb", [P, TT, 24])
        rs = sb("rs", [P, TT, 24])
        rr = sb("rr", [P, TT, 24])
        qsc = sb("qsc", [P, TT, 2, 16])
        one_row = sb("one_row", [1, P])
        ps = [ctx.enter_context(nc.psum_tensor(f"ps{i}", [P, CH], F32)) for i in range(8)]

        ident = con[:, C_IDENT:C_IDENT + P]
        cmask = con[:, C_MASK:C_MASK + P]
        tri = con[:, C_TRI:C_TRI + P]

        def table(col, w):
            return con[:, col:col + TT * w].rearrange("p (t w) -> p t w", t=TT)

        rope_d = table(C_ROPE_D, 64), table(C_ROPE_D + 128, 64)
        rope_m = table(C_ROPE_M, 128), table(C_ROPE_M + 256, 128)
        rope_x = table(C_ROPE_X, 64), table(C_ROPE_X + 128, 64)

        def ar(col, *dims):
            n = int(np.prod(dims))
            v = arena[:, col:col + n]
            if len(dims) == 2:
                v = v.rearrange("p (a b) -> p a b", b=dims[1])
            elif len(dims) == 3:
                v = v.rearrange("p (a b c) -> p a b c", b=dims[1], c=dims[2])
            return v

        xflat = xn[:, :, :].rearrange("p t d -> p (t d)")
        yT = xflat.rearrange("p (n t) -> p n t", t=T)
        mem = qk[:, 0:8, :].rearrange("p a b -> p (a b)").rearrange("p (t d) -> p t d", t=TT)
        qk_hi = qk[:, 8:16, :].rearrange("p a b -> p (a b)")
        wup = qk_hi[:, 0:512]
        bgate = qk_hi[0:1, 512:1024]
        hlow = qk_hi[:, 1024:1280]
        kd = xn[:, 0, :].rearrange("p (t n) -> p t n", t=TT)
        maskbf, identbf = bfc[:, 0:P], bfc[:, P:2 * P]
        lam_in = ar(HY_PT, 4, 64)
        xk = ar(XA_K, KT, T)
        mix = qk[:, 0:8, :]
        cw_rows = qk[0:2 * FT2, 0:4, :].rearrange("p a b -> p (a b)").rearrange("p (l a f) -> p l a f", l=2, f=P)
        gE = xflat.rearrange("p (e h t) -> p e h t", e=2, t=T)
        gTmp = xflat[:, 1024:2048].rearrange("p (t n) -> p t n", t=TT)

        def bank2(b):
            return ps[b][:, :].rearrange("p (a t) -> p a t", t=T)

        def bank4(b):
            return ps[b][:, :].rearrange("p (a t) -> p a t", t=P)

        def slab_a(buf, slot):
            return buf[:, slot, :].rearrange("p (k n) -> p k n", n=CH)

        def slab_b(buf, slot):
            return buf[:, slot, :].rearrange("p (k n) -> p k n", n=T)

        def slab_dn(buf, slot):
            return buf[:, slot, :].rearrange("p (k n) -> p k n", n=D)

        def two(v, s):
            return v.rearrange("p h (n a s) -> p (h n) a s", a=2, s=s)

        raw_loaded = [sem(f"raw_loaded{i}") for i in range(RAWS)]
        wh_ready = sem("wh_ready")
        wl_ready = sem("wl_ready")
        slab_used = sem("slab_used")
        bank_free = sem("bank_free")
        bank_ready = sem("bank_ready")
        tr_done = sem("tr_done")
        xh_done = sem("xh_done")
        x_loaded = sem("x_loaded")
        con_loaded = sem("con_loaded")
        rope_loaded = sem("rope_loaded")
        small_loaded = sem("small_loaded")
        cw_loaded = sem("cw_loaded")
        cw_T = sem("cw_T")
        cw_done = sem("cw_done")
        gain_loaded = [sem(f"gain_loaded{i}") for i in range(4)]
        pool_init = sem("pool_init")
        pool_order = sem("pool_order")
        dve_order = sem("dve_order")
        act_order = sem("act_order")
        var_ready = sem("var_ready")
        rstd_ready = sem("rstd_ready")
        x_ready = sem("x_ready")
        xn_ready = sem("xn_ready")
        lam_sum = sem("lam_sum")
        lam_exp = sem("lam_exp")
        rope_done = sem("rope_done")
        blk_T = sem("blk_T")
        blk_act = sem("blk_act")
        blk_dve = sem("blk_dve")
        kz_ready = sem("kz_ready")
        maskbf_ready = sem("maskbf_ready")
        scores_ready = sem("scores_ready")
        nb_ready = sem("nb_ready")
        exp_done = sem("exp_done")
        moba_free = sem("moba_free")
        diff_w = sem("diff_w")
        pT_ready = sem("pT_ready")
        pT_copied = sem("pT_copied")
        wT_copied = sem("wT_copied")
        pv_done = sem("pv_done")
        sq_done = sem("sq_done")
        hid_sq = sem("hid_sq")
        hid_hi = sem("hid_hi")
        hid_lo = sem("hid_lo")
        conv_mid = sem("conv_mid")
        conv_tap = sem("conv_tap")
        gate_act = sem("gate_act")
        ff_outA = sem("ff_outA")
        ff_outD = sem("ff_outD")
        ff_nat = sem("ff_nat")
        gla_small = sem("gla_small")
        z_ready = sem("z_ready")
        ln_done = sem("ln_done")
        g_ready = sem("g_ready")
        b_ready = sem("b_ready")
        b_copied = sem("b_copied")
        d_ready = sem("d_ready")
        e_ready = sem("e_ready")
        zlev_ready = sem("zlev_ready")
        lv_ready = sem("lv_ready")
        lv_done = sem("lv_done")
        a01_done = sem("a01_done")
        r_act = sem("r_act")
        sr_done = sem("sr_done")
        go_ready = sem("go_ready")
        mem_loaded = sem("mem_loaded")
        mem_normed = sem("mem_normed")
        pool_loaded = sem("pool_loaded")
        pmix_ready = sem("pmix_ready")
        pmix_done = sem("pmix_done")
        py_ready = sem("py_ready")
        out_done = sem("out_done")

        block = ctx.enter_context(nc.Block())

        HY_PAIRS = []
        for t in range(TT):
            HY_PAIRS += [("diff", t, h) for h in range(4)] + [("moba", t, j) for j in range(2)]
        QK_PAIRS = [("gqa", t, j) for t in range(TT) for j in range(8)]
        XA_PAIRS = [("x", t, j) for t in range(TT) for j in range(2)]
        Q_HY, Q_QK = 0, len(HY_PAIRS)
        Q_XA = [Q_QK + len(QK_PAIRS), Q_QK + len(QK_PAIRS) + len(XA_PAIRS)]
        SCALE = {"diff": 64 ** -0.5, "moba": 128 ** -0.5, "gqa": 64 ** -0.5, "x": 256 ** -0.5}

        HY_FILLS = [(None, 0), (None, 2), ("diff", 0), ("diff", 2)] + [(None, b) for b in (8, 10, 12, 14)]
        QK_FILLS = [("gqa", 0), ("gqa", 4)] + [(None, b) for b in (0, 2, 4, 6)]

        def cols(kind, j):
            return {"diff": 2 * j, "moba": 8 + 2 * j, "gqa": 2 * j, "x": 2 * j}[kind]

        def key_pairs(kind, j):
            if kind == "gqa":
                return qk[:, 8 + 2 * (j // 2):10 + 2 * (j // 2), :]
            if j < 2:
                return qk[:, 4 + 2 * j:6 + 2 * j, :]
            return xn[:, 1, :].rearrange("p (b t) -> p b t", t=T)[:, 2 * (j - 2):2 * (j - 2) + 2, :]

        def ring(kind):
            return 2 if kind == "x" else 3

        def out_bank(kind, t, j):
            if kind == "diff":
                return 5 if t == 0 else 7
            if kind == "moba":
                return 6
            if kind == "gqa":
                return (5, 6, 7, 5)[2 * t + j // 4]
            return 4 + 2 * t + j

        def width(kind, t):
            return P * (t + 1) if kind in ("diff", "moba") else T

        def pbuf(kind):
            return {"diff": (HY_P, HY_PT), "moba": (HY_P, HY_PT), "gqa": (QK_P, QK_PT), "x": (XA_P, XA_PT)}[kind]

        GAINS = ["ln_mix_g0", "ln_mix_b0", "ln_ffn_g0", "ln_ffn_b0", "ln_mix_g1", "ln_mix_b1", "mem_norm0", "ln_ffn_g1",
                 "ln_ffn_b1", "attn_norm", "xattn_norm0", "ffn_norm0", "mem_norm1", "pool_norm", "pool_scale",
                 "xattn_norm1", "ffn_norm1", "final_norm"]
        GK = {g: k for k, g in enumerate(GAINS)}

        @block.sync
        def _(sp):
            def load(s, src, view, i=None, step=0):
                if s >= RAWS:
                    sp.wait_ge(wl_ready, at(i, step, s - RAWS + 1))
                sp.dma_start(view(raw, s % RAWS), src).then_inc(raw_loaded[s % RAWS], 16)

            def kview(w):
                return w.rearrange("(k p) n -> p k n", p=P)

            def load_a(s, w, n0, i=None, step=0):
                for half in range(2):
                    load(s + half, kview(w)[:, 4 * half:4 * half + 4, bass.ds(n0, CH)], slab_a, i, step)

            def load_b(s, w, n0, i=None, step=0):
                load(s, kview(w)[:, :, bass.ds(n0, T)], slab_b, i, step)

            def load_dn(s, w, k0, i=None, step=0):
                load(s, kview(w)[:, bass.ds(k0, 2), :], slab_dn, i, step)

            def ffn(s0, w1, w2):
                load_b(s0, w1, 0)
                with sp.Fori(0, (SQ_GROUPS - 2) // 2) as i:
                    for j in (1, 2):
                        load_b(s0 + 2 * j - 1, w1, i * (2 * T) + j * T, i, 4)
                        load_dn(s0 + 2 * j, w2, i * 4 + 2 * (j - 1), i, 4)
                g = SQ_GROUPS - 1
                load_b(s0 + 2 * g - 1, w1, g * T)
                load_dn(s0 + 2 * g, w2, 2 * (g - 1))
                load_dn(s0 + 2 * g + 1, w2, 2 * g)

            def conv(s0, w1, w2):
                def group(g, i=None):
                    load_b(s0 + 3 * g - 1, w1, at(i, 4 * T, g * T), i, 12)
                    load_b(s0 + 3 * g, w1, at(i, 4 * T, D_FF2 + g * T), i, 12)
                    load_dn(s0 + 3 * g + 1, w2, at(i, 8, 2 * (g - 1)), i, 12)
                load_b(s0, w1, 0)
                load_b(s0 + 1, w1, D_FF2)
                with sp.Fori(0, (CV_GROUPS - 1) // 4) as i:
                    for g in range(1, 5):
                        group(g, i)
                for g in range(1 + (CV_GROUPS - 1) // 4 * 4, CV_GROUPS):
                    group(g)
                load_dn(s0 + 3 * CV_GROUPS - 1, w2, 2 * (CV_GROUPS - 1))

            sp.dma_start(X[:, :, :], d["x"][0].rearrange("(t p) d -> p t d", p=P)).then_inc(x_loaded, 16)
            for c, n0 in enumerate((0, 512, 1536, 2048, 1024, 2560)):
                load_a(st["hy_in"].s0 + 2 * c, d["hy_w_in"], n0)
            for c in range(2):
                load_a(st["hy_out"].s0 + 2 * c, d["hy_w_out"], c * CH)
            ffn(st["ffn0"].s0, d["ffn_w1"][0], d["ffn_w2"][0])
            s0 = st["gla"].s0
            load_b(s0, d["gla_w_in"], GLA_COLS - T)
            for j in range(4):
                load_b(s0 + 1 + j, d["gla_w_in"], j * T)
            for c in range(4):
                load_a(s0 + 5 + 2 * c, d["gla_w_in"], D + c * CH)
            for c in range(2):
                load_a(st["gla_out"].s0 + 2 * c, d["gla_w_out"], c * CH)
            ffn(st["ffn1"].s0, d["ffn_w1"][1], d["ffn_w2"][1])
            for l in range(2):
                for j in range(4):
                    load_b(st[f"mem{l}"].s0 + j, d["xattn_w_kv"][l], j * T)
                for c in range(2):
                    load_a(st[f"mem{l}"].s0 + 4 + 2 * c, d["xattn_w_kv"][l], D + c * CH)
                if l == 0:
                    for c in range(3):
                        load_a(st["qkv"].s0 + 2 * c, d["attn_w_qkv"], QKV_COLS[c])
                    for c in range(2):
                        load_a(st["wo"].s0 + 2 * c, d["attn_w_o"], c * CH)
                for j in range(4):
                    load_b(st[f"xq{l}"].s0 + j, d["xattn_w_q"][l], j * T)
                for c in range(2):
                    load_a(st[f"xo{l}"].s0 + 2 * c, d["xattn_w_o"][l], c * CH)
                conv(st[f"conv{l}"].s0, d["ffn_w_up"][l], d["ffn_w_down"][l])
            for t in range(TT):
                sp.wait_ge(xn_ready, xn_count("final", t))
                sp.dma_start(out[0, t * P:(t + 1) * P, :], xn[:, t, :]).then_inc(out_done, 16)
            sp.wait_ge(out_done, 16 * TT)

        @block.gpsimd
        def _(pool):
            def gain(k):
                nc.gpsimd.dma_start(gains[:, k % 4, :], d[GAINS[k]].partition_broadcast(P))\
                    .then_inc(gain_loaded[k % 4], 16)

            def small(dst, src):
                nc.gpsimd.dma_start(dst, src).then_inc(small_loaded, 16)

            order = [0]

            def step(ins):
                order[0] += 1
                ins.then_inc(pool_order, 1)
                pool.wait_ge(pool_order, order[0])

            def norm(name, nh, scale, eps, ln=False, col=0):
                for t in range(TT):
                    pool.wait_ge(var_ready, norm_count(name, t))
                    dst = rstd[:, t, col:col + nh]
                    src = mv[:, t, 1:2] if ln else var[:, t, col:col + nh]
                    step(nc.gpsimd.tensor_scalar(dst, src, scale, eps, ALU.mult, ALU.add))
                    nc.gpsimd.tensor_tensor(dst, dst, mhalf[:, 0:nh], ALU.pow).then_inc(rstd_ready, 1)

            def load_mem():
                nc.gpsimd.dma_start(mem, d["mem"][0].rearrange("(t p) d -> p t d", p=P)).then_inc(mem_loaded, 16)

            nc.gpsimd.memset(mhalf[:, :], -0.5).then_inc(pool_init, 1)
            nc.gpsimd.memset(zero_bf[:, :], 0.0).then_inc(pool_init, 1)
            nc.gpsimd.memset(one_row[:, :], 1.0).then_inc(pool_init, 1)

            def key_zeros(kind, js):
                for j in js:
                    ins = nc.gpsimd.memset(key_pairs(kind, j), 0.0)
                ins.then_inc(kz_ready, 1)

            key_zeros("diff", range(4))
            pool.wait_ge(raw_loaded[1], 16)
            small(lam_in[:, :, :], d["diff_lambda"].partition_broadcast(P))
            small(subln[:, :], d["diff_subln"].partition_broadcast(P))
            small(qkg[:, 0, :], d["attn_q_gain"].partition_broadcast(P))
            small(qkg[:, 1, :], d["attn_k_gain"].partition_broadcast(P))
            small(glag[:, :], d["gla_norm"].partition_broadcast(P))
            small(arena[:, HY_SQ:HY_SQ + 8 * P], d["c_levels"])
            for l in range(2):
                for a in range(4):
                    src = d["ffn_conv_w"][l, a] if a < 3 else d["ffn_conv_b"][l]
                    nc.gpsimd.dma_start(cw_rows[:, l, a, :], src.rearrange("(j f) -> j f", f=P)).then_inc(cw_loaded, 16)
            for k in range(4):
                gain(k)
            pool.wait_ge(pool_init, 3)
            norm("hy_heads", 4, 1.0 / 128, EPS_RMS1)
            norm("ln_mix0", 1, 1.0, EPS_LN, ln=True)
            pool.wait_ge(x_ready, x_count("mix0"))
            gain(4), gain(5)
            step(nc.gpsimd.memset(wup, 0.0))
            nc.gpsimd.dma_start(qk_hi[112:128, 0:512], d["gla_w_gate_up"]).then_inc(gla_small, 16)
            nc.gpsimd.dma_start(bgate, d["gla_b_gate"].unsqueeze(0)).then_inc(gla_small, 16)
            nc.gpsimd.memset(arena[:, GL_ATT:GL_ATT + 1024], 0.0).then_inc(pool_init, 1)
            norm("ln_ffn0", 1, 1.0, EPS_LN, ln=True)
            pool.wait_ge(x_ready, x_count("ffn0"))
            gain(6), gain(7)
            pool.wait_ge(b_copied, TT)
            for lv in range(1, len(LEVELS) + 2):
                s = (LEVELS + [P])[lv - 1]
                b2, e2 = two(ar(GL_B, 4, T), s), two(gE[:, lv % 2], s)
                mid = b2[:, :, 0, s - 1:s].to_broadcast([P, 4 * T // (2 * s), s])
                if lv >= 3:
                    pool.wait_ge(zlev_ready, lv - 2)
                ins = nc.gpsimd.tensor_tensor(e2[:, :, 0, :], mid, b2[:, :, 0, :], ALU.subtract)
                if s < P:
                    ins = nc.gpsimd.tensor_tensor(e2[:, :, 1, :], b2[:, :, 1, :], mid, ALU.subtract)
                ins.then_inc(d_ready, 1)
            norm("gla_heads", 4, 1.0 / 256, EPS_RMS1)
            pool.wait_ge(xn_ready, xn_count("gla_heads"))
            key_zeros("gqa", range(0, 8, 2))
            load_mem()
            norm("ln_mix1", 1, 1.0, EPS_LN, ln=True)
            pool.wait_ge(x_ready, x_count("mix1"))
            gain(8), gain(9)
            norm("mem0", 1, 1.0 / D, EPS_RMS2)
            pool.wait_ge(mem_normed, TT)
            gain(10)
            norm("ln_ffn1", 1, 1.0, EPS_LN, ln=True)
            pool.wait_ge(x_ready, x_count("ffn1"))
            gain(11), gain(12)
            norm("attn", 1, 1.0 / D, EPS_RMS2)
            pool.wait_ge(xn_ready, xn_count("attn"))
            gain(13)
            for name, (h0, nh) in zip(("qk_k", "qk_q0", "qk_q1"), QK_HEADS):
                norm(name, nh, 1.0 / 64, EPS_RMS2, col=h0)
            norm("xattn0", 1, 1.0 / D, EPS_RMS2)
            pool.wait_ge(xn_ready, xn_count("xattn0"))
            gain(14)
            pool.wait_ge(xn_ready, xn_count("x_heads0"))
            load_mem()
            norm("ffn0", 1, 1.0 / D, EPS_RMS2)
            pool.wait_ge(xn_ready, xn_count("ffn0"))
            gain(15)
            norm("mem1", 1, 1.0 / D, EPS_RMS2)
            pool.wait_ge(mem_normed, 2 * TT)
            gain(16)
            pool.wait_ge(hid_lo, 2 * SQ_GROUPS + CV_GROUPS)
            nc.gpsimd.dma_start(ar(PO_M, TT, 4 * T), d["c_pool"].rearrange("(t p) n -> p t n", p=P)).then_inc(pool_loaded, 16)
            nc.gpsimd.dma_start(ar(PO_W, 8, T), d["pool_w"].rearrange("g (k p) n -> p (g k) n", p=P)).then_inc(pool_loaded, 16)
            norm("pool", 1, 1.0 / D, EPS_RMS2)
            pool.wait_ge(xn_ready, xn_count("pool"))
            gain(17)
            for name in ("xattn1", "ffn1", "final"):
                norm(name, 1, 1.0 / D, EPS_RMS2)

        @block.scalar
        def _(act):
            order = [0]

            def step(ins):
                order[0] += 1
                ins.then_inc(act_order, 1)
                act.wait_ge(act_order, order[0])

            def split(s, i=None, dstep=0):
                if s >= S:
                    return
                act.wait_ge(raw_loaded[s % RAWS], at(i, 16 * dstep // RAWS, 16 * (s // RAWS + 1)))
                if s >= RING:
                    act.wait_ge(slab_used, at(i, dstep, s - RING + 1))
                nc.scalar.activation(wh[:, s % RING, :], raw[:, s % RAWS, :], ACT.Copy).then_inc(wh_ready, 1)

            def prep(name, base=0):
                for t in range(TT):
                    for half in range(2):
                        act.wait_ge(tr_done, 4 * PREPS.index(name) + 2 * t + half + 1)
                        nc.scalar.activation(xh[:, 4 * half:4 * half + 4, t * P:(t + 1) * P], bank4(base + t + 2 * half), ACT.Copy)\
                            .then_inc(xh_done, 1)

            def copy_a(stage, k, dst, i=None, nstep=0, base=0):
                s = stage.s0 + k[1]
                act.wait_ge(bank_ready, at(i, nstep, stage.r0 + k[0] + 1))
                nc.scalar.activation(dst(0), ps[base + 2 * (k[0] % 2)][:, :], ACT.Copy).then_inc(bank_free, 1)
                act.wait_ge(slab_used, at(i, 2 * nstep, s + 2))
                nc.scalar.activation(dst(1), ps[base + 2 * (k[0] % 2) + 1][:, :], ACT.Copy).then_inc(bank_free, 1)

            def copy_b(stage, j, dst, scale=1.0, base=0):
                act.wait_ge(slab_used, stage.s0 + j + 1)
                nc.scalar.activation(dst, bank2(base + j % 4), ACT.Copy, scale=scale).then_inc(bank_free, 1)

            def splits(stage, a, b):
                for j in range(a, b):
                    split(stage.s0 + j + LOOKAHEAD)

            def rms_stats(src, w, v):
                for t in range(TT):
                    act.wait_ge(w, v(t))
                    nc.scalar.activation(xn[:, t, :], src[:, t, :], ACT.Square, accum_out=var[:, t, 0:1]).then_inc(var_ready, 1)

            def x_at(name):
                return lambda t: x_count(name, t)

            def blocks(base, fills):
                for f in range(0, len(fills), 2):
                    kind, n = fills[f]
                    act.wait_ge(blk_T, base + f + 1)
                    if kind:
                        for a in range(2):
                            kp = key_pairs(kind, n + a * (2 if kind == "gqa" else 1))
                            for u in range(2):
                                hs = slice(64 * u, 64 * u + 64)
                                ins = nc.scalar.activation(kp[hs, u, :], bank2(4 + f % 4)[hs, a, :], ACT.Copy)
                    else:
                        ins = nc.scalar.activation(qk[:, n:n + 2, :], bank2(4 + f % 4), ACT.Copy)
                    ins.then_inc(blk_act, 1)

            def softmax(pairs, q0):
                def copy_pT(q):
                    kind, t, j = pairs[q - q0]
                    if kind != "diff":
                        return
                    w = width(kind, t)
                    act.wait_ge(pT_ready, q + 1)
                    if q >= 2:
                        act.wait_ge(pv_done, q - 1)
                    nc.scalar.activation(ar(HY_PT, 2, CH)[:, q % 2, 0:w], ps[ring(kind) + q % 2][:, 0:w], ACT.Copy).then_inc(wT_copied, 1)

                for q, (kind, t, j) in enumerate(pairs, q0):
                    w = width(kind, t)
                    pa, pt = pbuf(kind)
                    c = cols(kind, j)
                    act.wait_ge(nb_ready, q + 1)
                    if q >= 2:
                        act.wait_ge(pT_ready, q - 1)
                    for u in range(2):
                        ins = nc.scalar.activation(ar(pa, 2, 2, T)[:, q % 2, u, 0:w], bank2((q - q0) % ring(kind))[:, u, 0:w], ACT.Exp,
                                                   bias=nb[:, t, c + u:c + u + 1],
                                                   scale=qsc[:, t, 0, c + u:c + u + 1] if kind == "gqa" else SCALE[kind],
                                                   accum_out=rs[:, t, c + u:c + u + 1])
                    ins.then_inc(exp_done, 1)
                    if q > q0:
                        copy_pT(q - 1)

            def ffn(name, base):
                stage = st[name]
                s0 = stage.s0
                r, h = ar(SQ_R, 2, CH), ar(SQ_H, 2, CH)

                def group(g, i=None):
                    up = s0 + 2 * g - 1 if g else s0
                    act.wait_ge(slab_used, at(i, 4, up + 1))
                    nc.scalar.activation(r[:, g % 2, :], ps[g % 2][:, :], ACT.Relu).then_inc(bank_free, 1)
                    act.wait_ge(hid_sq, at(i, 2, base + g + 1))
                    nc.scalar.activation(hh[:, g % 2, :, :].rearrange("p k t -> p (k t)"), h[:, g % 2, :], ACT.Copy).then_inc(hid_hi, 1)

                split(s0 + LOOKAHEAD)
                group(0)
                with act.Fori(0, (SQ_GROUPS - 2) // 2) as i:
                    for g in (1, 2):
                        split(s0 + 2 * g - 1 + LOOKAHEAD, i, 4)
                        split(s0 + 2 * g + LOOKAHEAD, i, 4)
                        group(g, i)
                g = SQ_GROUPS - 1
                splits(stage, 2 * g - 1, 2 * g + 1)
                group(g)
                splits(stage, 2 * g + 1, 2 * g + 2)
                ffn_out(s0 + 2 * SQ_GROUPS)

            def ffn_out(s_end):
                act.wait_ge(slab_used, s_end)
                for b in range(2):
                    nc.scalar.activation(yT[:, 2 * b:2 * b + 2, :], bank2(4 + b), ACT.Copy).then_inc(ff_outA, 1)

            def conv(name, l, base, cbase):
                stage = st[name]
                s0 = stage.s0
                cg, cv, sg, h = ar(CV_G, 2, 2, T), ar(CV_V, 2, 2, T), ar(CV_S, 2, CH), ar(CV_H, 2, CH)

                def mid(bank, dst, ft, i):
                    for a in range(2):
                        f = at(i, 8, ft + a)
                        ins = nc.scalar.activation(dst[:, a, :], bank2(bank)[:, a, :], ACT.Identity,
                                                   scale=cw[:, l, 1, bass.ds(f, 1)], bias=cw[:, l, 3, bass.ds(f, 1)])
                    ins.then_inc(conv_mid, 1)

                def group(g, i=None):
                    up = s0 + 3 * g - 1 if g else s0
                    if g:
                        split(up + LOOKAHEAD, i, 12)
                    act.wait_ge(slab_used, at(i, 12, up + 1))
                    mid(2 * (g % 2), cg[:, g % 2], 2 * g, i)
                    split(up + 1 + LOOKAHEAD if g else up + LOOKAHEAD, i, 12)
                    act.wait_ge(bank_free, at(i, 8, stage.f0 + 4 + 2 * g + 1))
                    nc.scalar.activation(sg[:, g % 2, :], cg[:, g % 2].rearrange("p a t -> p (a t)"), ACT.Silu).then_inc(gate_act, 1)
                    act.wait_ge(slab_used, at(i, 12, up + 2))
                    mid(2 * (g % 2) + 1, cv[:, g % 2], FT2 + 2 * g, i)
                    if g < CV_GROUPS - 1:
                        split(up + 2 + LOOKAHEAD if g else up + 1 + LOOKAHEAD, i, 12)
                    act.wait_ge(hid_sq, at(i, 4, base + g + 1))
                    nc.scalar.activation(hh[:, g % 2, :, :].rearrange("p k t -> p (k t)"), h[:, g % 2, :], ACT.Copy).then_inc(hid_hi, 1)

                group(0)
                n = (CV_GROUPS - 1) // 4
                with act.Fori(0, n) as i:
                    for g in range(1, 5):
                        group(g, i)
                for g in range(1 + 4 * n, CV_GROUPS):
                    group(g)
                splits(stage, 3 * CV_GROUPS - 2, 3 * CV_GROUPS)
                ffn_out(s0 + 3 * CV_GROUPS)

            nc.scalar.dma_start(con[:, 0:C_ROPE_D], d["c_table"][:, 0:C_ROPE_D]).then_inc(con_loaded, 16)
            split(0)
            prep("hy_in")
            split(1), split(2)
            nc.scalar.dma_start(con[:, C_ROPE_D:C_ALL], d["c_table"][:, C_ROPE_D:C_ALL]).then_inc(rope_loaded, 16)

            g = st["hy_in"]
            with act.Fori(0, 3) as i:
                for c in range(2):
                    split(g.s0 + 2 * c + LOOKAHEAD, i, 4)
                    split(g.s0 + 2 * c + 1 + LOOKAHEAD, i, 4)
                    copy_a(g, (c, 2 * c), lambda t: ar(A_NAT, TT, 3072)[:, t, bass.ds(i * 1024 + c * CH, CH)], i, 2)
            act.wait_ge(cw_T, 1)
            nc.scalar.activation(cw[:, :, :, :].rearrange("p l a j -> p (l a j)"), ps[7][:, 0:16 * FT2], ACT.Copy).then_inc(cw_done, 1)
            act.wait_ge(lam_sum, 1)
            nc.scalar.activation(lam[:, 0:2], lam[:, 2:4], ACT.Exp).then_inc(lam_exp, 1)
            blocks(0, HY_FILLS)
            softmax(HY_PAIRS, Q_HY)
            for t in range(TT):
                act.wait_ge(pv_done, Q_HY + 6 * t + 4)
                nc.scalar.activation(ar(HY_SQ, TT, CH)[:, t, :], ps[out_bank("diff", t, 0)][:, :], ACT.Square).then_inc(sq_done, 1)
            prep("hy_out")
            splits(st["hy_out"], 0, 4)
            prep("ffn0")
            ffn("ffn0", 0)

            prep("gla")
            g = st["gla"]
            splits(g, 0, 1)
            act.wait_ge(slab_used, g.s0 + 1)
            nc.scalar.activation(hlow, bank2(2)[:, 1, :], ACT.Copy).then_inc(bank_free, 1)

            def qk_copy(j):
                splits(g, 1 + j, 2 + j)
                act.wait_ge(slab_used, g.s0 + 2 + j)
                nc.scalar.activation(qk[:, 2 * j:2 * j + 2, :], bank2((3 + j) % 4 if j < 3 else 2), ACT.Copy,
                                     scale=P ** -0.5 if j < 2 else 1.0).then_inc(bank_free, 1)

            qk_copy(0)
            for t in range(TT):
                act.wait_ge(z_ready, t + 1)
                step(nc.scalar.activation(gTmp[:, t, :], ps[4 + t][:, :], ACT.Abs))
                step(nc.scalar.activation(gTmp[:, t, :], gTmp[:, t, :], ACT.Exp, scale=-1.0))
                nc.scalar.activation(gTmp[:, t, :], gTmp[:, t, :], ACT.Ln, bias=1.0).then_inc(ln_done, 1)
            for j in (1, 2):
                qk_copy(j)
            for t in range(TT):
                act.wait_ge(b_ready, t + 1)
                nc.scalar.activation(ar(GL_B, 4, T)[:, :, t * P:(t + 1) * P], bank4(6 + t), ACT.Copy).then_inc(b_copied, 1)
            qk_copy(3)

            def exps(lv):
                act.wait_ge(d_ready, lv)
                E = gE[:, lv % 2]
                if lv <= len(LEVELS):
                    nc.scalar.activation(E, E, ACT.Exp).then_inc(e_ready, 1)
                else:
                    nc.scalar.activation(E[:, :, 0:P], E[:, :, 0:P], ACT.Exp)
                    nc.scalar.activation(E[:, :, P:T], ar(GL_B, 4, T)[:, :, P:T], ACT.Exp).then_inc(e_ready, 1)

            exps(1)
            for k in range(8):
                splits(g, 5 + k, 6 + k)
                if k < 7:
                    exps(k + 2)
                if k % 2:
                    c = k // 2
                    copy_a(g, (c, 5 + 2 * c), lambda t: ar(A_NAT, TT, 2048)[:, t, c * CH:(c + 1) * CH])
            for t in range(TT):
                rv = ar(A_NAT, TT, 2048)[:, t, D:2 * D]
                act.wait_ge(bank_free, g.f0 + 4 + 5 + 8)
                nc.scalar.activation(rv, rv, ACT.Silu).then_inc(r_act, 1)
            act.wait_ge(lv_ready, 17)
            nc.scalar.activation(ar(GL_A01, 4, P), bank4(4), ACT.Copy).then_inc(a01_done, 1)
            for t in range(TT):
                act.wait_ge(go_ready, t + 1)
                for hp in range(2):
                    ins = nc.scalar.activation(xn[:, t, hp * CH:(hp + 1) * CH], ps[t + 2 * hp][:, :], ACT.Square)
                ins.then_inc(sq_done, 1)
            prep("gla_out")
            splits(st["gla_out"], 0, 4)
            prep("ffn1")
            rms_stats(mem, mem_loaded, lambda t: 16)
            ffn("ffn1", SQ_GROUPS)

            def keys(l, j):
                copy_b(st[f"mem{l}"], j, xk[:, 2 * j:2 * j + 2, :], base=4)

            def mem_values(l, c, base):
                copy_a(st[f"mem{l}"], (c, 4 + 2 * c), lambda t: ar(XA_V, TT, D)[:, t, c * CH:(c + 1) * CH], base=base)

            g = st["mem0"]
            prep("mem0", 4)
            splits(g, 0, 1)
            rms_stats(X, x_ready, x_at("ffn1"))
            for j in range(4):
                keys(0, j)
                splits(g, j + 1, j + 2)
            splits(g, 5, 6)
            mem_values(0, 0, 4)
            splits(g, 6, 8)
            mem_values(0, 1, 4)

            prep("qkv")
            g = st["qkv"]
            nat = ar(A_NAT, TT, 1536)
            for c, (h0, nh) in enumerate(QK_HEADS):
                splits(g, 2 * c, 2 * c + 2)
                copy_a(g, (c, 2 * c), lambda t: nat[:, t, QKV_COLS[c]:QKV_COLS[c] + CH])
                for t in range(TT):
                    e = 2 * c + t
                    act.wait_ge(bank_free, g.f0 + 4 + e + 1)
                    if e >= 2:
                        act.wait_ge(var_ready, norm_count("qk_k", 0) + e - 2)
                    nc.scalar.activation(ar(QK_SQ, 2, CH)[:, e % 2, 0:64 * nh], nat[:, t, 64 * h0:64 * (h0 + nh)], ACT.Square).then_inc(sq_done, 1)
            blocks(8, QK_FILLS)
            softmax(QK_PAIRS, Q_QK)
            prep("wo")
            splits(st["wo"], 0, 4)

            for l in range(2):
                if l == 0:
                    rms_stats(X, x_ready, x_at("wo"))
                prep(f"xq{l}")
                g = st[f"xq{l}"]
                for j in range(4):
                    splits(g, j, j + 1)
                    copy_b(g, j, qk[:, 2 * j:2 * j + 2, :])
                softmax(XA_PAIRS, Q_XA[l])
                prep(f"xo{l}")
                splits(st[f"xo{l}"], 0, 4)
                rms_stats(X, x_ready, x_at(f"xo{l}"))
                prep(f"conv{l}")
                if l == 0:
                    rms_stats(mem, mem_loaded, lambda t: 32)
                conv(f"conv{l}", l, 2 * SQ_GROUPS + CV_GROUPS * l, 0)
                if l == 0:
                    g = st["mem1"]
                    prep("mem1", 4)
                    splits(g, 0, 1)
                    act.wait_ge(ff_nat, 4 * 3)
                    rms_stats(X, x_ready, x_at("conv0"))
                    for j in range(4):
                        keys(1, j)
                        if j < 3:
                            splits(g, j + 1, j + 2)
                    for b in range(4):
                        act.wait_ge(pmix_ready, b + 1)
                        nc.scalar.activation(mix[:, 2 * b:2 * b + 2, :], bank2(b), ACT.Copy).then_inc(pmix_done, 1)
                    splits(g, 4, 5)
                    rms_stats(X, x_ready, x_at("pool"))
                    splits(g, 5, 6)
                    mem_values(1, 0, 0)
                    splits(g, 6, 8)
                    mem_values(1, 1, 0)
            act.wait_ge(ff_nat, 4 * 4)
            rms_stats(X, x_ready, x_at("conv1"))

        @block.vector
        def _(dve):
            order = [0]

            def step(ins):
                order[0] += 1
                ins.then_inc(dve_order, 1)

            def sync():
                dve.wait_ge(dve_order, order[0])

            def split(s, i=None, dstep=0):
                if s >= S:
                    return
                dve.wait_ge(wh_ready, at(i, dstep, s + 1))
                nc.vector.tensor_tensor(wl[:, s % RING, :], raw[:, s % RAWS, :], wh[:, s % RING, :].bitcast(F32), ALU.subtract)\
                    .then_inc(wl_ready, 1)

            def splits(stage, a, b):
                for j in range(a, b):
                    split(stage.s0 + j + LOOKAHEAD)

            def prep(name, base=0):
                for t in range(TT):
                    for half in range(2):
                        dve.wait_ge(xh_done, 4 * PREPS.index(name) + 2 * t + half + 1)
                        part = slice(4 * half, 4 * half + 4), slice(t * P, (t + 1) * P)
                        nc.vector.tensor_tensor(xl[:, part[0], part[1]], bank4(base + t + 2 * half), xh[:, part[0], part[1]].bitcast(F32),
                                                ALU.subtract).then_inc(bank_free, 1)

            def gain(name):
                k = GK[name]
                dve.wait_ge(gain_loaded[k % 4], 16 * (k // 4 + 1))
                return gains[:, k % 4, :]

            def ln_part(c, t, wait_ct):
                cs = slice(c * CH, (c + 1) * CH)
                wait_ct(c, t)
                step(nc.vector.scalar_tensor_tensor(X[:, t, cs], X[:, t, cs], ALPHA, ps[2 * c + t][:, :], ALU.mult, ALU.add))
                sync()
                step(nc.vector.bn_stats(bst[:, t, c, :], X[:, t, cs]))
                if c == 1:
                    sync()
                    nc.vector.bn_aggr(mv[:, t, :], bst[:, t, :, :].rearrange("p c s -> p (c s)")).then_inc(var_ready, 1)

            def ln_center(kind, l, t):
                gg = gain(f"ln_{kind}_g{l}")
                dve.wait_ge(var_ready, norm_count(f"ln_{kind}{l}", t))
                step(nc.vector.scalar_tensor_tensor(X[:, t, :], X[:, t, :], mv[:, t, 0:1], gg, ALU.subtract, ALU.mult))

            def ln_scale(kind, l, t):
                bb = gain(f"ln_{kind}_b{l}")
                sync()
                dve.wait_ge(rstd_ready, norm_count(f"ln_{kind}{l}", t))
                nc.vector.scalar_tensor_tensor(X[:, t, :], X[:, t, :], rstd[:, t, 0:1], bb, ALU.mult, ALU.add).then_inc(x_ready, 1)

            def ln_mix(l, stage):
                w = wait_a(stage)
                splits(stage, 0, 2)
                ln_part(0, 0, w), ln_part(0, 1, w)
                splits(stage, 2, 3)
                ln_part(1, 0, w), ln_center("mix", l, 0)
                ln_part(1, 1, w), ln_scale("mix", l, 0)
                ln_center("mix", l, 1), ln_scale("mix", l, 1)
                splits(stage, 3, 4)

            def ln_ffn(l, f):
                w = wait_nat(f)
                ln_part(0, 0, w), ln_part(1, 0, w)
                if l:
                    ln_part(0, 1, w), ln_part(1, 1, w)
                ln_center("ffn", l, 0), ln_scale("ffn", l, 0)
                if not l:
                    ln_part(0, 1, w), ln_part(1, 1, w)
                ln_center("ffn", l, 1), ln_scale("ffn", l, 1)

            CT = [(c, t) for c in range(2) for t in range(TT)]
            TC = [(c, t) for t in range(TT) for c in range(2)]

            def wait_a(stage):
                def w(c, t):
                    if t == 0:
                        dve.wait_ge(bank_ready, stage.r0 + c + 1)
                    else:
                        dve.wait_ge(slab_used, stage.s0 + 2 * c + 2)
                return w

            def wait_nat(f):
                return lambda c, t: dve.wait_ge(ff_nat, 4 * f + 2 * t + c + 1)

            def residual(order_ct, wait_ct):
                done = [0, 0]
                for c, t in order_ct:
                    cs = slice(c * CH, (c + 1) * CH)
                    wait_ct(c, t)
                    ins = nc.vector.tensor_tensor(X[:, t, cs], ps[2 * c + t][:, :], X[:, t, cs], ALU.add)
                    done[t] += 1
                    if done[t] == 2:
                        ins.then_inc(x_ready, 1)

            def rms_apply(name, gain_name, src=X, dst=xn, done=xn_ready):
                gg = gain(gain_name)
                for t in range(TT):
                    dve.wait_ge(rstd_ready, norm_count(name, t))
                    nc.vector.scalar_tensor_tensor(dst[:, t, :], src[:, t, :], rstd[:, t, 0:1], gg, ALU.mult, ALU.mult).then_inc(done, 1)

            def blocks(base, fills):
                for f in range(1, len(fills), 2):
                    kind, n = fills[f]
                    dve.wait_ge(blk_T, base + f + 1)
                    if kind:
                        for a in range(2):
                            kp = key_pairs(kind, n + a * (2 if kind == "gqa" else 1))
                            for u in range(2):
                                hs = slice(64 * u, 64 * u + 64)
                                ins = nc.vector.tensor_copy(kp[hs, u, :], bank2(4 + f % 4)[hs, a, :])
                    else:
                        ins = nc.vector.tensor_copy(qk[:, n:n + 2, :], bank2(4 + f % 4))
                    ins.then_inc(blk_dve, 1)

            def softmax(pairs, q0, after):
                def post(q):
                    kind, t, j = pairs[q - q0]
                    w = width(kind, t)
                    if kind == "diff":
                        c = cols(kind, j)
                        p = ar(pbuf(kind)[0], 2, 2, T)[:, q % 2]
                        dve.wait_ge(exp_done, q + 1)
                        step(nc.vector.reciprocal(rr[:, t, c:c + 2], rs[:, t, c:c + 2]))
                        sync()
                        step(nc.vector.tensor_scalar(p[:, 1, 0:w], p[:, 1, 0:w], rr[:, t, c + 1:c + 2], lam[:, 2:3], ALU.mult, ALU.mult))
                        sync()
                        nc.vector.scalar_tensor_tensor(p[:, 0, 0:w], p[:, 0, 0:w], rr[:, t, c:c + 1], p[:, 1, 0:w],
                                                       ALU.mult, ALU.subtract).then_inc(diff_w, 1)
                    else:
                        dve.wait_ge(pT_ready, q + 1)
                        if q >= 2:
                            dve.wait_ge(pv_done, q - 1)
                        nc.vector.tensor_copy(ar(pbuf(kind)[1], 2, CH)[:, q % 2, 0:2 * w], ps[ring(kind) + q % 2][:, 0:2 * w]).then_inc(pT_copied, 1)
                    after(q - q0)

                for q, (kind, t, j) in enumerate(pairs, q0):
                    w = width(kind, t)
                    c = cols(kind, j)
                    dve.wait_ge(scores_ready, q + 1)
                    step(nc.vector.tensor_reduce(mx[:, t, c:c + 2], bank2((q - q0) % ring(kind))[:, :, 0:w], AX, ALU.max))
                    sync()
                    if kind == "gqa":
                        ins = nc.vector.tensor_tensor(nb[:, t, c:c + 2], mx[:, t, c:c + 2], qsc[:, t, 1, c:c + 2], ALU.mult)
                    else:
                        ins = nc.vector.tensor_scalar(nb[:, t, c:c + 2], mx[:, t, c:c + 2], -SCALE[kind], None, ALU.mult)
                    ins.then_inc(nb_ready, 1)
                    if q > q0:
                        post(q - 1)
                post(q0 + len(pairs) - 1)

            def heads_out(dst, src, col, n, w, t):
                return nc.vector.tensor_tensor(dst.rearrange("p (h w) -> p h w", w=w), src.rearrange("p (h w) -> p h w", w=w),
                                               rr[:, t, col:col + n].unsqueeze(2).to_broadcast([P, n, w]), ALU.mult)

            def rope(x, tmp, g, half, cos, sin):
                xg = x.rearrange("p (g a h) -> p g a h", a=2, h=half)
                tg = tmp.rearrange("p (g a h) -> p g a h", a=2, h=half)
                for a in range(2):
                    tab = sin[:, a * half:(a + 1) * half].unsqueeze(1).to_broadcast([P, g, half])
                    step(nc.vector.tensor_tensor(tg[:, :, a, :], xg[:, :, 1 - a, :], tab, ALU.mult))
                sync()
                xw = x.rearrange("p (g w) -> p g w", w=2 * half)
                step(nc.vector.tensor_tensor(xw, xw, cos.unsqueeze(1).to_broadcast([P, g, 2 * half]), ALU.mult))
                sync()
                return nc.vector.tensor_tensor(x, x, tmp, ALU.add)

            def ffn_out(s_end):
                dve.wait_ge(slab_used, s_end)
                for b in range(2, 4):
                    nc.vector.tensor_copy(yT[:, 2 * b:2 * b + 2, :], bank2(4 + b)).then_inc(ff_outD, 1)

            def low(g, base, i, istep):
                dve.wait_ge(hid_hi, at(i, istep, base + g + 1))

            def ffn(name, base):
                stage = st[name]
                s0 = stage.s0
                r, h = ar(SQ_R, 2, CH), ar(SQ_H, 2, CH)

                def group(g, i=None):
                    dve.wait_ge(bank_free, at(i, 2, stage.f0 + 4 + g + 1))
                    nc.vector.tensor_tensor(h[:, g % 2, :], r[:, g % 2, :], r[:, g % 2, :], ALU.mult).then_inc(hid_sq, 1)
                    dve.wait_ge(hid_hi, at(i, 2, base + g + 1))
                    nc.vector.tensor_tensor(hl[:, g % 2, :, :].rearrange("p k t -> p (k t)"), h[:, g % 2, :],
                                            hh[:, g % 2, :, :].rearrange("p k t -> p (k t)").bitcast(F32), ALU.subtract).then_inc(hid_lo, 1)

                split(s0 + LOOKAHEAD)
                group(0)
                with dve.Fori(0, (SQ_GROUPS - 2) // 2) as i:
                    for g in (1, 2):
                        split(s0 + 2 * g - 1 + LOOKAHEAD, i, 4)
                        split(s0 + 2 * g + LOOKAHEAD, i, 4)
                        group(g, i)
                g = SQ_GROUPS - 1
                splits(stage, 2 * g - 1, 2 * g + 1)
                group(g)
                splits(stage, 2 * g + 1, 2 * g + 2)
                ffn_out(s0 + 2 * SQ_GROUPS)

            def conv(name, l, base, cbase):
                stage = st[name]
                s0 = stage.s0
                cg, cv, sg, h = ar(CV_G, 2, 2, T), ar(CV_V, 2, 2, T), ar(CV_S, 2, CH), ar(CV_H, 2, CH)

                def taps(bank, dst, ft, e, i):
                    dve.wait_ge(conv_mid, at(i, 8, cbase + e + 1))
                    for a in range(2):
                        ins = nc.vector.scalar_tensor_tensor(dst[:, a, 1:T], bank2(bank)[:, a, 0:T - 1], cw[:, l, 0, bass.ds(at(i, 8, ft + a), 1)],
                                                             dst[:, a, 1:T], ALU.mult, ALU.add)
                    ins.then_inc(conv_tap, 1)
                    dve.wait_ge(conv_tap, at(i, 8, cbase + e + 1))
                    for a in range(2):
                        ins = nc.vector.scalar_tensor_tensor(dst[:, a, 0:T - 1], bank2(bank)[:, a, 1:T], cw[:, l, 2, bass.ds(at(i, 8, ft + a), 1)],
                                                             dst[:, a, 0:T - 1], ALU.mult, ALU.add)
                    ins.then_inc(bank_free, 1)

                def group(g, i=None):
                    up = s0 + 3 * g - 1 if g else s0
                    if g:
                        split(up + LOOKAHEAD, i, 12)
                    taps(2 * (g % 2), cg[:, g % 2], 2 * g, 2 * g, i)
                    split(up + 1 + LOOKAHEAD if g else up + LOOKAHEAD, i, 12)
                    taps(2 * (g % 2) + 1, cv[:, g % 2], FT2 + 2 * g, 2 * g + 1, i)
                    dve.wait_ge(gate_act, at(i, 4, CV_GROUPS * l + g + 1))
                    dve.wait_ge(bank_free, at(i, 8, stage.f0 + 4 + 2 * g + 2))
                    nc.vector.tensor_tensor(h[:, g % 2, :], sg[:, g % 2, :], cv[:, g % 2].rearrange("p a t -> p (a t)"), ALU.mult).then_inc(hid_sq, 1)
                    if g < CV_GROUPS - 1:
                        split(up + 2 + LOOKAHEAD if g else up + 1 + LOOKAHEAD, i, 12)
                    dve.wait_ge(hid_hi, at(i, 4, base + g + 1))
                    nc.vector.tensor_tensor(hl[:, g % 2, :, :].rearrange("p k t -> p (k t)"), h[:, g % 2, :],
                                            hh[:, g % 2, :, :].rearrange("p k t -> p (k t)").bitcast(F32), ALU.subtract).then_inc(hid_lo, 1)

                group(0)
                n = (CV_GROUPS - 1) // 4
                with dve.Fori(0, n) as i:
                    for g in range(1, 5):
                        group(g, i)
                for g in range(1 + 4 * n, CV_GROUPS):
                    group(g)
                splits(stage, 3 * CV_GROUPS - 2, 3 * CV_GROUPS)
                ffn_out(s0 + 3 * CV_GROUPS)

            split(0)
            prep("hy_in")
            split(1), split(2)
            g = st["hy_in"]
            nat = ar(A_NAT, TT, 3072)
            splits(g, 0, 4)
            dve.wait_ge(small_loaded, 16 * 6)
            step(nc.vector.tensor_copy(lvmask[:, :], arena[:, HY_SQ:HY_SQ + 8 * P]))
            pairs4 = lam_in[:, :, :].rearrange("p (a b) w -> p a b w", b=2)
            step(nc.vector.tensor_tensor(pairs4[:, :, 0, :], pairs4[:, :, 0, :], pairs4[:, :, 1, :], ALU.mult))
            sync()
            nc.vector.tensor_reduce(lam[:, 2:4], pairs4[:, :, 0, :], AX, ALU.add).then_inc(lam_sum, 1)
            dve.wait_ge(con_loaded, 16)
            nc.vector.tensor_copy(maskbf, cmask).then_inc(maskbf_ready, 1)
            nc.vector.tensor_copy(identbf, ident).then_inc(maskbf_ready, 1)
            dve.wait_ge(rope_loaded, 16)
            for k in range(2):
                gk = qkg[:, k, :]
                step(nc.vector.tensor_tensor(ropeg[:, 2 * k, :, :], rope_x[0], gk.unsqueeze(1).to_broadcast([P, TT, 64]), ALU.mult))
                for a in range(2):
                    def half(v, b):
                        return v.rearrange("p t (x b h) -> p (t x) b h", b=2, h=16)[:, :, b, :]
                    gs = gk.rearrange("p (x b h) -> p x b h", b=2, h=16)[:, :, 1 - a, :]
                    for t in range(TT):
                        so = ropeg[:, 2 * k + 1, t, :].rearrange("p (x b h) -> p x b h", b=2, h=16)[:, :, a, :]
                        si = rope_x[1][:, t, :].rearrange("p (x b h) -> p x b h", b=2, h=16)[:, :, a, :]
                        step(nc.vector.tensor_tensor(so, si, gs, ALU.mult))
            step(nc.vector.tensor_scalar(subln[:, :], subln[:, :], 1.0 - LAMBDA_INIT, None, ALU.mult))
            splits(g, 4, 6)
            dve.wait_ge(bank_free, g.f0 + 4 + 4)
            for t in range(TT):
                rope(nat[:, t, 0:1024], xn[:, 0, :], 16, 32, rope_d[0][:, t, :], rope_d[1][:, t, :]).then_inc(rope_done, 1)
                dve.wait_ge(rope_done, t + 1)
            splits(g, 6, 10)
            dve.wait_ge(bank_free, g.f0 + 4 + 8)
            for t in range(TT):
                rope(nat[:, t, 1024:2048], xn[:, 0, :], 8, 64, rope_m[0][:, t, :], rope_m[1][:, t, :]).then_inc(rope_done, 1)
                dve.wait_ge(rope_done, 2 + t + 1)
            splits(g, 10, 12)
            dve.wait_ge(lam_exp, 1)
            step(nc.vector.tensor_tensor(lam[:, 2:3], lam[:, 0:1], lam[:, 1:2], ALU.subtract))
            sync()
            step(nc.vector.tensor_scalar(lam[:, 2:3], lam[:, 2:3], LAMBDA_INIT, None, ALU.add))
            blocks(0, HY_FILLS)

            def moba_out(t):
                dve.wait_ge(pv_done, Q_HY + 6 * t + 6)
                step(nc.vector.reciprocal(rr[:, t, 8:12], rs[:, t, 8:12]))
                sync()
                return heads_out(xn[:, t, CH:D], ps[out_bank("moba", t, 0)][:, :], 8, 4, P, t)

            softmax(HY_PAIRS, Q_HY, lambda k: moba_out(0).then_inc(moba_free, 1) if k == 6 else None)
            for t in range(TT):
                dve.wait_ge(sq_done, t + 1)
                nc.vector.tensor_reduce(var[:, t, 0:4], ar(HY_SQ, TT, CH)[:, t, :].rearrange("p (h w) -> p h w", w=P), AX, ALU.add)\
                    .then_inc(var_ready, 1)
            for t in range(TT):
                if t:
                    moba_out(t)
                dve.wait_ge(rstd_ready, t + 1)
                dst = xn[:, t, 0:CH].rearrange("p (h w) -> p h w", w=P)
                step(nc.vector.tensor_tensor(dst, bank4(out_bank("diff", t, 0)), rstd[:, t, 0:4].unsqueeze(2).to_broadcast([P, 4, P]), ALU.mult))
                sync()
                nc.vector.tensor_tensor(dst, dst, subln[:, :].unsqueeze(1).to_broadcast([P, 4, P]), ALU.mult).then_inc(xn_ready, 1)
            prep("hy_out")
            ln_mix(0, st["hy_out"])
            prep("ffn0")
            ffn("ffn0", 0)
            ln_ffn(0, 0)

            prep("gla")
            g = st["gla"]
            splits(g, 0, 2)
            gg = ar(GL_G, TT, CH)
            for t in range(TT):
                dve.wait_ge(ln_done, t + 1)
                nc.vector.scalar_tensor_tensor(gg[:, t, :], ps[4 + t][:, :], 0.0, gTmp[:, t, :], ALU.min, ALU.subtract).then_inc(g_ready, 1)
            splits(g, 2, 5)
            att = ar(GL_ATT, TT, 4, P)
            dve.wait_ge(pool_init, 4)

            def decayed(lv):
                s = (LEVELS + [P])[lv - 1]
                z2, e2 = two(ar(GL_Z, 2, 4, T)[:, lv % 2], s), two(gE[:, lv % 2], s)
                q2, k2 = two(qk[:, 0:4, :], s), two(qk[:, 4:8, :], s)
                dve.wait_ge(e_ready, lv)
                if lv >= 3:
                    dve.wait_ge(lv_ready, 2 * (lv - 2) + 2)
                nc.vector.tensor_tensor(z2[:, :, 0, :], k2[:, :, 0, :], e2[:, :, 0, :], ALU.mult)
                nc.vector.tensor_tensor(z2[:, :, 1, :], q2[:, :, 1, :], e2[:, :, 1, :], ALU.mult).then_inc(zlev_ready, 1)

            def place(lv):
                m = lvmask[:, lv * P:(lv + 1) * P].unsqueeze(1).to_broadcast([P, 4, P])
                for t in range(TT):
                    dve.wait_ge(lv_ready, 2 * lv + t + 1)
                    if lv:
                        dve.wait_ge(lv_done, 2 * (lv - 1) + t + 1)
                    nc.vector.copy_predicated(att[:, t, :, :], m, bank4(4 + 2 * (lv % 2) + t)).then_inc(lv_done, 1)

            for k in range(8):
                splits(g, 5 + k, 6 + k)
                if k:
                    place(k - 1)
                decayed(k + 1)
            place(7)
            for t in range(TT):
                rv = ar(A_NAT, TT, 2048)[:, t, D:2 * D].rearrange("p (h w) -> p h w", w=T)
                dve.wait_ge(r_act, t + 1)
                nc.vector.tensor_tensor(rv, rv, glag[:, :].unsqueeze(1).to_broadcast([P, 4, T]), ALU.mult).then_inc(sr_done, 1)
            for t in range(TT):
                dve.wait_ge(sq_done, TT + t + 1)
                nc.vector.tensor_reduce(var[:, t, 0:4], xn[:, t, :].rearrange("p (h w) -> p h w", w=T), AX, ALU.add).then_inc(var_ready, 1)
            for t in range(TT):
                dve.wait_ge(rstd_ready, norm_count("gla_heads", t))
                for hp in range(2):
                    step(nc.vector.tensor_tensor(xn[:, t, hp * CH:(hp + 1) * CH].rearrange("p (h w) -> p h w", w=T), bank2(t + 2 * hp),
                                                 rstd[:, t, 2 * hp:2 * hp + 2].unsqueeze(2).to_broadcast([P, 2, T]), ALU.mult))
                sync()
                dve.wait_ge(sr_done, t + 1)
                nc.vector.tensor_tensor(xn[:, t, :], xn[:, t, :], ar(A_NAT, TT, 2048)[:, t, D:2 * D], ALU.mult).then_inc(xn_ready, 1)
            prep("gla_out")
            ln_mix(1, st["gla_out"])
            prep("ffn1")
            rms_apply("mem0", "mem_norm0", mem, mem, mem_normed)
            ffn("ffn1", SQ_GROUPS)

            g = st["mem0"]
            prep("mem0", 4)
            splits(g, 0, 1)
            ln_ffn(1, 1)
            rms_apply("attn", "attn_norm")
            splits(g, 1, 8)

            prep("qkv")
            g = st["qkv"]
            nat = ar(A_NAT, TT, 1536)

            def head_sums(c, t):
                h0, nh = QK_HEADS[c]
                dve.wait_ge(sq_done, 2 * TT + 2 * c + t + 1)
                nc.vector.tensor_reduce(var[:, t, h0:h0 + nh], ar(QK_SQ, 2, CH)[:, t, 0:64 * nh].rearrange("p (h w) -> p h w", w=64),
                                        AX, ALU.add).then_inc(var_ready, 1)

            def axial(c, t):
                h0, nh = QK_HEADS[c]
                k = 2 if c == 0 else 0
                x = nat[:, t, 64 * h0:64 * (h0 + nh)]
                tmp = ar(QK_TMP, TT, CH)[:, t, 0:64 * nh]
                x5 = x.rearrange("p (h x b w) -> p h x b w", x=2, b=2, w=16)
                t5 = tmp.rearrange("p (h x b w) -> p h x b w", x=2, b=2, w=16)
                s5 = ropeg[:, k + 1, t, :].rearrange("p (x b w) -> p x b w", b=2, w=16)
                for b in range(2):
                    step(nc.vector.tensor_tensor(t5[:, :, :, b, :], x5[:, :, :, 1 - b, :],
                                                 s5[:, :, b, :].unsqueeze(1).to_broadcast([P, nh, 2, 16]), ALU.mult))
                sync()
                x3 = x.rearrange("p (h w) -> p h w", w=64)
                dve.wait_ge(sq_done, 2 * TT + 2 * c + t + 1)
                step(nc.vector.tensor_tensor(x3, x3, ropeg[:, k, t, :].unsqueeze(1).to_broadcast([P, nh, 64]), ALU.mult))
                sync()
                return x, tmp

            splits(g, 0, 2)
            for t in range(TT):
                head_sums(0, t)
            for t in range(TT):
                x3 = nat[:, t, D:D + 256].rearrange("p (h w) -> p h w", w=64)
                dve.wait_ge(rstd_ready, norm_count("qk_k", t))
                step(nc.vector.tensor_tensor(x3, x3, rstd[:, t, 16:20].unsqueeze(2).to_broadcast([P, 4, 64]), ALU.mult))
                sync()
                x, tmp = axial(0, t)
                kdt = kd[:, t, :].rearrange("p (g u w) -> p g u w", u=2, w=64)
                for u in range(2):
                    ins = nc.vector.tensor_tensor(kdt[:, :, u, :], x.rearrange("p (g w) -> p g w", w=64),
                                                  tmp.rearrange("p (g w) -> p g w", w=64), ALU.add)
                ins.then_inc(rope_done, 1)
            for c in (1, 2):
                splits(g, 2 * c, 2 * c + 2)
                for t in range(TT):
                    dve.wait_ge(bank_free, g.f0 + 4 + 2 * c + t + 1)
                    dve.wait_ge(rope_done, 4 + 2 * (c - 1) + t + 1)
                    x, tmp = axial(c, t)
                    nc.vector.tensor_tensor(x, x, tmp, ALU.add).then_inc(rope_done, 1)
                for t in range(TT):
                    head_sums(c, t)
            blocks(8, QK_FILLS)
            for t in range(TT):
                dve.wait_ge(rstd_ready, norm_count("qk_q1", t))
                step(nc.vector.tensor_scalar(qsc[:, t, 0, :], rstd[:, t, 0:16], SCALE["gqa"], None, ALU.mult))
                step(nc.vector.tensor_scalar(qsc[:, t, 1, :], rstd[:, t, 0:16], -SCALE["gqa"], None, ALU.mult))
            sync()

            def qk_after(k):
                if k % 8 == 7:
                    t = k // 8
                    dve.wait_ge(pv_done, Q_QK + 8 * t + 8)
                    step(nc.vector.reciprocal(rr[:, t, 0:16], rs[:, t, 0:16]))
                    sync()
                    heads_out(xn[:, t, 0:CH], ps[out_bank("gqa", t, 0)][:, :], 0, 8, 64, t)
                    heads_out(xn[:, t, CH:D], ps[out_bank("gqa", t, 4)][:, :], 8, 8, 64, t).then_inc(xn_ready, 1)

            softmax(QK_PAIRS, Q_QK, qk_after)
            prep("wo")
            splits(st["wo"], 0, 4)
            residual(CT, wait_a(st["wo"]))

            for l in range(2):
                if l == 0:
                    rms_apply("xattn0", "xattn_norm0")
                prep(f"xq{l}")
                splits(st[f"xq{l}"], 0, 4)

                def xa_after(k):
                    t, j = k // 2, k % 2
                    dve.wait_ge(pv_done, Q_XA[l] + k + 1)
                    step(nc.vector.reciprocal(rr[:, t, 2 * j:2 * j + 2], rs[:, t, 2 * j:2 * j + 2]))
                    sync()
                    ins = heads_out(xn[:, t, j * CH:(j + 1) * CH], ps[4 + 2 * t + j][:, :], 2 * j, 2, T, t)
                    if j == 1:
                        ins.then_inc(xn_ready, 1)

                softmax(XA_PAIRS, Q_XA[l], lambda k: None)
                for k in range(4):
                    xa_after(k)
                prep(f"xo{l}")
                splits(st[f"xo{l}"], 0, 4)
                residual(CT, wait_a(st[f"xo{l}"]))
                rms_apply(f"ffn{l}", f"ffn_norm{l}")
                prep(f"conv{l}")
                if l == 0:
                    rms_apply("mem1", "mem_norm1", mem, mem, mem_normed)
                    dve.wait_ge(cw_done, 1)
                conv(f"conv{l}", l, 2 * SQ_GROUPS + CV_GROUPS * l, 2 * CV_GROUPS * l)
                residual(TC, wait_nat(2 + l))
                if l == 0:
                    g = st["mem1"]
                    prep("mem1", 4)
                    splits(g, 0, 1)
                    rms_apply("pool", "pool_norm")
                    splits(g, 1, 4)
                    gs = gain("pool_scale")
                    for t in range(TT):
                        for c in range(2):
                            cs = slice(c * CH, (c + 1) * CH)
                            dve.wait_ge(py_ready, 2 * t + c + 1)
                            step(nc.vector.tensor_tensor(xn[:, t, cs], ps[4 + 2 * t + c][:, :], gs[:, cs], ALU.mult))
                            sync()
                            ins = nc.vector.tensor_tensor(X[:, t, cs], X[:, t, cs], xn[:, t, cs], ALU.add)
                        ins.then_inc(x_ready, 1)
                    splits(g, 4, 5)
                    rms_apply("xattn1", "xattn_norm1")
                    splits(g, 5, 8)
            rms_apply("final", "final_norm")

        @block.tensor
        def _(pe):
            def slab(s, i=None, step=0):
                pe.wait_ge(wl_ready, at(i, step, s + 1))

            def prep(src, w, v, base=0, warm=0):
                for t in range(TT):
                    if t:
                        stay_warm(warm, 4)
                    pe.wait_ge(w, v(t))
                    for half in range(2):
                        for k in range(4):
                            c = (4 * half + k) * P
                            ins = nc.tensor.transpose(ps[base + t + 2 * half][:, k * P:(k + 1) * P], src[:, t, c:c + P], ident)
                        ins.then_inc(tr_done, 1)

            def stay_warm(n, bank):
                for _ in range(n):
                    nc.tensor.matmul(ps[bank][:, :], zero_bf[:, 0:P], zero_bf[:, :], start=True, stop=True)

            def chunk_a(stage, c, j, i=None, cstep=0, free=None, base=0, between=None):
                for half in range(2):
                    s = stage.s0 + j + half
                    slab(s, i, 2 * cstep)
                    wa, wb = slab_a(wh, s % RING), slab_a(wl, s % RING)
                    for t in range(TT):
                        if half == 0:
                            pe.wait_ge(bank_free, at(i, 2 * cstep, (stage.f0 if free is None else free) + 2 * c + t + 1))
                        if free is None and c == 0:
                            pe.wait_ge(bank_free, stage.f0 + (4 if half else 2 * t + 1))
                        o = ps[base + 2 * (c % 2) + t][:, :]
                        ts = slice(t * P, (t + 1) * P)
                        for k in range(4):
                            kt = 4 * half + k
                            nc.tensor.matmul(o, xh[:, kt, ts], wa[:, k, :], start=(kt == 0), stop=False)
                            nc.tensor.matmul(o, xh[:, kt, ts], wb[:, k, :], start=False, stop=False)
                            ins = nc.tensor.matmul(o, xl[:, kt, ts], wa[:, k, :], start=False, stop=(kt == KT - 1))
                        if half == 1 and t == 0:
                            ins.then_inc(bank_ready, 1)
                    ins.then_inc(slab_used, 1)
                    if between:
                        between(half)

            def slab_up(s, bank, tiles=(0, 1), i=None, step=0, stage=None):
                slab(s, i, step)
                wa, wb = slab_b(wh, s % RING), slab_b(wl, s % RING)
                for a in tiles:
                    o = bank2(bank)[:, a, :]
                    cs = slice(a * P, (a + 1) * P)
                    for kt in range(KT):
                        if stage and a == tiles[0] and kt % 4 == 0:
                            pe.wait_ge(bank_free, stage.f0 + 3 + kt // 4)
                        nc.tensor.matmul(o, wa[:, kt, cs], xh[:, kt, :], start=(kt == 0), stop=False)
                        nc.tensor.matmul(o, wa[:, kt, cs], xl[:, kt, :], start=False, stop=False)
                        ins = nc.tensor.matmul(o, wb[:, kt, cs], xh[:, kt, :], start=False, stop=(kt == KT - 1))
                ins.then_inc(slab_used, 1)

            def open_down():
                for b in range(4, 8):
                    nc.tensor.matmul(ps[b][:, :], zero_bf[:, 0:P], zero_bf[:, :], start=True, stop=False, skip_group_check=True)

            def slab_down(s, par, i=None, step=0, last=False):
                slab(s, i, step)
                wa, wb = slab_dn(wh, s % RING), slab_dn(wl, s % RING)
                for k in range(2):
                    for n in range(KT):
                        o = bank2(4 + n // 2)[:, n % 2, :]
                        cs = slice(n * P, (n + 1) * P)
                        nc.tensor.matmul(o, wa[:, k, cs], hh[:, par, k, :], start=False, stop=False, skip_group_check=True)
                        nc.tensor.matmul(o, wa[:, k, cs], hl[:, par, k, :], start=False, stop=False, skip_group_check=True)
                        ins = nc.tensor.matmul(o, wb[:, k, cs], hh[:, par, k, :], start=False, stop=last and k == 1, skip_group_check=True)
                ins.then_inc(slab_used, 1)

            def ffn_nat(f):
                pe.wait_ge(ff_outA, 2 * f + 2)
                pe.wait_ge(ff_outD, 2 * f + 2)
                for t in range(TT):
                    for c in range(2):
                        for k in range(4):
                            ins = nc.tensor.transpose(ps[2 * c + t][:, k * P:(k + 1) * P], yT[:, 4 * c + k, t * P:(t + 1) * P], ident)
                        ins.then_inc(ff_nat, 1)

            def ffn(name, f, base):
                stage = st[name]
                s0 = stage.s0

                def up(g, i=None):
                    pe.wait_ge(bank_free, at(i, 2, stage.f0 + g + 3))
                    slab_up(s0 + 2 * g - 1 if g else s0, g % 2, i=i, step=4, stage=None if g else stage)

                def down(g, i=None, last=False):
                    pe.wait_ge(hid_lo, at(i, 2, base + g + 1))
                    slab_down(s0 + 2 * g + 2 if not last else s0 + 2 * g + 1, g % 2, i, 4, last)

                open_down()
                up(0)
                with pe.Fori(0, (SQ_GROUPS - 2) // 2) as i:
                    for g in (1, 2):
                        up(g, i)
                        down(g - 1, i)
                up(SQ_GROUPS - 1)
                down(SQ_GROUPS - 2)
                down(SQ_GROUPS - 1, last=True)
                ffn_nat(f)

            def conv(name, f, base):
                stage = st[name]
                s0 = stage.s0

                def up(g, i=None):
                    s = s0 + 3 * g - 1 if g else s0
                    for a in range(2):
                        pe.wait_ge(bank_free, at(i, 8, stage.f0 + 2 * g + a + 1))
                        slab_up(s + a, 2 * (g % 2) + a, i=i, step=12, stage=None if g or a else stage)

                def down(g, i=None, last=False):
                    pe.wait_ge(hid_lo, at(i, 4, base + g + 1))
                    slab_down(s0 + 3 * g + 4 if not last else s0 + 3 * g + 2, g % 2, i, 12, last)

                open_down()
                up(0)
                n = (CV_GROUPS - 1) // 4
                with pe.Fori(0, n) as i:
                    for g in range(1, 5):
                        up(g, i)
                        down(g - 1, i)
                for g in range(1 + 4 * n, CV_GROUPS):
                    up(g)
                    down(g - 1)
                down(CV_GROUPS - 1, last=True)
                ffn_nat(f)

            def blocks(base, fills, src, w, v, warm=0):
                ea = (base + 1) // 2
                for f in range(len(fills)):
                    if f == 2:
                        stay_warm(warm, 7)
                    pe.wait_ge(w, v(f))
                    if f >= 4:
                        pe.wait_ge(blk_act if f % 2 == 0 else blk_dve, ea + (f - 4) // 2 + 1)
                    for a in range(2):
                        for t in range(TT):
                            ins = nc.tensor.transpose(bank2(4 + f % 4)[:, a, t * P:(t + 1) * P], src(2 * f + a, t), ident)
                    ins.then_inc(blk_T, 1)
                pe.wait_ge(blk_act, ea + (len(fills) + 1) // 2)
                pe.wait_ge(blk_dve, ea + len(fills) // 2)

            def scores(q, bank, kind, t, j):
                w = width(kind, t)
                ts = slice(t * P, (t + 1) * P)
                both = bank2(bank)[:, :, 0:w]
                if kind in ("diff", "moba"):
                    nc.tensor.matmul(bank2(bank)[:, :, ts], identbf, maskbf.unsqueeze(1).to_broadcast([P, 2, P]), start=True, stop=False, skip_group_check=True)
                if kind == "diff":
                    ins = nc.tensor.matmul(both, qk[:, j, ts], key_pairs(kind, j)[:, :, 0:w], start=False, stop=True, skip_group_check=True)
                elif kind == "gqa":
                    ins = nc.tensor.matmul(both, qk[:, j, ts], key_pairs(kind, j), start=True, stop=True)
                else:
                    for u in range(2):
                        o = bank2(bank)[:, u, 0:w]
                        if kind == "moba":
                            ins = nc.tensor.matmul(o, qk[:, 8 + 2 * j + u, ts], qk[:, 12 + 2 * j + u, 0:w], start=False, stop=True, skip_group_check=True)
                        else:
                            for k in range(2):
                                b = 2 * (2 * j + u) + k
                                ins = nc.tensor.matmul(o, qk[:, b, ts], xk[:, b, :], start=(k == 0), stop=(k == 1))
                ins.then_inc(scores_ready, 1)

            ndiff = [0]
            copied = [0, 0]

            def probs_T(q, kind, t, j):
                w = width(kind, t)
                p = ar(pbuf(kind)[0], 2, 2, T)[:, q % 2]
                if kind == "diff":
                    ndiff[0] += 1
                    pe.wait_ge(diff_w, ndiff[0])
                else:
                    pe.wait_ge(exp_done, q + 1)
                for u in range(1 if kind == "diff" else 2):
                    for k in range(w // P):
                        c = u * w + k * P
                        ins = nc.tensor.transpose(ps[ring(kind) + q % 2][:, c:c + P], p[:, u, k * P:(k + 1) * P], ident)
                ins.then_inc(pT_ready, 1)

            def values(q, kind, t, j, v):
                w = width(kind, t)
                pT = ar(pbuf(kind)[1], 2, CH)[:, q % 2]
                copied[kind == "diff"] += 1
                pe.wait_ge(wT_copied if kind == "diff" else pT_copied, copied[kind == "diff"])
                n = w // P
                if kind == "moba" and t:
                    pe.wait_ge(moba_free, 1)
                if kind == "gqa" and t and j >= 4:
                    pe.wait_ge(xn_ready, xn_count("qk_heads", 0))
                bank = ps[out_bank(kind, t, j)]
                for u in range(1 if kind == "diff" else 2):
                    h = j if kind == "diff" else 2 * j + u
                    if kind == "diff":
                        o, vc, vw = bank[:, j * P:(j + 1) * P], 2048 + j * P, P
                    elif kind == "moba":
                        o, vc, vw = bank[:, h * P:(h + 1) * P], 2560 + h * P, P
                    elif kind == "gqa":
                        o, vc, vw = bank[:, (h % 8) * 64:(h % 8 + 1) * 64], 1280 + (h // 4) * 64, 64
                    else:
                        o, vc, vw = bank[:, u * T:(u + 1) * T], h * T, T
                    for k in range(n):
                        c = u * w + k * P
                        ins = nc.tensor.matmul(o, pT[:, c:c + P], v[:, k, vc:vc + vw], start=(k == 0), stop=(k == n - 1))
                ins.then_inc(pv_done, 1)

            def attention(pairs, q0, v):
                n = ring(pairs[0][0])
                for k in range(n - 1):
                    scores(q0 + k, k, *pairs[k])
                for k, pair in enumerate(pairs):
                    a = k + n - 1
                    if a < len(pairs):
                        scores(q0 + a, a % n, *pairs[a])
                    probs_T(q0 + k, *pair)
                    if k:
                        values(q0 + k - 1, *pairs[k - 1], v)
                values(q0 + len(pairs) - 1, *pairs[-1], v)

            def x_at(name):
                return lambda t: x_count(name, t)

            def xn_at(name):
                return lambda t: xn_count(name, t)

            pe.wait_ge(pool_init, 2)
            stay_warm(14, 4)
            pe.wait_ge(con_loaded, 16)
            prep(X, x_loaded, lambda t: 16)
            stay_warm(14, 4)
            with pe.Fori(0, 3) as i:
                for c in range(2):
                    chunk_a(st["hy_in"], c, 2 * c, i, 2)
            pe.wait_ge(cw_loaded, 16 * 8)
            for l in range(2):
                for a in range(4):
                    c = (4 * l + a) * 2 * FT2
                    ins = nc.tensor.transpose(ps[7][:, c:c + 2 * FT2], cw_rows[:, l, a, :], con[0:2 * FT2, C_IDENT:C_IDENT + 2 * FT2])
            ins.then_inc(cw_T, 1)
            stay_warm(14, 4)
            pe.wait_ge(cw_done, 1)
            nat = ar(A_NAT, TT, 3072)
            pe.wait_ge(kz_ready, 1)
            pe.wait_ge(maskbf_ready, 2)
            blocks(0, HY_FILLS, lambda b, t: nat[:, t, b * P:(b + 1) * P], rope_done, lambda f: 2 if f < 4 else 4)
            attention(HY_PAIRS, Q_HY, nat)
            stay_warm(6, 0)
            prep(xn, xn_ready, xn_at("hy_heads"))
            for c in range(2):
                chunk_a(st["hy_out"], c, 2 * c)
            stay_warm(12, 4)
            prep(X, x_ready, x_at("mix0"))
            ffn("ffn0", 0, 0)

            stay_warm(18, 4)
            prep(X, x_ready, x_at("ffn0"), warm=10)
            g = st["gla"]
            slab_up(g.s0, 2, tiles=(1,), stage=g)
            slab_up(g.s0 + 1, 3)
            pe.wait_ge(gla_small, 32)
            pe.wait_ge(pool_init, 3)
            pe.wait_ge(bank_free, g.f0 + 5)
            for t in range(TT):
                nc.tensor.matmul(ps[4 + t][:, :], one_row[:, :], bgate, start=True, stop=False)
                nc.tensor.matmul(ps[4 + t][:, :], hlow[:, t * P:(t + 1) * P], wup, start=False, stop=True).then_inc(z_ready, 1)
            slab_up(g.s0 + 2, 0)
            slab_up(g.s0 + 3, 1)
            for t in range(TT):
                pe.wait_ge(g_ready, t + 1)
                for h in range(4):
                    ins = nc.tensor.matmul(bank4(6 + t)[:, h, :], ar(GL_G, TT, CH)[:, t, h * P:(h + 1) * P], tri, start=True, stop=True)
                ins.then_inc(b_ready, 1)
            slab_up(g.s0 + 4, 2)

            def level(lv):
                z = ar(GL_Z, 2, 4, T)[:, lv % 2]
                if lv:
                    pe.wait_ge(zlev_ready, lv)
                if lv == 0:
                    pe.wait_ge(bank_free, g.f0 + 9)
                    pe.wait_ge(g_ready, TT)
                if lv == 1:
                    pe.wait_ge(b_copied, TT)
                for t in range(1 if lv == 8 else TT):
                    ts = slice(t * P, (t + 1) * P)
                    if lv >= 2:
                        pe.wait_ge(lv_done, 2 * (lv - 2) + t + 1)
                    for h in range(4):
                        o = bank4(4 + 2 * (lv % 2) + t)[:, h, :]
                        if lv == 0:
                            ins = nc.tensor.matmul(o, qk[:, 4 + h, ts], qk[:, h, ts], start=True, stop=True)
                        elif lv == 8:
                            ins = nc.tensor.matmul(o, z[:, h, 0:P], z[:, h, P:T], start=True, stop=True)
                        else:
                            ins = nc.tensor.matmul(o, z[:, h, ts], z[:, h, ts], start=True, stop=True)
                    ins.then_inc(lv_ready, 1)

            pe.wait_ge(bank_free, g.f0 + 8)
            for c in range(4):
                chunk_a(g, c, 5 + 2 * c, free=g.f0 + 5, between=lambda half: level(2 * c + half))
            level(8)
            vv = ar(A_NAT, TT, 2048)
            att = ar(GL_ATT, TT, 4, P)
            pe.wait_ge(bank_free, g.f0 + 4 + 5 + 8)
            pe.wait_ge(lv_done, 16)
            pe.wait_ge(a01_done, 1)
            for t in range(TT):
                for h in range(4):
                    o = bank2(t + 2 * (h // 2))[:, h % 2, :]
                    if t == 1:
                        nc.tensor.matmul(o, ar(GL_A01, 4, P)[:, h, :], vv[:, 0, h * T:(h + 1) * T], start=True, stop=False)
                    ins = nc.tensor.matmul(o, att[:, t, h, :], vv[:, t, h * T:(h + 1) * T], start=(t == 0), stop=True)
                ins.then_inc(go_ready, 1)
            stay_warm(18, 4)
            prep(xn, xn_ready, xn_at("gla_heads"))
            for c in range(2):
                chunk_a(st["gla_out"], c, 2 * c)
            stay_warm(12, 4)
            prep(X, x_ready, x_at("mix1"))
            ffn("ffn1", 1, SQ_GROUPS)

            def keys(l):
                prep(mem, mem_normed, lambda t: 2 * l + t + 1, base=4)
                g = st[f"mem{l}"]
                for j in range(4):
                    slab_up(g.s0 + j, 4 + j, stage=None if j else g)

            def mem_values(l, base):
                for c in range(2):
                    chunk_a(st[f"mem{l}"], c, 4 + 2 * c, free=st[f"mem{l}"].f0 + 4, base=base)

            keys(0)
            mem_values(0, 4)

            prep(xn, xn_ready, xn_at("attn"))
            pe.wait_ge(bank_free, st["mem0"].f0 + 10)
            stay_warm(16, 4)
            for c in range(3):
                chunk_a(st["qkv"], c, 2 * c)
            nat = ar(A_NAT, TT, 1536)
            pe.wait_ge(kz_ready, 2)
            blocks(8, QK_FILLS, lambda b, t: kd[:, t, b * P:(b + 1) * P] if b < 4 else nat[:, t, (b - 4) * P:(b - 3) * P],
                   rope_done, lambda f: 4 + 2 * (f // 2 + 1), warm=12)
            attention(QK_PAIRS, Q_QK, nat)
            prep(xn, xn_ready, xn_at("qk_heads"))
            for c in range(2):
                chunk_a(st["wo"], c, 2 * c)

            for l in range(2):
                g = st[f"xq{l}"]
                if l:
                    pe.wait_ge(bank_free, st["mem1"].f0 + 12)
                if l == 0:
                    stay_warm(16, 4)
                prep(xn, xn_ready, xn_at(f"xattn{l}"))
                for j in range(4):
                    slab_up(g.s0 + j, j, stage=None if j else g)
                pe.wait_ge(bank_free, g.f0 + 8)
                attention(XA_PAIRS, Q_XA[l], ar(XA_V, TT, D))
                prep(xn, xn_ready, xn_at(f"x_heads{l}"))
                for c in range(2):
                    chunk_a(st[f"xo{l}"], c, 2 * c)
                stay_warm(16, 4)
                prep(xn, xn_ready, xn_at(f"ffn{l}"))
                conv(f"conv{l}", 2 + l, 2 * SQ_GROUPS + CV_GROUPS * l)
                if l == 0:
                    keys(1)
                    M = ar(PO_M, TT, 4 * T)
                    pe.wait_ge(pool_loaded, 32)
                    for t in range(TT):
                        pe.wait_ge(xn_ready, xn_count("pool", t))
                    for ct in range(KT):
                        for t in range(TT):
                            ins = nc.tensor.matmul(bank2(ct // 2)[:, ct % 2, :], xn[:, t, ct * P:(ct + 1) * P],
                                                   M[:, t, (ct // 2) * T:(ct // 2 + 1) * T], start=(t == 0), stop=(t == 1))
                        if ct % 2:
                            ins.then_inc(pmix_ready, 1)
                    pe.wait_ge(bank_free, st["mem1"].f0 + 8)
                    pe.wait_ge(pmix_done, 4)
                    for t in range(TT):
                        for gr in range(4):
                            o = ps[4 + 2 * t + gr // 2][:, (gr % 2) * T:(gr % 2 + 1) * T]
                            for k in range(2):
                                ins = nc.tensor.matmul(o, mix[:, 2 * gr + k, t * P:(t + 1) * P], ar(PO_W, 8, T)[:, 2 * gr + k, :],
                                                       start=(k == 0), stop=(k == 1))
                            if gr % 2:
                                ins.then_inc(py_ready, 1)
                    mem_values(1, 0)


def constants():
    f = np.float32

    def rope(dim):
        inv = (f(1.0) / (f(10000.0) ** (np.arange(0, dim, 2, dtype=f) / f(dim)))).astype(f)
        ang = np.arange(T, dtype=f)[:, None] * inv[None, :]
        c, s = np.cos(ang), np.sin(ang)
        return np.concatenate([c, c], 1), np.concatenate([-s, s], 1)

    def axial():
        row = np.repeat(np.arange(T // 64, dtype=f), 64)
        col = np.tile(np.arange(64, dtype=f), T // 64)
        inv = f(10000.0) ** (-np.arange(16, dtype=f) / f(16))
        c, s = [], []
        for pos in (row, col):
            ang = pos[:, None] * inv
            c += [np.cos(ang), np.cos(ang)]
            s += [-np.sin(ang), np.sin(ang)]
        return np.concatenate(c, 1), np.concatenate(s, 1)

    def tiles(a):
        return a.reshape(TT, P, -1).transpose(1, 0, 2).reshape(P, -1)

    i = np.arange(P)
    parts = [np.eye(P), np.where(i[None, :] <= i[:, None], 0.0, NEG), np.where(i[:, None] <= i[None, :], 1.0 / 16, 0.0)]
    for c, s in (rope(64), rope(128), axial()):
        parts += [tiles(c), tiles(s)]
    table = np.concatenate([np.asarray(p, dtype=f) for p in parts], 1)
    j, q = i[:, None], i[None, :]
    levels = [j == q] + [(j // (2 * s) == q // (2 * s)) & (j % (2 * s) < s) & (q % (2 * s) >= s) for s in LEVELS]
    levels = np.concatenate(levels, 1).astype(f)
    pool = np.zeros((T, 4, T), f)
    for gr, w in enumerate((2, 4, 8, 16)):
        for t in range(T):
            lo, hi = max(t - w // 2, 0), min(t + w - w // 2, T)
            pool[lo:hi, gr, t] = f(1.0) / f(hi - lo)
            pool[t, gr, t] -= f(1.0)
    return {"c_table": np.ascontiguousarray(table), "c_levels": np.ascontiguousarray(levels), "c_pool": pool.reshape(T, 4 * T)}


def kernel(**inputs):
    import concourse.bacc as bacc
    from concourse.bass_utils import run_bass_kernel_spmd

    a = {k: np.asarray(v) for k, v in inputs.items()}
    arrays = {"x": a["x"], "hy_w_in": a["hy_w_in"][0], "diff_lambda": a["diff_lambda"][0], "diff_subln": a["diff_subln"][0],
              "hy_w_out": a["hy_w_out"][0], "gla_w_in": a["gla_w_in"][0], "gla_w_gate_up": a["gla_w_gate_up"][0],
              "gla_b_gate": a["gla_b_gate"][0], "gla_norm": a["gla_norm"][0], "gla_w_out": a["gla_w_out"][0],
              "ffn_w1": a["ffn_w1"], "ffn_w2": a["ffn_w2"], "mem": a["mem_2"], "attn_norm": a["attn_norm_2"][0],
              "attn_w_qkv": a["attn_w_qkv_2"][0], "attn_q_gain": a["attn_q_gain_2"][0], "attn_k_gain": a["attn_k_gain_2"][0],
              "attn_w_o": a["attn_w_o_2"][0], "pool_norm": a["pool_norm_2"][0], "pool_w": a["pool_w_2"][0],
              "pool_scale": a["pool_scale_2"][0], "xattn_w_q": a["xattn_w_q_2"], "xattn_w_kv": a["xattn_w_kv_2"],
              "xattn_w_o": a["xattn_w_o_2"], "ffn_w_up": a["ffn_w_up_2"], "ffn_conv_w": a["ffn_conv_w_2"],
              "ffn_conv_b": a["ffn_conv_b_2"], "ffn_w_down": a["ffn_w_down_2"], "final_norm": a["final_norm_2"]}
    for l in range(DEPTH):
        for kind in ("mix", "ffn"):
            arrays[f"ln_{kind}_g{l}"] = a[f"ln_{kind}_g"][l]
            arrays[f"ln_{kind}_b{l}"] = a[f"ln_{kind}_b"][l]
        arrays[f"mem_norm{l}"] = a["mem_norm_2"][l]
        arrays[f"xattn_norm{l}"] = a["xattn_norm_2"][l]
        arrays[f"ffn_norm{l}"] = a["ffn_norm_2"][l]
    arrays.update(constants())
    arrays = {f"in_{k}": np.ascontiguousarray(v) for k, v in arrays.items()}
    nc = bacc.Bacc("TRN2", target_bir_lowering=False, num_devices=1)
    d = {k[3:]: nc.dram_tensor(k, v.shape, mybir.dt.from_np(v.dtype), kind="ExternalInput").ap() for k, v in arrays.items()}
    d["out"] = nc.dram_tensor("out", (1, T, D), F32, kind="ExternalOutput").ap()
    build(nc, d)
    r = run_bass_kernel_spmd(nc, [arrays], core_ids=[0])
    return r.results[0]["out"]
```

```python
from contextlib import ExitStack

import numpy as np
import concourse.bass as bass
from concourse import mybir
from concourse.alu_op_type import AluOpType as ALU

ACT = mybir.ActivationFunctionType
AX = mybir.AxisListType.X
F32 = mybir.dt.float32
F32R = mybir.dt.float32r
BF16 = mybir.dt.bfloat16
U8 = mybir.dt.uint8

P = 128
D = 1024
T = 256
TT = T // P
KT = D // P
D_FF = 4096
D_FF2 = 2816
DEPTH = 2
ALPHA = (2 * DEPTH) ** 0.25
EPS_LN = 1e-5
EPS_RMS1 = 1e-5
EPS_RMS2 = 1e-6
LAMBDA_INIT = 0.2
NEG = -3.0e38

SLAB = 2048
RING = 4
RAWS = 2
LOOKAHEAD = 3
CH = 512
GLA_COLS = 3088
SQ_GROUPS = D_FF // 256
CV_GROUPS = D_FF2 // 256
FT2 = D_FF2 // P
POOL_WINDOWS = (2, 4, 8, 16)
POOL_REACH = max(POOL_WINDOWS) // 2
LEVELS = [1, 2, 4, 8, 16, 32, 64]

C_IDENT = 0
C_MASK = C_IDENT + P
C_TRI = C_MASK + P
C_ROPE_D = C_TRI + P
C_ROPE_M = C_ROPE_D + 4 * 64
C_ROPE_X = C_ROPE_M + 4 * 128
C_ALL = C_ROPE_X + 4 * 64

A_NAT = 0
HY_P, HY_PT, HY_SQ = 6144, 7168, 8192
SQ_R, SQ_H, SQ_JUNK = 0, 1024, 2048
CV_G, CV_V, CV_S, CV_H = 0, 1024, 2048, 3072
GL_G, GL_B, GL_Z, GL_ATT, GL_A01 = 4096, 5120, 6144, 8192, 9216
QK_SQ, QK_TMP, QK_P, QK_PT = 3072, 4096, 3072, 4096
XA_P, XA_PT, XA_K, XA_V = 0, 1024, 5632, 7680
PO_M, PO_W = 0, 2048
A_ALL = 9728


class Stage:
    slabs = frees = readies = 0

    def __init__(self, n, evacs, readies=0):
        self.s0, self.f0, self.r0 = Stage.slabs, Stage.frees, Stage.readies
        Stage.slabs += n
        Stage.frees += 4 + evacs
        Stage.readies += readies


def plan():
    Stage.slabs = Stage.frees = Stage.readies = 0
    st = {}
    st["hy_in"] = Stage(12, 12, 6)
    st["hy_out"] = Stage(4, 0, 2)
    st["ffn0"] = Stage(2 * SQ_GROUPS, SQ_GROUPS)
    st["gla"] = Stage(13, 5 + 8, 4)
    st["gla_out"] = Stage(4, 0, 2)
    st["ffn1"] = Stage(2 * SQ_GROUPS, SQ_GROUPS)
    for i in range(2):
        st[f"mem{i}"] = Stage(8, 4 + 4, 2)
        if i == 0:
            st["qkv"] = Stage(6, 6, 3)
            st["wo"] = Stage(4, 0, 2)
        st[f"xq{i}"] = Stage(4, 4)
        st[f"xo{i}"] = Stage(4, 0, 2)
        st[f"conv{i}"] = Stage(3 * CV_GROUPS, 2 * CV_GROUPS)
    for name, stage in st.items():
        stage.prep = PREPS.index(name)
    return st, Stage.slabs


NORMS = ["hy_heads", "ln_mix0", "ln_ffn0", "gla_heads", "ln_mix1", "mem0", "ln_ffn1", "attn", "qk_k", "qk_q0", "qk_q1",
         "xattn0", "ffn0", "mem1", "pool", "xattn1", "ffn1", "final"]
PREPS = ["hy_in", "hy_out", "ffn0", "gla", "gla_out", "ffn1", "mem0", "qkv", "wo", "xq0", "xo0", "conv0", "mem1", "xq1", "xo1", "conv1"]
XNS = ["hy_heads", "gla_heads", "attn", "qk_heads", "xattn0", "x_heads0", "ffn0", "pool", "xattn1", "x_heads1", "ffn1", "final"]
XS = ["mix0", "ffn0", "mix1", "ffn1", "wo", "xo0", "conv0", "pool", "xo1", "conv1"]
QKV_COLS = [D, 0, CH]
QK_HEADS = [(16, 4), (0, 8), (8, 8)]


def xn_count(name, t=TT - 1):
    return 2 * XNS.index(name) + t + 1


def x_count(name, t=TT - 1):
    return 2 * XS.index(name) + t + 1


def norm_count(name, t=TT - 1):
    return 2 * NORMS.index(name) + t + 1


def at(i, step, k):
    return k if i is None else i * step + k


def build(nc, d):
    st, S = plan()
    out = d["out"]
    with ExitStack() as ctx:
        def sb(name, shape, dt=F32):
            return ctx.enter_context(nc.sbuf_tensor(name, shape, dt))

        def sem(name):
            return ctx.enter_context(nc.semaphore(name))

        raw = sb("raw", [P, RAWS, SLAB])
        wh = sb("wh", [P, RING, SLAB], F32R)
        wl = sb("wl", [P, RING, SLAB], F32R)
        xh = sb("xh", [P, KT, T], F32R)
        xl = sb("xl", [P, KT, T], F32R)
        hh = sb("hh", [P, 2, 2, T], F32R)
        hl = sb("hl", [P, 2, 2, T], F32R)
        X = sb("X", [P, TT, D])
        xn = sb("xn", [P, TT, D])
        arena = sb("arena", [P, A_ALL])
        qk = sb("qk", [P, 16, T])
        gains = sb("gains", [P, 4, D])
        con = sb("con", [P, C_ALL])
        lvmask = sb("lvmask", [P, 8 * P], U8)
        zero_bf = sb("zero_bf", [P, CH], BF16)
        bfc = sb("bfc", [P, 2 * P], BF16)
        lam = sb("lam", [P, 4])
        subln = sb("subln", [P, P])
        qkg = sb("qkg", [P, 2, 64])
        ropeg = sb("ropeg", [P, 4, TT, 64])
        glag = sb("glag", [P, T])
        cw = sb("cw", [P, 2, 4, 2 * FT2])
        var = sb("var", [P, TT, 20])
        rstd = sb("rstd", [P, TT, 20])
        mhalf = sb("mhalf", [P, 20])
        bst = sb("bst", [P, TT, 2, 6])
        mv = sb("mv", [P, TT, 2])
        lnsum = sb("lnsum", [P, TT, 2])
        nmean = sb("nmean", [P, TT])
        mx = sb("mx", [P, TT, 24])
        nb = sb("nb", [P, TT, 24])
        rs = sb("rs", [P, TT, 24])
        rr = sb("rr", [P, TT, 24])
        qsc = sb("qsc", [P, TT, 2, 16])
        one_row = sb("one_row", [1, P])
        ps = [ctx.enter_context(nc.psum_tensor(f"ps{i}", [P, CH], F32)) for i in range(8)]

        ident = con[:, C_IDENT:C_IDENT + P]
        cmask = con[:, C_MASK:C_MASK + P]
        tri = con[:, C_TRI:C_TRI + P]

        def table(col, w):
            return con[:, col:col + TT * w].rearrange("p (t w) -> p t w", t=TT)

        rope_d = table(C_ROPE_D, 64), table(C_ROPE_D + 128, 64)
        rope_m = table(C_ROPE_M, 128), table(C_ROPE_M + 256, 128)
        rope_x = table(C_ROPE_X, 64), table(C_ROPE_X + 128, 64)

        def ar(col, *dims):
            n = int(np.prod(dims))
            v = arena[:, col:col + n]
            if len(dims) == 2:
                v = v.rearrange("p (a b) -> p a b", b=dims[1])
            elif len(dims) == 3:
                v = v.rearrange("p (a b c) -> p a b c", b=dims[1], c=dims[2])
            return v

        xflat = xn[:, :, :].rearrange("p t d -> p (t d)")
        mem = qk[:, 0:8, :].rearrange("p a b -> p (a b)").rearrange("p (t d) -> p t d", t=TT)
        qk_hi = qk[:, 8:16, :].rearrange("p a b -> p (a b)")
        wup = qk_hi[:, 0:512]
        bgate = qk_hi[0:1, 512:1024]
        hlow = qk_hi[:, 1024:1280]
        kd = xn[:, 0, :].rearrange("p (t n) -> p t n", t=TT)
        maskbf, identbf = bfc[:, 0:P], bfc[:, P:2 * P]
        lam_in = ar(HY_PT, 4, 64)
        xk = ar(XA_K, KT, T)
        mix = qk[:, 0:8, :]
        cw_rows = qk[0:2 * FT2, 0:4, :].rearrange("p a b -> p (a b)").rearrange("p (l a f) -> p l a f", l=2, f=P)
        gE = xflat.rearrange("p (e h t) -> p e h t", e=2, t=T)
        gTmp = xflat[:, 1024:2048].rearrange("p (t n) -> p t n", t=TT)

        def bank2(b):
            return ps[b][:, :].rearrange("p (a t) -> p a t", t=T)

        def bank4(b):
            return ps[b][:, :].rearrange("p (a t) -> p a t", t=P)

        def slab_a(buf, slot):
            return buf[:, slot, :].rearrange("p (k n) -> p k n", n=CH)

        def slab_b(buf, slot):
            return buf[:, slot, :].rearrange("p (k n) -> p k n", n=T)

        def slab_dn(buf, slot):
            return buf[:, slot, :].rearrange("p (k n) -> p k n", n=D)

        def two(v, s):
            return v.rearrange("p h (n a s) -> p (h n) a s", a=2, s=s)

        raw_loaded = [sem(f"raw_loaded{i}") for i in range(RAWS)]
        wh_ready = sem("wh_ready")
        wl_ready = sem("wl_ready")
        slab_used = sem("slab_used")
        bank_free = sem("bank_free")
        bank_ready = sem("bank_ready")
        tr_done = sem("tr_done")
        xh_done = sem("xh_done")
        x_loaded = sem("x_loaded")
        con_loaded = sem("con_loaded")
        rope_loaded = sem("rope_loaded")
        small_loaded = sem("small_loaded")
        cw_loaded = sem("cw_loaded")
        cw_T = sem("cw_T")
        cw_done = sem("cw_done")
        gain_loaded = [sem(f"gain_loaded{i}") for i in range(4)]
        pool_init = sem("pool_init")
        pool_order = sem("pool_order")
        dve_order = sem("dve_order")
        act_order = sem("act_order")
        var_ready = sem("var_ready")
        mean_ready = sem("mean_ready")
        rstd_ready = sem("rstd_ready")
        x_ready = sem("x_ready")
        xn_ready = sem("xn_ready")
        lam_sum = sem("lam_sum")
        lam_exp = sem("lam_exp")
        rope_done = sem("rope_done")
        blk_T = sem("blk_T")
        blk_act = sem("blk_act")
        blk_dve = sem("blk_dve")
        kz_ready = sem("kz_ready")
        maskbf_ready = sem("maskbf_ready")
        scores_ready = sem("scores_ready")
        nb_ready = sem("nb_ready")
        exp_done = sem("exp_done")
        moba_free = sem("moba_free")
        diff_w = sem("diff_w")
        pT_ready = sem("pT_ready")
        pT_copied = sem("pT_copied")
        wT_copied = sem("wT_copied")
        pv_done = sem("pv_done")
        sq_done = sem("sq_done")
        hid_sq = sem("hid_sq")
        hid_hi = sem("hid_hi")
        hid_lo = sem("hid_lo")
        conv_mid = sem("conv_mid")
        conv_tap = sem("conv_tap")
        gate_act = sem("gate_act")
        ff_first = sem("ff_first")
        gla_small = sem("gla_small")
        z_ready = sem("z_ready")
        ln_done = sem("ln_done")
        g_ready = sem("g_ready")
        b_ready = sem("b_ready")
        b_copied = sem("b_copied")
        d_ready = sem("d_ready")
        e_ready = sem("e_ready")
        zlev_ready = sem("zlev_ready")
        lv_ready = sem("lv_ready")
        lv_done = sem("lv_done")
        a01_done = sem("a01_done")
        r_act = sem("r_act")
        sr_done = sem("sr_done")
        go_ready = sem("go_ready")
        mem_loaded = sem("mem_loaded")
        mem_normed = sem("mem_normed")
        pool_loaded = sem("pool_loaded")
        pmix_ready = sem("pmix_ready")
        pmix_done = sem("pmix_done")
        py_ready = sem("py_ready")
        out_done = sem("out_done")

        block = ctx.enter_context(nc.Block())

        HY_PAIRS = []
        for t in range(TT):
            HY_PAIRS += [("diff", t, h) for h in range(4)] + [("moba", t, j) for j in range(2)]
        QK_PAIRS = [("gqa", t, j) for t in range(TT) for j in range(8)]
        XA_PAIRS = [("x", t, j) for t in range(TT) for j in range(2)]
        Q_HY, Q_QK = 0, len(HY_PAIRS)
        Q_XA = [Q_QK + len(QK_PAIRS), Q_QK + len(QK_PAIRS) + len(XA_PAIRS)]
        SCALE = {"diff": 64 ** -0.5, "moba": 128 ** -0.5, "gqa": 64 ** -0.5, "x": 256 ** -0.5}

        HY_FILLS = [(None, 0), (None, 2), ("diff", 0), ("diff", 2)] + [(None, b) for b in (8, 10, 12, 14)]
        QK_FILLS = [("gqa", 0), ("gqa", 4)] + [(None, b) for b in (0, 2, 4, 6)]

        def cols(kind, j):
            return {"diff": 2 * j, "moba": 8 + 2 * j, "gqa": 2 * j, "x": 2 * j}[kind]

        def key_pairs(kind, j):
            if kind == "gqa":
                return qk[:, 8 + 2 * (j // 2):10 + 2 * (j // 2), :]
            if j < 2:
                return qk[:, 4 + 2 * j:6 + 2 * j, :]
            return xn[:, 1, :].rearrange("p (b t) -> p b t", t=T)[:, 2 * (j - 2):2 * (j - 2) + 2, :]

        def ring(kind):
            return 2 if kind == "x" else 3

        def out_bank(kind, t, j):
            if kind == "diff":
                return 5 if t == 0 else 7
            if kind == "moba":
                return 6
            if kind == "gqa":
                return (5, 6, 7, 5)[2 * t + j // 4]
            return 4 + 2 * t + j

        def width(kind, t):
            return P * (t + 1) if kind in ("diff", "moba") else T

        def pbuf(kind):
            return {"diff": (HY_P, HY_PT), "moba": (HY_P, HY_PT), "gqa": (QK_P, QK_PT), "x": (XA_P, XA_PT)}[kind]

        GAINS = ["ln_mix_g0", "ln_mix_b0", "ln_ffn_g0", "ln_ffn_b0", "ln_mix_g1", "ln_mix_b1", "mem_norm0", "ln_ffn_g1",
                 "ln_ffn_b1", "attn_norm", "xattn_norm0", "ffn_norm0", "mem_norm1", "pool_norm", "pool_scale",
                 "xattn_norm1", "ffn_norm1", "final_norm"]
        GK = {g: k for k, g in enumerate(GAINS)}

        @block.sync
        def _(sp):
            def load(s, src, view, i=None, step=0):
                if s >= RAWS:
                    sp.wait_ge(wl_ready, at(i, step, s - RAWS + 1))
                sp.dma_start(view(raw, s % RAWS), src).then_inc(raw_loaded[s % RAWS], 16)

            def kview(w):
                return w.rearrange("(k p) n -> p k n", p=P)

            def load_a(s, w, n0, i=None, step=0):
                for half in range(2):
                    load(s + half, kview(w)[:, 4 * half:4 * half + 4, bass.ds(n0, CH)], slab_a, i, step)

            def load_b(s, w, n0, i=None, step=0):
                load(s, kview(w)[:, :, bass.ds(n0, T)], slab_b, i, step)

            def load_dn(s, w, k0, i=None, step=0):
                load(s, kview(w)[:, bass.ds(k0, 2), :], slab_dn, i, step)

            def ffn(s0, w1, w2):
                load_b(s0, w1, 0)
                with sp.Fori(0, (SQ_GROUPS - 2) // 2) as i:
                    for j in (1, 2):
                        load_b(s0 + 2 * j - 1, w1, i * (2 * T) + j * T, i, 4)
                        load_dn(s0 + 2 * j, w2, i * 4 + 2 * (j - 1), i, 4)
                g = SQ_GROUPS - 1
                load_b(s0 + 2 * g - 1, w1, g * T)
                load_dn(s0 + 2 * g, w2, 2 * (g - 1))
                load_dn(s0 + 2 * g + 1, w2, 2 * g)

            def conv(s0, w1, w2):
                def group(g, i=None):
                    load_b(s0 + 3 * g - 1, w1, at(i, 4 * T, g * T), i, 12)
                    load_b(s0 + 3 * g, w1, at(i, 4 * T, D_FF2 + g * T), i, 12)
                    load_dn(s0 + 3 * g + 1, w2, at(i, 8, 2 * (g - 1)), i, 12)
                load_b(s0, w1, 0)
                load_b(s0 + 1, w1, D_FF2)
                with sp.Fori(0, (CV_GROUPS - 1) // 4) as i:
                    for g in range(1, 5):
                        group(g, i)
                for g in range(1 + (CV_GROUPS - 1) // 4 * 4, CV_GROUPS):
                    group(g)
                load_dn(s0 + 3 * CV_GROUPS - 1, w2, 2 * (CV_GROUPS - 1))

            sp.dma_start(X[:, :, :], d["x"][0].rearrange("(t p) d -> p t d", p=P)).then_inc(x_loaded, 16)
            for c, n0 in enumerate((0, 512, 1536, 2048, 1024, 2560)):
                load_a(st["hy_in"].s0 + 2 * c, d["hy_w_in"], n0)
            for c in range(2):
                load_a(st["hy_out"].s0 + 2 * c, d["hy_w_out"], c * CH)
            ffn(st["ffn0"].s0, d["ffn_w1"][0], d["ffn_w2"][0])
            s0 = st["gla"].s0
            load_b(s0, d["gla_w_in"], GLA_COLS - T)
            for j in range(4):
                load_b(s0 + 1 + j, d["gla_w_in"], j * T)
            for c in range(4):
                load_a(s0 + 5 + 2 * c, d["gla_w_in"], D + c * CH)
            for c in range(2):
                load_a(st["gla_out"].s0 + 2 * c, d["gla_w_out"], c * CH)
            ffn(st["ffn1"].s0, d["ffn_w1"][1], d["ffn_w2"][1])
            for l in range(2):
                for j in range(4):
                    load_b(st[f"mem{l}"].s0 + j, d["xattn_w_kv"][l], j * T)
                for c in range(2):
                    load_a(st[f"mem{l}"].s0 + 4 + 2 * c, d["xattn_w_kv"][l], D + c * CH)
                if l == 0:
                    for c in range(3):
                        load_a(st["qkv"].s0 + 2 * c, d["attn_w_qkv"], QKV_COLS[c])
                    for c in range(2):
                        load_a(st["wo"].s0 + 2 * c, d["attn_w_o"], c * CH)
                for j in range(4):
                    load_b(st[f"xq{l}"].s0 + j, d["xattn_w_q"][l], j * T)
                for c in range(2):
                    load_a(st[f"xo{l}"].s0 + 2 * c, d["xattn_w_o"][l], c * CH)
                conv(st[f"conv{l}"].s0, d["ffn_w_up"][l], d["ffn_w_down"][l])
            for t in range(TT):
                sp.wait_ge(xn_ready, xn_count("final", t))
                sp.dma_start(out[0, t * P:(t + 1) * P, :], xn[:, t, :]).then_inc(out_done, 16)
            sp.wait_ge(out_done, 16 * TT)

        @block.gpsimd
        def _(pool):
            def gain(k):
                nc.gpsimd.dma_start(gains[:, k % 4, :], d[GAINS[k]].partition_broadcast(P))\
                    .then_inc(gain_loaded[k % 4], 16)

            def small(dst, src):
                nc.gpsimd.dma_start(dst, src).then_inc(small_loaded, 16)

            order = [0]

            def step(ins):
                order[0] += 1
                ins.then_inc(pool_order, 1)
                pool.wait_ge(pool_order, order[0])

            def norm(name, nh, scale, eps, ln=False, col=0):
                for t in range(TT):
                    pool.wait_ge(var_ready, norm_count(name, t))
                    dst = rstd[:, t, col:col + nh]
                    src = mv[:, t, 1:2] if ln else var[:, t, col:col + nh]
                    step(nc.gpsimd.tensor_scalar(dst, src, scale, eps, ALU.mult, ALU.add))
                    nc.gpsimd.tensor_tensor(dst, dst, mhalf[:, 0:nh], ALU.pow).then_inc(rstd_ready, 1)

            def split(s):
                pool.wait_ge(wh_ready, s + 1)
                pool.wait_ge(wl_ready, s)
                nc.gpsimd.tensor_tensor(wl[:, s % RING, :], raw[:, s % RAWS, :], wh[:, s % RING, :].bitcast(F32), ALU.subtract)\
                    .then_inc(wl_ready, 1)

            def load_mem():
                nc.gpsimd.dma_start(mem, d["mem"][0].rearrange("(t p) d -> p t d", p=P)).then_inc(mem_loaded, 16)

            nc.gpsimd.memset(mhalf[:, :], -0.5).then_inc(pool_init, 1)
            nc.gpsimd.memset(zero_bf[:, :], 0.0).then_inc(pool_init, 1)
            nc.gpsimd.memset(one_row[:, :], 1.0).then_inc(pool_init, 1)

            def key_zeros(kind, js):
                for j in js:
                    ins = nc.gpsimd.memset(key_pairs(kind, j), 0.0)
                ins.then_inc(kz_ready, 1)

            key_zeros("diff", range(4))
            pool.wait_ge(raw_loaded[1], 16)
            small(lam_in[:, :, :], d["diff_lambda"].partition_broadcast(P))
            small(subln[:, :], d["diff_subln"].partition_broadcast(P))
            small(qkg[:, 0, :], d["attn_q_gain"].partition_broadcast(P))
            small(qkg[:, 1, :], d["attn_k_gain"].partition_broadcast(P))
            small(glag[:, :], d["gla_norm"].partition_broadcast(P))
            small(arena[:, HY_SQ:HY_SQ + 8 * P], d["c_levels"])
            for l in range(2):
                for a in range(4):
                    src = d["ffn_conv_w"][l, a] if a < 3 else d["ffn_conv_b"][l]
                    nc.gpsimd.dma_start(cw_rows[:, l, a, :], src.rearrange("(j f) -> j f", f=P)).then_inc(cw_loaded, 16)
            pool.wait_ge(rope_done, 4)
            for k in range(4):
                gain(k)
            for j in range(1, LOOKAHEAD):
                split(st["hy_out"].s0 + j)
            pool.wait_ge(pool_init, 3)
            norm("hy_heads", 4, 1.0 / 128, EPS_RMS1)
            norm("ln_mix0", 1, 1.0, EPS_LN, ln=True)
            pool.wait_ge(x_ready, x_count("mix0"))
            gain(4), gain(5)
            step(nc.gpsimd.memset(wup, 0.0))
            nc.gpsimd.dma_start(qk_hi[112:128, 0:512], d["gla_w_gate_up"]).then_inc(gla_small, 16)
            nc.gpsimd.dma_start(bgate, d["gla_b_gate"].unsqueeze(0)).then_inc(gla_small, 16)
            nc.gpsimd.memset(arena[:, GL_ATT:GL_ATT + 1024], 0.0).then_inc(pool_init, 1)
            norm("ln_ffn0", 1, 1.0 / D, EPS_LN)
            pool.wait_ge(x_ready, x_count("ffn0"))
            gain(6), gain(7)
            pool.wait_ge(b_copied, TT)
            for lv in range(1, len(LEVELS) + 2):
                s = (LEVELS + [P])[lv - 1]
                b2, e2 = two(ar(GL_B, 4, T), s), two(gE[:, lv % 2], s)
                mid = b2[:, :, 0, s - 1:s].to_broadcast([P, 4 * T // (2 * s), s])
                if lv >= 3:
                    pool.wait_ge(zlev_ready, lv - 2)
                ins = nc.gpsimd.tensor_tensor(e2[:, :, 0, :], mid, b2[:, :, 0, :], ALU.subtract)
                if s < P:
                    ins = nc.gpsimd.tensor_tensor(e2[:, :, 1, :], b2[:, :, 1, :], mid, ALU.subtract)
                ins.then_inc(d_ready, 1)
            norm("gla_heads", 4, 1.0 / 256, EPS_RMS1)
            pool.wait_ge(xn_ready, xn_count("gla_heads"))
            key_zeros("gqa", range(0, 8, 2))
            load_mem()
            norm("ln_mix1", 1, 1.0, EPS_LN, ln=True)
            pool.wait_ge(x_ready, x_count("mix1"))
            gain(8), gain(9)
            norm("mem0", 1, 1.0 / D, EPS_RMS2)
            pool.wait_ge(mem_normed, TT)
            gain(10)
            norm("ln_ffn1", 1, 1.0 / D, EPS_LN)
            pool.wait_ge(x_ready, x_count("ffn1"))
            gain(11), gain(12)
            norm("attn", 1, 1.0 / D, EPS_RMS2)
            pool.wait_ge(xn_ready, xn_count("attn"))
            gain(13)
            for name, (h0, nh) in zip(("qk_k", "qk_q0", "qk_q1"), QK_HEADS):
                norm(name, nh, 1.0 / 64, EPS_RMS2, col=h0)
            for j in range(1, LOOKAHEAD):
                split(st["wo"].s0 + j)
            norm("xattn0", 1, 1.0 / D, EPS_RMS2)
            pool.wait_ge(xn_ready, xn_count("xattn0"))
            gain(14)
            pool.wait_ge(xn_ready, xn_count("x_heads0"))
            load_mem()
            norm("ffn0", 1, 1.0 / D, EPS_RMS2)
            pool.wait_ge(xn_ready, xn_count("ffn0"))
            gain(15)
            norm("mem1", 1, 1.0 / D, EPS_RMS2)
            pool.wait_ge(mem_normed, 2 * TT)
            gain(16)
            pool.wait_ge(hid_lo, 2 * SQ_GROUPS + CV_GROUPS)
            nc.gpsimd.dma_start(ar(PO_M, TT, 4 * T), d["c_pool"].rearrange("(t p) n -> p t n", p=P)).then_inc(pool_loaded, 16)
            nc.gpsimd.dma_start(ar(PO_W, 8, T), d["pool_w"].rearrange("g (k p) n -> p (g k) n", p=P)).then_inc(pool_loaded, 16)
            norm("pool", 1, 1.0 / D, EPS_RMS2)
            pool.wait_ge(xn_ready, xn_count("pool"))
            gain(17)
            for name in ("xattn1", "ffn1", "final"):
                norm(name, 1, 1.0 / D, EPS_RMS2)

        @block.scalar
        def _(act):
            order = [0]

            def step(ins):
                order[0] += 1
                ins.then_inc(act_order, 1)
                act.wait_ge(act_order, order[0])

            def split(s, i=None, dstep=0):
                if s >= S:
                    return
                act.wait_ge(raw_loaded[s % RAWS], at(i, 16 * dstep // RAWS, 16 * (s // RAWS + 1)))
                if s >= RING:
                    act.wait_ge(slab_used, at(i, dstep, s - RING + 1))
                nc.scalar.activation(wh[:, s % RING, :], raw[:, s % RAWS, :], ACT.Copy).then_inc(wh_ready, 1)

            def prep(name, base=0, ts=range(TT)):
                for t in ts:
                    for half in range(2):
                        act.wait_ge(tr_done, 4 * PREPS.index(name) + 2 * t + half + 1)
                        nc.scalar.activation(xh[:, 4 * half:4 * half + 4, t * P:(t + 1) * P], bank4(base + t + 2 * half), ACT.Copy)\
                            .then_inc(xh_done, 1)

            def copy_a(stage, k, dst, i=None, nstep=0, base=0):
                s = stage.s0 + k[1]
                act.wait_ge(bank_ready, at(i, nstep, stage.r0 + k[0] + 1))
                nc.scalar.activation(dst(0), ps[base + 2 * (k[0] % 2)][:, :], ACT.Copy).then_inc(bank_free, 1)
                act.wait_ge(slab_used, at(i, 2 * nstep, s + 2))
                nc.scalar.activation(dst(1), ps[base + 2 * (k[0] % 2) + 1][:, :], ACT.Copy).then_inc(bank_free, 1)

            def copy_b(stage, j, dst, scale=1.0, base=0):
                act.wait_ge(slab_used, stage.s0 + j + 1)
                nc.scalar.activation(dst, bank2(base + j % 4), ACT.Copy, scale=scale).then_inc(bank_free, 1)

            def splits(stage, a, b):
                for j in range(a, b):
                    split(stage.s0 + j + LOOKAHEAD)

            def rms_stats(src, w, v, ts=range(TT)):
                for t in ts:
                    act.wait_ge(w, v(t))
                    nc.scalar.activation(xn[:, t, :], src[:, t, :], ACT.Square, accum_out=var[:, t, 0:1]).then_inc(var_ready, 1)

            def ln_squares(l):
                for t in range(TT):
                    act.wait_ge(mean_ready, TT * l + t + 1)
                    nc.scalar.activation(ar(SQ_JUNK, TT, D)[:, t, :], X[:, t, :], ACT.Square, bias=nmean[:, t:t + 1], accum_out=var[:, t, 0:1])\
                        .then_inc(var_ready, 1)

            def x_at(name):
                return lambda t: x_count(name, t)

            def blocks(base, fills, bank=4, fs=None):
                for f in fs or range(0, len(fills), 2):
                    kind, n = fills[f]
                    act.wait_ge(blk_T, base + f + 1)
                    if kind:
                        for a in range(2):
                            kp = key_pairs(kind, n + a * (2 if kind == "gqa" else 1))
                            for u in range(2):
                                hs = slice(64 * u, 64 * u + 64)
                                ins = nc.scalar.activation(kp[hs, u, :], bank2(bank + f % 4)[hs, a, :], ACT.Copy)
                    else:
                        ins = nc.scalar.activation(qk[:, n:n + 2, :], bank2(bank + f % 4), ACT.Copy)
                    ins.then_inc(blk_act, 1)

            def softmax(pairs, q0, beside=None):
                def copy_pT(q):
                    kind, t, j = pairs[q - q0]
                    if kind != "diff":
                        return
                    w = width(kind, t)
                    act.wait_ge(pT_ready, q + 1)
                    if q >= 2:
                        act.wait_ge(pv_done, q - 1)
                    nc.scalar.activation(ar(HY_PT, 2, CH)[:, q % 2, 0:w], ps[ring(kind) + q % 2][:, 0:w], ACT.Copy).then_inc(wT_copied, 1)

                for q, (kind, t, j) in enumerate(pairs, q0):
                    w = width(kind, t)
                    pa, pt = pbuf(kind)
                    c = cols(kind, j)
                    act.wait_ge(nb_ready, q + 1)
                    if q >= 2:
                        act.wait_ge(pT_ready, q - 1)
                    for u in range(2):
                        ins = nc.scalar.activation(ar(pa, 2, 2, T)[:, q % 2, u, 0:w], bank2((q - q0) % ring(kind))[:, u, 0:w], ACT.Exp,
                                                   bias=nb[:, t, c + u:c + u + 1],
                                                   scale=qsc[:, t, 0, c + u:c + u + 1] if kind == "gqa" else SCALE[kind],
                                                   accum_out=rs[:, t, c + u:c + u + 1])
                    ins.then_inc(exp_done, 1)
                    if q > q0:
                        copy_pT(q - 1)
                    if beside:
                        beside(q - q0)

            def ffn(name, base):
                stage = st[name]
                s0 = stage.s0
                r, h = ar(SQ_R, 2, CH), ar(SQ_H, 2, CH)

                def group(g, i=None):
                    up = s0 + 2 * g - 1 if g else s0
                    act.wait_ge(slab_used, at(i, 4, up + 1))
                    nc.scalar.activation(r[:, g % 2, :], ps[g % 2][:, :], ACT.Relu).then_inc(bank_free, 1)
                    act.wait_ge(hid_sq, at(i, 2, base + g + 1))
                    nc.scalar.activation(hh[:, g % 2, :, :].rearrange("p k t -> p (k t)"), h[:, g % 2, :], ACT.Copy).then_inc(hid_hi, 1)

                split(s0 + LOOKAHEAD)
                group(0)
                with act.Fori(0, (SQ_GROUPS - 2) // 2) as i:
                    for g in (1, 2):
                        split(s0 + 2 * g - 1 + LOOKAHEAD, i, 4)
                        split(s0 + 2 * g + LOOKAHEAD, i, 4)
                        group(g, i)
                g = SQ_GROUPS - 1
                splits(stage, 2 * g - 1, 2 * g)
                group(g)
                splits(stage, 2 * g, 2 * g + 1)

            def conv(name, l, base, cbase):
                stage = st[name]
                s0 = stage.s0
                cg, cv, sg, h = ar(CV_G, 2, 2, T), ar(CV_V, 2, 2, T), ar(CV_S, 2, CH), ar(CV_H, 2, CH)

                def mid(bank, dst, ft, i):
                    for a in range(2):
                        f = at(i, 8, ft + a)
                        ins = nc.scalar.activation(dst[:, a, :], bank2(bank)[:, a, :], ACT.Identity,
                                                   scale=cw[:, l, 1, bass.ds(f, 1)], bias=cw[:, l, 3, bass.ds(f, 1)])
                    ins.then_inc(conv_mid, 1)

                def group(g, i=None):
                    up = s0 + 3 * g - 1 if g else s0
                    if g:
                        split(up + LOOKAHEAD, i, 12)
                    act.wait_ge(slab_used, at(i, 12, up + 1))
                    mid(2 * (g % 2), cg[:, g % 2], 2 * g, i)
                    split(up + 1 + LOOKAHEAD if g else up + LOOKAHEAD, i, 12)
                    act.wait_ge(bank_free, at(i, 8, stage.f0 + 4 + 2 * g + 1))
                    nc.scalar.activation(sg[:, g % 2, :], cg[:, g % 2].rearrange("p a t -> p (a t)"), ACT.Silu).then_inc(gate_act, 1)
                    act.wait_ge(slab_used, at(i, 12, up + 2))
                    mid(2 * (g % 2) + 1, cv[:, g % 2], FT2 + 2 * g, i)
                    if g < CV_GROUPS - 1:
                        split(up + 2 + LOOKAHEAD if g else up + 1 + LOOKAHEAD, i, 12)
                    act.wait_ge(hid_sq, at(i, 4, base + g + 1))
                    nc.scalar.activation(hh[:, g % 2, :, :].rearrange("p k t -> p (k t)"), h[:, g % 2, :], ACT.Copy).then_inc(hid_hi, 1)

                group(0)
                n = (CV_GROUPS - 1) // 4
                with act.Fori(0, n) as i:
                    for g in range(1, 5):
                        group(g, i)
                for g in range(1 + 4 * n, CV_GROUPS):
                    group(g)
                splits(stage, 3 * CV_GROUPS - 2, 3 * CV_GROUPS)

            nc.scalar.dma_start(con[:, 0:C_ROPE_D], d["c_table"][:, 0:C_ROPE_D]).then_inc(con_loaded, 16)
            split(0)
            prep("hy_in")
            split(1), split(2)
            nc.scalar.dma_start(con[:, C_ROPE_D:C_ALL], d["c_table"][:, C_ROPE_D:C_ALL]).then_inc(rope_loaded, 16)

            g = st["hy_in"]
            nat = ar(A_NAT, TT, 3072)
            with act.Fori(0, 2) as i:
                for c in range(2):
                    split(g.s0 + 2 * c + LOOKAHEAD, i, 4)
                    split(g.s0 + 2 * c + 1 + LOOKAHEAD, i, 4)
                    copy_a(g, (c, 2 * c), lambda t: nat[:, t, bass.ds(i * 1024 + c * CH, CH)], i, 2)
            for c in (4, 5):
                splits(g, 2 * c, min(2 * c + 2, 11))
                copy_a(g, (c, 2 * c), lambda t: nat[:, t, c * CH:(c + 1) * CH])
            act.wait_ge(cw_T, 1)
            nc.scalar.activation(cw[:, :, :, :].rearrange("p l a j -> p (l a j)"), ps[7][:, 0:16 * FT2], ACT.Copy).then_inc(cw_done, 1)
            act.wait_ge(lam_sum, 1)
            nc.scalar.activation(lam[:, 0:2], lam[:, 2:4], ACT.Exp).then_inc(lam_exp, 1)
            blocks(0, HY_FILLS)
            splits(g, 11, 12)
            def diff_squares(t):
                act.wait_ge(pv_done, Q_HY + 6 * t + 4)
                nc.scalar.activation(ar(HY_SQ, TT, CH)[:, t, :], ps[out_bank("diff", t, 0)][:, :], ACT.Square).then_inc(sq_done, 1)

            softmax(HY_PAIRS, Q_HY, lambda k: diff_squares(0) if k == 6 else None)
            diff_squares(1)
            splits(st["hy_out"], 0, 1)
            prep("hy_out")
            splits(st["hy_out"], 1, 3)
            prep("ffn0")
            splits(st["hy_out"], 3, 4)
            ffn("ffn0", 0)

            ln_squares(0)

            prep("gla")
            splits(st["ffn0"], 2 * SQ_GROUPS - 1, 2 * SQ_GROUPS)
            g = st["gla"]
            splits(g, 0, 1)
            act.wait_ge(slab_used, g.s0 + 1)
            nc.scalar.activation(hlow, bank2(2)[:, 1, :], ACT.Copy).then_inc(bank_free, 1)

            def qk_copy(j):
                splits(g, 1 + j, 2 + j)
                act.wait_ge(slab_used, g.s0 + 2 + j)
                nc.scalar.activation(qk[:, 2 * j:2 * j + 2, :], bank2((3 + j) % 4 if j < 3 else 2), ACT.Copy,
                                     scale=P ** -0.5 if j < 2 else 1.0).then_inc(bank_free, 1)

            qk_copy(0)
            for t in range(TT):
                act.wait_ge(z_ready, t + 1)
                step(nc.scalar.activation(gTmp[:, t, :], ps[4 + t][:, :], ACT.Abs))
                step(nc.scalar.activation(gTmp[:, t, :], gTmp[:, t, :], ACT.Exp, scale=-1.0))
                nc.scalar.activation(gTmp[:, t, :], gTmp[:, t, :], ACT.Ln, bias=1.0).then_inc(ln_done, 1)
            for j in (1, 2):
                qk_copy(j)
            for t in range(TT):
                act.wait_ge(b_ready, t + 1)
                nc.scalar.activation(ar(GL_B, 4, T)[:, :, t * P:(t + 1) * P], bank4(6 + t), ACT.Copy).then_inc(b_copied, 1)
            qk_copy(3)

            def exps(lv):
                act.wait_ge(d_ready, lv)
                E = gE[:, lv % 2]
                if lv <= len(LEVELS):
                    nc.scalar.activation(E, E, ACT.Exp).then_inc(e_ready, 1)
                else:
                    nc.scalar.activation(E[:, :, 0:P], E[:, :, 0:P], ACT.Exp)
                    nc.scalar.activation(E[:, :, P:T], ar(GL_B, 4, T)[:, :, P:T], ACT.Exp).then_inc(e_ready, 1)

            exps(1)
            for k in range(8):
                splits(g, 5 + k, 6 + k)
                if k < 7:
                    exps(k + 2)
                if k % 2:
                    c = k // 2
                    copy_a(g, (c, 5 + 2 * c), lambda t: ar(A_NAT, TT, 2048)[:, t, c * CH:(c + 1) * CH])
            for t in range(TT):
                rv = ar(A_NAT, TT, 2048)[:, t, D:2 * D]
                act.wait_ge(bank_free, g.f0 + 4 + 5 + 8)
                nc.scalar.activation(rv, rv, ACT.Silu).then_inc(r_act, 1)
                if t == 0:
                    act.wait_ge(lv_ready, 17)
                    nc.scalar.activation(ar(GL_A01, 4, P), bank4(4), ACT.Copy).then_inc(a01_done, 1)
            for t in range(TT):
                act.wait_ge(go_ready, t + 1)
                for hp in range(2):
                    ins = nc.scalar.activation(xn[:, t, hp * CH:(hp + 1) * CH], ps[t + 2 * hp][:, :], ACT.Square)
                ins.then_inc(sq_done, 1)
            splits(st["gla_out"], 0, 1)
            prep("gla_out")
            splits(st["gla_out"], 1, 3)
            prep("ffn1")
            splits(st["gla_out"], 3, 4)
            rms_stats(mem, mem_loaded, lambda t: 16)
            ffn("ffn1", SQ_GROUPS)

            def splits_stats(stage, x):
                rms_stats(X, x_ready, x_at(x), (0,))
                splits(stage, 1, 3)
                rms_stats(X, x_ready, x_at(x), (1,))

            def keys(l, j):
                copy_b(st[f"mem{l}"], j, xk[:, 2 * j:2 * j + 2, :])

            def mem_values(l, c, base):
                copy_a(st[f"mem{l}"], (c, 4 + 2 * c), lambda t: ar(XA_V, TT, D)[:, t, c * CH:(c + 1) * CH], base=base)

            g = st["mem0"]
            prep("mem0")
            splits(st["ffn1"], 2 * SQ_GROUPS - 1, 2 * SQ_GROUPS)
            ln_squares(1)
            splits(g, 0, 1)
            rms_stats(X, x_ready, x_at("ffn1"))
            for j in range(4):
                keys(0, j)
                splits(g, j + 1, j + 2)
            splits(g, 5, 6)
            mem_values(0, 0, 0)
            splits(g, 6, 7)
            mem_values(0, 1, 0)

            prep("qkv", 4)
            splits(g, 7, 8)
            g = st["qkv"]
            nat = ar(A_NAT, TT, 1536)
            for c, (h0, nh) in enumerate(QK_HEADS):
                splits(g, 2 * c, 2 * c + 2)
                copy_a(g, (c, 2 * c), lambda t: nat[:, t, QKV_COLS[c]:QKV_COLS[c] + CH], base=4)
                for t in range(TT):
                    e = 2 * c + t
                    act.wait_ge(bank_free, g.f0 + 4 + e + 1)
                    if e >= 2:
                        act.wait_ge(var_ready, norm_count("qk_k", 0) + e - 2)
                    nc.scalar.activation(ar(QK_SQ, 2, CH)[:, e % 2, 0:64 * nh], nat[:, t, 64 * h0:64 * (h0 + nh)], ACT.Square).then_inc(sq_done, 1)
                if c == 1:
                    blocks(8, QK_FILLS, 0, (0,))
            blocks(8, QK_FILLS, 0, (2, 4))
            softmax(QK_PAIRS, Q_QK)
            splits(st["wo"], 0, 1)
            prep("wo")
            splits_stats(st["wo"], "wo")

            for l in range(2):
                prep(f"xq{l}")
                if l == 0:
                    splits(st["wo"], 3, 4)
                g = st[f"xq{l}"]
                for j in range(4):
                    splits(g, j, j + 1)
                    copy_b(g, j, qk[:, 2 * j:2 * j + 2, :])
                splits(st[f"xo{l}"], 0, 1)
                softmax(XA_PAIRS, Q_XA[l])
                prep(f"xo{l}")
                splits_stats(st[f"xo{l}"], f"xo{l}")
                prep(f"conv{l}")
                splits(st[f"xo{l}"], 3, 4)
                if l == 0:
                    rms_stats(mem, mem_loaded, lambda t: 32)
                conv(f"conv{l}", l, 2 * SQ_GROUPS + CV_GROUPS * l, 0)
                if l == 0:
                    g = st["mem1"]
                    prep("mem1")
                    splits(g, 0, 1)
                    rms_stats(X, x_ready, x_at("conv0"))
                    for j in range(4):
                        keys(1, j)
                        if j < 3:
                            splits(g, j + 1, j + 2)
                    for b in range(4):
                        act.wait_ge(pmix_ready, b + 1)
                        nc.scalar.activation(mix[:, 2 * b:2 * b + 2, :], bank2(4 + b), ACT.Copy).then_inc(pmix_done, 1)
                    splits(g, 4, 5)
                    rms_stats(X, x_ready, x_at("pool"))
                    splits(g, 5, 6)
                    mem_values(1, 0, 4)
                    splits(g, 6, 8)
                    mem_values(1, 1, 4)
            rms_stats(X, x_ready, x_at("conv1"))

        @block.vector
        def _(dve):
            order = [0]

            def step(ins):
                order[0] += 1
                ins.then_inc(dve_order, 1)

            def sync():
                dve.wait_ge(dve_order, order[0])

            def split(s, i=None, dstep=0):
                if s >= S:
                    return
                dve.wait_ge(wh_ready, at(i, dstep, s + 1))
                nc.vector.tensor_tensor(wl[:, s % RING, :], raw[:, s % RAWS, :], wh[:, s % RING, :].bitcast(F32), ALU.subtract)\
                    .then_inc(wl_ready, 1)

            def splits(stage, a, b):
                for j in range(a, b):
                    split(stage.s0 + j + LOOKAHEAD)

            def prep(name, base=0, ts=range(TT)):
                for t in ts:
                    for half in range(2):
                        dve.wait_ge(xh_done, 4 * PREPS.index(name) + 2 * t + half + 1)
                        part = slice(4 * half, 4 * half + 4), slice(t * P, (t + 1) * P)
                        nc.vector.tensor_tensor(xl[:, part[0], part[1]], bank4(base + t + 2 * half), xh[:, part[0], part[1]].bitcast(F32),
                                                ALU.subtract).then_inc(bank_free, 1)

            def gain(name):
                k = GK[name]
                dve.wait_ge(gain_loaded[k % 4], 16 * (k // 4 + 1))
                return gains[:, k % 4, :]

            def ln_part(c, t, wait_ct, base=0):
                cs = slice(c * CH, (c + 1) * CH)
                wait_ct(c, t)
                step(nc.vector.scalar_tensor_tensor(X[:, t, cs], X[:, t, cs], ALPHA, ps[base + 2 * c + t][:, :], ALU.mult, ALU.add))
                sync()
                step(nc.vector.bn_stats(bst[:, t, c, :], X[:, t, cs]))
                if c == 1:
                    sync()
                    nc.vector.bn_aggr(mv[:, t, :], bst[:, t, :, :].rearrange("p c s -> p (c s)")).then_inc(var_ready, 1)

            def ln_center(kind, l, t):
                gg = gain(f"ln_{kind}_g{l}")
                dve.wait_ge(var_ready, norm_count(f"ln_{kind}{l}", t))
                step(nc.vector.scalar_tensor_tensor(X[:, t, :], X[:, t, :], mv[:, t, 0:1], gg, ALU.subtract, ALU.mult))

            def ln_scale(kind, l, t):
                bb = gain(f"ln_{kind}_b{l}")
                sync()
                dve.wait_ge(rstd_ready, norm_count(f"ln_{kind}{l}", t))
                nc.vector.scalar_tensor_tensor(X[:, t, :], X[:, t, :], rstd[:, t, 0:1], bb, ALU.mult, ALU.add).then_inc(x_ready, 1)

            def ln_mix(l, stage):
                w = wait_a(stage)
                ln_part(0, 0, w), ln_part(1, 0, w)
                ln_center("mix", l, 0), ln_scale("mix", l, 0)
                splits(stage, 1, 2)
                ln_part(0, 1, w)
                splits(stage, 2, 3)
                ln_part(1, 1, w)
                ln_center("mix", l, 1), ln_scale("mix", l, 1)

            def ln_ffn(l, f):
                w = wait_ffn(st[f"ffn{l}"].s0 + 2 * SQ_GROUPS, f)
                gg, bb = gain(f"ln_ffn_g{l}"), gain(f"ln_ffn_b{l}")
                for t in range(TT):
                    for c in range(2):
                        cs = slice(c * CH, (c + 1) * CH)
                        w(c, t)
                        step(nc.vector.scalar_tensor_tensor(X[:, t, cs], X[:, t, cs], ALPHA, ps[4 + 2 * c + t][:, :], ALU.mult, ALU.add,
                                                            accum_out=lnsum[:, t, c:c + 1]))
                    sync()
                    nc.vector.tensor_scalar(nmean[:, t:t + 1], lnsum[:, t, 0:1], lnsum[:, t, 1:2], -1.0 / D, ALU.add, ALU.mult)\
                        .then_inc(mean_ready, 1)
                    dve.wait_ge(mean_ready, TT * l + t + 1)
                    step(nc.vector.scalar_tensor_tensor(xn[:, t, :], X[:, t, :], nmean[:, t:t + 1], gg, ALU.add, ALU.mult))
                    sync()
                    dve.wait_ge(rstd_ready, norm_count(f"ln_ffn{l}", t))
                    nc.vector.scalar_tensor_tensor(X[:, t, :], xn[:, t, :], rstd[:, t, 0:1], bb, ALU.mult, ALU.add).then_inc(x_ready, 1)

            def wait_a(stage):
                def w(c, t):
                    if t == 0:
                        dve.wait_ge(bank_ready, stage.r0 + c + 1)
                    else:
                        dve.wait_ge(slab_used, stage.s0 + 2 * c + 2)
                return w

            def wait_ffn(s_end, f):
                def w(c, t):
                    if t == 0:
                        dve.wait_ge(ff_first, f + 1)
                    else:
                        dve.wait_ge(slab_used, s_end)
                return w

            def residual(c, t, wait_ct, base=0):
                cs = slice(c * CH, (c + 1) * CH)
                wait_ct(c, t)
                ins = nc.vector.tensor_tensor(X[:, t, cs], ps[base + 2 * c + t][:, :], X[:, t, cs], ALU.add)
                if c == 1:
                    ins.then_inc(x_ready, 1)

            def residual_rms(stage, name, gain_name):
                w = wait_a(stage)
                residual(0, 0, w), residual(1, 0, w)
                splits(stage, 1, 2)
                rms_apply(name, gain_name, ts=(0,))
                residual(0, 1, w)
                splits(stage, 2, 3)
                residual(1, 1, w)
                rms_apply(name, gain_name, ts=(1,))

            def rms_apply(name, gain_name, src=X, dst=xn, done=xn_ready, ts=range(TT)):
                gg = gain(gain_name)
                for t in ts:
                    dve.wait_ge(rstd_ready, norm_count(name, t))
                    nc.vector.scalar_tensor_tensor(dst[:, t, :], src[:, t, :], rstd[:, t, 0:1], gg, ALU.mult, ALU.mult).then_inc(done, 1)

            def blocks(base, fills, bank=4, fs=None):
                for f in fs or range(1, len(fills), 2):
                    kind, n = fills[f]
                    dve.wait_ge(blk_T, base + f + 1)
                    if kind:
                        for a in range(2):
                            kp = key_pairs(kind, n + a * (2 if kind == "gqa" else 1))
                            for u in range(2):
                                hs = slice(64 * u, 64 * u + 64)
                                ins = nc.vector.tensor_copy(kp[hs, u, :], bank2(bank + f % 4)[hs, a, :])
                    else:
                        ins = nc.vector.tensor_copy(qk[:, n:n + 2, :], bank2(bank + f % 4))
                    ins.then_inc(blk_dve, 1)

            def softmax(pairs, q0, after):
                def post(q):
                    kind, t, j = pairs[q - q0]
                    w = width(kind, t)
                    if kind == "diff":
                        c = cols(kind, j)
                        p = ar(pbuf(kind)[0], 2, 2, T)[:, q % 2]
                        dve.wait_ge(exp_done, q + 1)
                        step(nc.vector.reciprocal(rr[:, t, c:c + 2], rs[:, t, c:c + 2]))
                        sync()
                        step(nc.vector.tensor_scalar(p[:, 1, 0:w], p[:, 1, 0:w], rr[:, t, c + 1:c + 2], lam[:, 2:3], ALU.mult, ALU.mult))
                        sync()
                        nc.vector.scalar_tensor_tensor(p[:, 0, 0:w], p[:, 0, 0:w], rr[:, t, c:c + 1], p[:, 1, 0:w],
                                                       ALU.mult, ALU.subtract).then_inc(diff_w, 1)
                    else:
                        dve.wait_ge(pT_ready, q + 1)
                        if q >= 2:
                            dve.wait_ge(pv_done, q - 1)
                        nc.vector.tensor_copy(ar(pbuf(kind)[1], 2, CH)[:, q % 2, 0:2 * w], ps[ring(kind) + q % 2][:, 0:2 * w]).then_inc(pT_copied, 1)

                for q, (kind, t, j) in enumerate(pairs, q0):
                    w = width(kind, t)
                    c = cols(kind, j)
                    dve.wait_ge(scores_ready, q + 1)
                    step(nc.vector.tensor_reduce(mx[:, t, c:c + 2], bank2((q - q0) % ring(kind))[:, :, 0:w], AX, ALU.max))
                    sync()
                    if kind == "gqa":
                        ins = nc.vector.tensor_tensor(nb[:, t, c:c + 2], mx[:, t, c:c + 2], qsc[:, t, 1, c:c + 2], ALU.mult)
                    else:
                        ins = nc.vector.tensor_scalar(nb[:, t, c:c + 2], mx[:, t, c:c + 2], -SCALE[kind], None, ALU.mult)
                    ins.then_inc(nb_ready, 1)
                    if q > q0:
                        post(q - 1)
                    if q >= q0 + 3:
                        after(q - q0 - 3)
                post(q0 + len(pairs) - 1)
                for k in range(len(pairs) - 3, len(pairs)):
                    after(k)

            def heads_out(dst, src, col, n, w, t):
                return nc.vector.tensor_tensor(dst.rearrange("p (h w) -> p h w", w=w), src.rearrange("p (h w) -> p h w", w=w),
                                               rr[:, t, col:col + n].unsqueeze(2).to_broadcast([P, n, w]), ALU.mult)

            def rope(x, tmp, g, half, cos, sin):
                xg = x.rearrange("p (g a h) -> p g a h", a=2, h=half)
                tg = tmp.rearrange("p (g a h) -> p g a h", a=2, h=half)
                for a in range(2):
                    tab = sin[:, a * half:(a + 1) * half].unsqueeze(1).to_broadcast([P, g, half])
                    step(nc.vector.tensor_tensor(tg[:, :, a, :], xg[:, :, 1 - a, :], tab, ALU.mult))
                sync()
                xw = x.rearrange("p (g w) -> p g w", w=2 * half)
                step(nc.vector.tensor_tensor(xw, xw, cos.unsqueeze(1).to_broadcast([P, g, 2 * half]), ALU.mult))
                sync()
                return nc.vector.tensor_tensor(x, x, tmp, ALU.add)

            def ffn(name, base):
                stage = st[name]
                s0 = stage.s0
                r, h = ar(SQ_R, 2, CH), ar(SQ_H, 2, CH)

                def group(g, i=None):
                    dve.wait_ge(bank_free, at(i, 2, stage.f0 + 4 + g + 1))
                    nc.vector.tensor_tensor(h[:, g % 2, :], r[:, g % 2, :], r[:, g % 2, :], ALU.mult).then_inc(hid_sq, 1)
                    dve.wait_ge(hid_hi, at(i, 2, base + g + 1))
                    nc.vector.tensor_tensor(hl[:, g % 2, :, :].rearrange("p k t -> p (k t)"), h[:, g % 2, :],
                                            hh[:, g % 2, :, :].rearrange("p k t -> p (k t)").bitcast(F32), ALU.subtract).then_inc(hid_lo, 1)

                split(s0 + LOOKAHEAD)
                group(0)
                with dve.Fori(0, (SQ_GROUPS - 2) // 2) as i:
                    for g in (1, 2):
                        split(s0 + 2 * g - 1 + LOOKAHEAD, i, 4)
                        split(s0 + 2 * g + LOOKAHEAD, i, 4)
                        group(g, i)
                g = SQ_GROUPS - 1
                splits(stage, 2 * g - 1, 2 * g)
                group(g)
                splits(stage, 2 * g, 2 * g + 1)

            def conv(name, l, base, cbase):
                stage = st[name]
                s0 = stage.s0
                cg, cv, sg, h = ar(CV_G, 2, 2, T), ar(CV_V, 2, 2, T), ar(CV_S, 2, CH), ar(CV_H, 2, CH)

                def taps(bank, dst, ft, e, i):
                    dve.wait_ge(conv_mid, at(i, 8, cbase + e + 1))
                    for a in range(2):
                        ins = nc.vector.scalar_tensor_tensor(dst[:, a, 1:T], bank2(bank)[:, a, 0:T - 1], cw[:, l, 0, bass.ds(at(i, 8, ft + a), 1)],
                                                             dst[:, a, 1:T], ALU.mult, ALU.add)
                    ins.then_inc(conv_tap, 1)
                    dve.wait_ge(conv_tap, at(i, 8, cbase + e + 1))
                    for a in range(2):
                        ins = nc.vector.scalar_tensor_tensor(dst[:, a, 0:T - 1], bank2(bank)[:, a, 1:T], cw[:, l, 2, bass.ds(at(i, 8, ft + a), 1)],
                                                             dst[:, a, 0:T - 1], ALU.mult, ALU.add)
                    ins.then_inc(bank_free, 1)

                def group(g, i=None):
                    up = s0 + 3 * g - 1 if g else s0
                    if g:
                        split(up + LOOKAHEAD, i, 12)
                    taps(2 * (g % 2), cg[:, g % 2], 2 * g, 2 * g, i)
                    split(up + 1 + LOOKAHEAD if g else up + LOOKAHEAD, i, 12)
                    taps(2 * (g % 2) + 1, cv[:, g % 2], FT2 + 2 * g, 2 * g + 1, i)
                    dve.wait_ge(gate_act, at(i, 4, CV_GROUPS * l + g + 1))
                    dve.wait_ge(bank_free, at(i, 8, stage.f0 + 4 + 2 * g + 2))
                    nc.vector.tensor_tensor(h[:, g % 2, :], sg[:, g % 2, :], cv[:, g % 2].rearrange("p a t -> p (a t)"), ALU.mult).then_inc(hid_sq, 1)
                    if g < CV_GROUPS - 1:
                        split(up + 2 + LOOKAHEAD if g else up + 1 + LOOKAHEAD, i, 12)
                    dve.wait_ge(hid_hi, at(i, 4, base + g + 1))
                    nc.vector.tensor_tensor(hl[:, g % 2, :, :].rearrange("p k t -> p (k t)"), h[:, g % 2, :],
                                            hh[:, g % 2, :, :].rearrange("p k t -> p (k t)").bitcast(F32), ALU.subtract).then_inc(hid_lo, 1)

                group(0)
                n = (CV_GROUPS - 1) // 4
                with dve.Fori(0, n) as i:
                    for g in range(1, 5):
                        group(g, i)
                for g in range(1 + 4 * n, CV_GROUPS):
                    group(g)
                splits(stage, 3 * CV_GROUPS - 2, 3 * CV_GROUPS - 1)

            split(0)
            prep("hy_in")
            split(1), split(2)
            g = st["hy_in"]
            nat = ar(A_NAT, TT, 3072)
            splits(g, 0, 4)
            dve.wait_ge(small_loaded, 16 * 6)
            step(nc.vector.tensor_copy(lvmask[:, :], arena[:, HY_SQ:HY_SQ + 8 * P]))
            pairs4 = lam_in[:, :, :].rearrange("p (a b) w -> p a b w", b=2)
            step(nc.vector.tensor_tensor(pairs4[:, :, 0, :], pairs4[:, :, 0, :], pairs4[:, :, 1, :], ALU.mult))
            sync()
            nc.vector.tensor_reduce(lam[:, 2:4], pairs4[:, :, 0, :], AX, ALU.add).then_inc(lam_sum, 1)
            dve.wait_ge(con_loaded, 16)
            nc.vector.tensor_copy(maskbf, cmask).then_inc(maskbf_ready, 1)
            nc.vector.tensor_copy(identbf, ident).then_inc(maskbf_ready, 1)
            dve.wait_ge(rope_loaded, 16)
            for k in range(2):
                gk = qkg[:, k, :]
                step(nc.vector.tensor_tensor(ropeg[:, 2 * k, :, :], rope_x[0], gk.unsqueeze(1).to_broadcast([P, TT, 64]), ALU.mult))
                for a in range(2):
                    def half(v, b):
                        return v.rearrange("p t (x b h) -> p (t x) b h", b=2, h=16)[:, :, b, :]
                    gs = gk.rearrange("p (x b h) -> p x b h", b=2, h=16)[:, :, 1 - a, :]
                    for t in range(TT):
                        so = ropeg[:, 2 * k + 1, t, :].rearrange("p (x b h) -> p x b h", b=2, h=16)[:, :, a, :]
                        si = rope_x[1][:, t, :].rearrange("p (x b h) -> p x b h", b=2, h=16)[:, :, a, :]
                        step(nc.vector.tensor_tensor(so, si, gs, ALU.mult))
            step(nc.vector.tensor_scalar(subln[:, :], subln[:, :], 1.0 - LAMBDA_INIT, None, ALU.mult))
            splits(g, 4, 6)
            dve.wait_ge(bank_free, g.f0 + 4 + 4)
            for t in range(TT):
                rope(nat[:, t, 0:1024], xn[:, 0, :], 16, 32, rope_d[0][:, t, :], rope_d[1][:, t, :]).then_inc(rope_done, 1)
                dve.wait_ge(rope_done, t + 1)
            splits(g, 6, 8)
            dve.wait_ge(bank_free, g.f0 + 4 + 8)
            for t in range(TT):
                rope(nat[:, t, 1024:2048], xn[:, 0, :], 8, 64, rope_m[0][:, t, :], rope_m[1][:, t, :]).then_inc(rope_done, 1)
                dve.wait_ge(rope_done, 2 + t + 1)
                splits(g, 8 + t, 9 + t)
            blocks(0, HY_FILLS)
            dve.wait_ge(lam_exp, 1)
            step(nc.vector.tensor_tensor(lam[:, 2:3], lam[:, 0:1], lam[:, 1:2], ALU.subtract))
            sync()
            step(nc.vector.tensor_scalar(lam[:, 2:3], lam[:, 2:3], LAMBDA_INIT, None, ALU.add))

            def moba_out(t):
                dve.wait_ge(pv_done, Q_HY + 6 * t + 6)
                step(nc.vector.reciprocal(rr[:, t, 8:12], rs[:, t, 8:12]))
                sync()
                return heads_out(xn[:, t, CH:D], ps[out_bank("moba", t, 0)][:, :], 8, 4, P, t)

            def diff_sums(t):
                dve.wait_ge(sq_done, t + 1)
                nc.vector.tensor_reduce(var[:, t, 0:4], ar(HY_SQ, TT, CH)[:, t, :].rearrange("p (h w) -> p h w", w=P), AX, ALU.add)\
                    .then_inc(var_ready, 1)

            def diff_out(t):
                dve.wait_ge(rstd_ready, t + 1)
                dst = xn[:, t, 0:CH].rearrange("p (h w) -> p h w", w=P)
                step(nc.vector.tensor_tensor(dst, bank4(out_bank("diff", t, 0)), rstd[:, t, 0:4].unsqueeze(2).to_broadcast([P, 4, P]), ALU.mult))
                sync()
                nc.vector.tensor_tensor(dst, dst, subln[:, :].unsqueeze(1).to_broadcast([P, 4, P]), ALU.mult).then_inc(xn_ready, 1)

            def beside_hy(k):
                if k == 4:
                    diff_sums(0)
                if k == 5:
                    moba_out(0).then_inc(moba_free, 1)
                if k == 7:
                    diff_out(0)

            softmax(HY_PAIRS, Q_HY, beside_hy)
            diff_sums(1)
            prep("hy_out", ts=(0,))
            moba_out(1)
            diff_out(1)
            dve.wait_ge(wl_ready, st["hy_out"].s0 + LOOKAHEAD)
            splits(st["hy_out"], 0, 1)
            prep("hy_out", ts=(1,))
            ln_mix(0, st["hy_out"])
            prep("ffn0")
            splits(st["hy_out"], 3, 4)
            ffn("ffn0", 0)
            ln_ffn(0, 0)

            prep("gla")
            splits(st["ffn0"], 2 * SQ_GROUPS - 1, 2 * SQ_GROUPS)
            g = st["gla"]
            splits(g, 0, 2)
            gg = ar(GL_G, TT, CH)
            for t in range(TT):
                dve.wait_ge(ln_done, t + 1)
                nc.vector.scalar_tensor_tensor(gg[:, t, :], ps[4 + t][:, :], 0.0, gTmp[:, t, :], ALU.min, ALU.subtract).then_inc(g_ready, 1)
            splits(g, 2, 5)
            att = ar(GL_ATT, TT, 4, P)
            dve.wait_ge(pool_init, 4)

            def decayed(lv):
                s = (LEVELS + [P])[lv - 1]
                z2, e2 = two(ar(GL_Z, 2, 4, T)[:, lv % 2], s), two(gE[:, lv % 2], s)
                q2, k2 = two(qk[:, 0:4, :], s), two(qk[:, 4:8, :], s)
                dve.wait_ge(e_ready, lv)
                if lv >= 3:
                    dve.wait_ge(lv_ready, 2 * (lv - 2) + 2)
                nc.vector.tensor_tensor(z2[:, :, 0, :], k2[:, :, 0, :], e2[:, :, 0, :], ALU.mult)
                nc.vector.tensor_tensor(z2[:, :, 1, :], q2[:, :, 1, :], e2[:, :, 1, :], ALU.mult).then_inc(zlev_ready, 1)

            def place(lv):
                m = lvmask[:, lv * P:(lv + 1) * P].unsqueeze(1).to_broadcast([P, 4, P])
                for t in range(TT):
                    dve.wait_ge(lv_ready, 2 * lv + t + 1)
                    if lv:
                        dve.wait_ge(lv_done, 2 * (lv - 1) + t + 1)
                    nc.vector.copy_predicated(att[:, t, :, :], m, bank4(4 + 2 * (lv % 2) + t)).then_inc(lv_done, 1)

            for k in range(8):
                splits(g, 5 + k, 6 + k)
                if k:
                    place(k - 1)
                decayed(k + 1)
            place(7)
            for t in range(TT):
                rv = ar(A_NAT, TT, 2048)[:, t, D:2 * D].rearrange("p (h w) -> p h w", w=T)
                dve.wait_ge(r_act, t + 1)
                nc.vector.tensor_tensor(rv, rv, glag[:, :].unsqueeze(1).to_broadcast([P, 4, T]), ALU.mult).then_inc(sr_done, 1)

            def gla_sums(t):
                dve.wait_ge(sq_done, TT + t + 1)
                nc.vector.tensor_reduce(var[:, t, 0:4], xn[:, t, :].rearrange("p (h w) -> p h w", w=T), AX, ALU.add).then_inc(var_ready, 1)

            gla_sums(0)
            for t in range(TT):
                dve.wait_ge(rstd_ready, norm_count("gla_heads", t))
                for hp in range(2):
                    step(nc.vector.tensor_tensor(xn[:, t, hp * CH:(hp + 1) * CH].rearrange("p (h w) -> p h w", w=T), bank2(t + 2 * hp),
                                                 rstd[:, t, 2 * hp:2 * hp + 2].unsqueeze(2).to_broadcast([P, 2, T]), ALU.mult))
                sync()
                dve.wait_ge(sr_done, t + 1)
                nc.vector.tensor_tensor(xn[:, t, :], xn[:, t, :], ar(A_NAT, TT, 2048)[:, t, D:2 * D], ALU.mult).then_inc(xn_ready, 1)
                if t == 0:
                    gla_sums(1)
                prep("gla_out", ts=(t,))
                if t == 0:
                    splits(st["gla_out"], 0, 1)
            ln_mix(1, st["gla_out"])
            prep("ffn1")
            splits(st["gla_out"], 3, 4)
            rms_apply("mem0", "mem_norm0", mem, mem, mem_normed)
            ffn("ffn1", SQ_GROUPS)

            g = st["mem0"]
            prep("mem0")
            splits(st["ffn1"], 2 * SQ_GROUPS - 1, 2 * SQ_GROUPS)
            ln_ffn(1, 1)
            splits(g, 0, 1)
            rms_apply("attn", "attn_norm")
            splits(g, 1, 7)

            prep("qkv", 4)
            splits(g, 7, 8)
            g = st["qkv"]
            nat = ar(A_NAT, TT, 1536)

            def head_sums(c, t):
                h0, nh = QK_HEADS[c]
                dve.wait_ge(sq_done, 2 * TT + 2 * c + t + 1)
                nc.vector.tensor_reduce(var[:, t, h0:h0 + nh], ar(QK_SQ, 2, CH)[:, t, 0:64 * nh].rearrange("p (h w) -> p h w", w=64),
                                        AX, ALU.add).then_inc(var_ready, 1)

            def axial(c, t):
                h0, nh = QK_HEADS[c]
                k = 2 if c == 0 else 0
                x = nat[:, t, 64 * h0:64 * (h0 + nh)]
                tmp = ar(QK_TMP, TT, CH)[:, t, 0:64 * nh]
                x5 = x.rearrange("p (h x b w) -> p h x b w", x=2, b=2, w=16)
                t5 = tmp.rearrange("p (h x b w) -> p h x b w", x=2, b=2, w=16)
                s5 = ropeg[:, k + 1, t, :].rearrange("p (x b w) -> p x b w", b=2, w=16)
                for b in range(2):
                    step(nc.vector.tensor_tensor(t5[:, :, :, b, :], x5[:, :, :, 1 - b, :],
                                                 s5[:, :, b, :].unsqueeze(1).to_broadcast([P, nh, 2, 16]), ALU.mult))
                sync()
                x3 = x.rearrange("p (h w) -> p h w", w=64)
                dve.wait_ge(sq_done, 2 * TT + 2 * c + t + 1)
                step(nc.vector.tensor_tensor(x3, x3, ropeg[:, k, t, :].unsqueeze(1).to_broadcast([P, nh, 64]), ALU.mult))
                sync()
                return x, tmp

            splits(g, 0, 2)
            for t in range(TT):
                head_sums(0, t)
            for t in range(TT):
                x3 = nat[:, t, D:D + 256].rearrange("p (h w) -> p h w", w=64)
                dve.wait_ge(rstd_ready, norm_count("qk_k", t))
                step(nc.vector.tensor_tensor(x3, x3, rstd[:, t, 16:20].unsqueeze(2).to_broadcast([P, 4, 64]), ALU.mult))
                sync()
                x, tmp = axial(0, t)
                kdt = kd[:, t, :].rearrange("p (g u w) -> p g u w", u=2, w=64)
                for u in range(2):
                    ins = nc.vector.tensor_tensor(kdt[:, :, u, :], x.rearrange("p (g w) -> p g w", w=64),
                                                  tmp.rearrange("p (g w) -> p g w", w=64), ALU.add)
                ins.then_inc(rope_done, 1)
            for c in (1, 2):
                if c == 1:
                    splits(g, 2, 4)
                for t in range(TT):
                    dve.wait_ge(bank_free, g.f0 + 4 + 2 * c + t + 1)
                    dve.wait_ge(rope_done, 4 + 2 * (c - 1) + t + 1)
                    x, tmp = axial(c, t)
                    nc.vector.tensor_tensor(x, x, tmp, ALU.add).then_inc(rope_done, 1)
                if c == 1:
                    blocks(8, QK_FILLS, 0, (1,))
                for t in range(TT):
                    head_sums(c, t)
            blocks(8, QK_FILLS, 0, (3, 5))
            for t in range(TT):
                dve.wait_ge(rstd_ready, norm_count("qk_q1", t))
                step(nc.vector.tensor_scalar(qsc[:, t, 0, :], rstd[:, t, 0:16], SCALE["gqa"], None, ALU.mult))
                step(nc.vector.tensor_scalar(qsc[:, t, 1, :], rstd[:, t, 0:16], -SCALE["gqa"], None, ALU.mult))
            sync()

            def qk_heads(t):
                dve.wait_ge(pv_done, Q_QK + 8 * t + 8)
                step(nc.vector.reciprocal(rr[:, t, 0:16], rs[:, t, 0:16]))
                sync()
                heads_out(xn[:, t, 0:CH], ps[out_bank("gqa", t, 0)][:, :], 0, 8, 64, t)
                heads_out(xn[:, t, CH:D], ps[out_bank("gqa", t, 4)][:, :], 8, 8, 64, t).then_inc(xn_ready, 1)

            softmax(QK_PAIRS, Q_QK, lambda k: qk_heads(0) if k == 7 else None)
            prep("wo", ts=(0,))
            dve.wait_ge(wl_ready, st["wo"].s0 + LOOKAHEAD)
            splits(st["wo"], 0, 1)
            qk_heads(1)
            prep("wo", ts=(1,))
            residual_rms(st["wo"], "xattn0", "xattn_norm0")

            for l in range(2):
                prep(f"xq{l}")
                if l == 0:
                    splits(st["wo"], 3, 4)
                splits(st[f"xq{l}"], 0, 4)

                def xa_after(k):
                    t, j = k // 2, k % 2
                    dve.wait_ge(pv_done, Q_XA[l] + k + 1)
                    step(nc.vector.reciprocal(rr[:, t, 2 * j:2 * j + 2], rs[:, t, 2 * j:2 * j + 2]))
                    sync()
                    ins = heads_out(xn[:, t, j * CH:(j + 1) * CH], ps[4 + 2 * t + j][:, :], 2 * j, 2, T, t)
                    if j == 1:
                        ins.then_inc(xn_ready, 1)

                softmax(XA_PAIRS, Q_XA[l], lambda k: None)
                for t in range(TT):
                    xa_after(2 * t), xa_after(2 * t + 1)
                    prep(f"xo{l}", ts=(t,))
                    if t == 0:
                        splits(st[f"xo{l}"], 0, 1)
                residual_rms(st[f"xo{l}"], f"ffn{l}", f"ffn_norm{l}")
                prep(f"conv{l}")
                splits(st[f"xo{l}"], 3, 4)
                if l == 0:
                    rms_apply("mem1", "mem_norm1", mem, mem, mem_normed)
                    dve.wait_ge(cw_done, 1)
                conv(f"conv{l}", l, 2 * SQ_GROUPS + CV_GROUPS * l, 2 * CV_GROUPS * l)
                w = wait_ffn(st[f"conv{l}"].s0 + 3 * CV_GROUPS, 2 + l)
                residual(0, 0, w, 4), residual(1, 0, w, 4)
                if l == 0:
                    prep("mem1")
                    splits(st["conv0"], 3 * CV_GROUPS - 1, 3 * CV_GROUPS)
                residual(0, 1, w, 4), residual(1, 1, w, 4)
                if l == 0:
                    g = st["mem1"]
                    splits(g, 0, 1)
                    rms_apply("pool", "pool_norm")
                    splits(g, 1, 4)
                    gs = gain("pool_scale")
                    for t in range(TT):
                        for c in range(2):
                            cs = slice(c * CH, (c + 1) * CH)
                            dve.wait_ge(py_ready, 2 * t + c + 1)
                            step(nc.vector.tensor_tensor(xn[:, t, cs], ps[2 * t + c][:, :], gs[:, cs], ALU.mult))
                            sync()
                            ins = nc.vector.tensor_tensor(X[:, t, cs], X[:, t, cs], xn[:, t, cs], ALU.add)
                        ins.then_inc(x_ready, 1)
                    splits(g, 4, 5)
                    rms_apply("xattn1", "xattn_norm1")
                    splits(g, 5, 8)
            rms_apply("final", "final_norm")

        @block.tensor
        def _(pe):
            def slab(s, i=None, step=0):
                pe.wait_ge(wl_ready, at(i, step, s + 1))

            def prep(src, w, v, base=0, warm=0, ts=range(TT)):
                for t in ts:
                    if t:
                        stay_warm(warm, 4)
                    pe.wait_ge(w, v(t))
                    for half in range(2):
                        for k in range(4):
                            c = (4 * half + k) * P
                            ins = nc.tensor.transpose(ps[base + t + 2 * half][:, k * P:(k + 1) * P], src[:, t, c:c + P], ident)
                        ins.then_inc(tr_done, 1)

            def stay_warm(n, bank):
                for _ in range(n):
                    nc.tensor.matmul(ps[bank][:, :], zero_bf[:, 0:P], zero_bf[:, :], start=True, stop=True)

            def chunk_a(stage, c, j, i=None, cstep=0, free=None, base=0, between=None):
                for half in range(2):
                    s = stage.s0 + j + half
                    slab(s, i, 2 * cstep)
                    wa, wb = slab_a(wh, s % RING), slab_a(wl, s % RING)
                    for t in range(TT):
                        if half == 0:
                            pe.wait_ge(bank_free, at(i, 2 * cstep, (stage.f0 if free is None else free) + 2 * c + t + 1))
                        if free is None and c == 0:
                            pe.wait_ge(bank_free, stage.f0 + (4 if half else 2 * t + 1))
                        o = ps[base + 2 * (c % 2) + t][:, :]
                        ts = slice(t * P, (t + 1) * P)
                        for k in range(4):
                            kt = 4 * half + k
                            nc.tensor.matmul(o, xh[:, kt, ts], wa[:, k, :], start=(kt == 0), stop=False)
                            nc.tensor.matmul(o, xh[:, kt, ts], wb[:, k, :], start=False, stop=False)
                            ins = nc.tensor.matmul(o, xl[:, kt, ts], wa[:, k, :], start=False, stop=(kt == KT - 1))
                        if half == 1 and t == 0:
                            ins.then_inc(bank_ready, 1)
                    ins.then_inc(slab_used, 1)
                    if between:
                        between(half)

            def project_out(stage, src, w, v):
                prep(src, w, v, ts=(0,))
                for t in range(TT):
                    ts = slice(t * P, (t + 1) * P)
                    for c in range(2):
                        for half in range(2):
                            if (t, c, half) == (0, 1, 1):
                                prep(src, w, v, ts=(1,))
                            s = stage.s0 + 2 * c + half
                            slab(s)
                            if c == 0:
                                pe.wait_ge(bank_free, stage.f0 + 2 * t + half + 1)
                            wa, wb = slab_a(wh, s % RING), slab_a(wl, s % RING)
                            o = ps[2 * c + t][:, :]
                            for k in range(4):
                                kt = 4 * half + k
                                nc.tensor.matmul(o, xh[:, kt, ts], wa[:, k, :], start=(kt == 0), stop=False)
                                nc.tensor.matmul(o, xh[:, kt, ts], wb[:, k, :], start=False, stop=False)
                                ins = nc.tensor.matmul(o, xl[:, kt, ts], wa[:, k, :], start=False, stop=(kt == KT - 1))
                            if t == 1:
                                ins.then_inc(slab_used, 1)
                        if t == 0:
                            ins.then_inc(bank_ready, 1)

            def slab_up(s, bank, tiles=(0, 1), i=None, step=0, stage=None):
                slab(s, i, step)
                wa, wb = slab_b(wh, s % RING), slab_b(wl, s % RING)
                if stage:
                    pe.wait_ge(bank_free, stage.f0 + 2)
                for a in tiles:
                    o = bank2(bank)[:, a, :]
                    cs = slice(a * P, (a + 1) * P)
                    for kt in range(KT):
                        if stage and a == tiles[0] and kt % 4 == 0:
                            pe.wait_ge(xh_done, 4 * stage.prep + 3 + kt // 4)
                        nc.tensor.matmul(o, wa[:, kt, cs], xh[:, kt, :], start=(kt == 0), stop=False)
                        nc.tensor.matmul(o, wb[:, kt, cs], xh[:, kt, :], start=False, stop=False)
                    for kt in range(KT):
                        if stage and a == tiles[0] and kt % 4 == 0:
                            pe.wait_ge(bank_free, stage.f0 + 3 + kt // 4)
                        ins = nc.tensor.matmul(o, wa[:, kt, cs], xl[:, kt, :], start=False, stop=(kt == KT - 1))
                ins.then_inc(slab_used, 1)

            def open_down():
                for b in range(4, 8):
                    nc.tensor.matmul(ps[b][:, :], zero_bf[:, 0:P], zero_bf[:, :], start=True, stop=False, skip_group_check=True)

            def down_part(s, par, t, c, last=False):
                wa, wb = slab_dn(wh, s % RING), slab_dn(wl, s % RING)
                o = ps[4 + 2 * c + t][:, :]
                ts, cs = slice(t * P, (t + 1) * P), slice(c * CH, (c + 1) * CH)
                for k in range(2):
                    nc.tensor.matmul(o, hh[:, par, k, ts], wa[:, k, cs], start=False, stop=False, skip_group_check=True)
                    nc.tensor.matmul(o, hh[:, par, k, ts], wb[:, k, cs], start=False, stop=False, skip_group_check=True)
                    ins = nc.tensor.matmul(o, hl[:, par, k, ts], wa[:, k, cs], start=False, stop=last and k == 1, skip_group_check=True)
                return ins

            def slab_down(s, par, i=None, step=0, last=False):
                slab(s, i, step)
                for t in range(TT):
                    for c in range(2):
                        ins = down_part(s, par, t, c, last)
                    if last and t == 0:
                        ins.then_inc(ff_first, 1)
                ins.then_inc(slab_used, 1)

            def ffn(name, base):
                stage = st[name]
                s0 = stage.s0

                def up(g, i=None):
                    if g:
                        pe.wait_ge(bank_free, at(i, 2, stage.f0 + g + 3))
                    slab_up(s0 + 2 * g - 1 if g else s0, g % 2, i=i, step=4, stage=None if g else stage)

                def down(g, i=None):
                    pe.wait_ge(hid_lo, at(i, 2, base + g + 1))
                    slab_down(s0 + 2 * g + 2, g % 2, i, 4)

                open_down()
                up(0)
                with pe.Fori(0, (SQ_GROUPS - 2) // 2) as i:
                    for g in (1, 2):
                        up(g, i)
                        down(g - 1, i)
                up(SQ_GROUPS - 1)
                g, s = SQ_GROUPS - 2, s0 + 2 * SQ_GROUPS - 2
                pe.wait_ge(hid_lo, base + g + 1)
                slab(s)
                for t, c in ((0, 0), (0, 1), (1, 0)):
                    down_part(s, g % 2, t, c)
                pe.wait_ge(hid_lo, base + g + 2)
                slab(s + 1)
                for c in range(2):
                    ins = down_part(s + 1, (g + 1) % 2, 0, c, last=True)
                ins.then_inc(ff_first, 1)
                down_part(s, g % 2, 1, 1).then_inc(slab_used, 1)
                for c in range(2):
                    ins = down_part(s + 1, (g + 1) % 2, 1, c, last=True)
                ins.then_inc(slab_used, 1)

            def conv(name, base):
                stage = st[name]
                s0 = stage.s0

                def up(g, i=None):
                    s = s0 + 3 * g - 1 if g else s0
                    for a in range(2):
                        pe.wait_ge(bank_free, at(i, 8, stage.f0 + 2 * g + a + 1))
                        slab_up(s + a, 2 * (g % 2) + a, i=i, step=12, stage=None if g or a else stage)

                def down(g, i=None, last=False):
                    pe.wait_ge(hid_lo, at(i, 4, base + g + 1))
                    slab_down(s0 + 3 * g + 4 if not last else s0 + 3 * g + 2, g % 2, i, 12, last)

                open_down()
                up(0)
                n = (CV_GROUPS - 1) // 4
                with pe.Fori(0, n) as i:
                    for g in range(1, 5):
                        up(g, i)
                        down(g - 1, i)
                for g in range(1 + 4 * n, CV_GROUPS):
                    up(g)
                    down(g - 1)
                down(CV_GROUPS - 1, last=True)

            def blocks(base, fills, src, w, v, warm=0, warm_at=0, bank=4, fs=None):
                ea = (base + 1) // 2
                fs = fs or range(len(fills))
                for f in fs:
                    if f == warm_at:
                        stay_warm(warm, 0 if bank else 7)
                    pe.wait_ge(w, v(f))
                    if base == 0 and f == 3:
                        pe.wait_ge(cw_done, 1)
                    if f >= 4:
                        pe.wait_ge(blk_act if f % 2 == 0 else blk_dve, ea + (f - 4) // 2 + 1)
                    for a in range(2):
                        for t in range(TT):
                            ins = nc.tensor.transpose(bank2(bank + f % 4)[:, a, t * P:(t + 1) * P], src(2 * f + a, t), ident)
                    ins.then_inc(blk_T, 1)
                if fs[-1] == len(fills) - 1:
                    pe.wait_ge(blk_act, ea + (len(fills) + 1) // 2)
                    pe.wait_ge(blk_dve, ea + len(fills) // 2)

            def scores(q, bank, kind, t, j):
                w = width(kind, t)
                if kind == "x" and t == 0:
                    pe.wait_ge(bank_free, st[f"xq{Q_XA.index(q - j)}"].f0 + 4 + 2 * (j + 1))
                ts = slice(t * P, (t + 1) * P)
                both = bank2(bank)[:, :, 0:w]
                if kind in ("diff", "moba"):
                    nc.tensor.matmul(bank2(bank)[:, :, ts], identbf, maskbf.unsqueeze(1).to_broadcast([P, 2, P]), start=True, stop=False, skip_group_check=True)
                if kind == "diff":
                    ins = nc.tensor.matmul(both, qk[:, j, ts], key_pairs(kind, j)[:, :, 0:w], start=False, stop=True, skip_group_check=True)
                elif kind == "gqa":
                    ins = nc.tensor.matmul(both, qk[:, j, ts], key_pairs(kind, j), start=True, stop=True)
                else:
                    for u in range(2):
                        o = bank2(bank)[:, u, 0:w]
                        if kind == "moba":
                            ins = nc.tensor.matmul(o, qk[:, 8 + 2 * j + u, ts], qk[:, 12 + 2 * j + u, 0:w], start=False, stop=True, skip_group_check=True)
                        else:
                            for k in range(2):
                                b = 2 * (2 * j + u) + k
                                ins = nc.tensor.matmul(o, qk[:, b, ts], xk[:, b, :], start=(k == 0), stop=(k == 1))
                ins.then_inc(scores_ready, 1)

            ndiff = [0]
            copied = [0, 0]

            def probs_T(q, kind, t, j):
                w = width(kind, t)
                p = ar(pbuf(kind)[0], 2, 2, T)[:, q % 2]
                if kind == "diff":
                    ndiff[0] += 1
                    pe.wait_ge(diff_w, ndiff[0])
                else:
                    pe.wait_ge(exp_done, q + 1)
                for u in range(1 if kind == "diff" else 2):
                    for k in range(w // P):
                        c = u * w + k * P
                        ins = nc.tensor.transpose(ps[ring(kind) + q % 2][:, c:c + P], p[:, u, k * P:(k + 1) * P], ident)
                ins.then_inc(pT_ready, 1)

            def values(q, kind, t, j, v):
                w = width(kind, t)
                pT = ar(pbuf(kind)[1], 2, CH)[:, q % 2]
                copied[kind == "diff"] += 1
                pe.wait_ge(wT_copied if kind == "diff" else pT_copied, copied[kind == "diff"])
                n = w // P
                if kind == "moba" and t:
                    pe.wait_ge(moba_free, 1)
                if kind == "gqa" and t and j >= 4:
                    pe.wait_ge(xn_ready, xn_count("qk_heads", 0))
                bank = ps[out_bank(kind, t, j)]
                for u in range(1 if kind == "diff" else 2):
                    h = j if kind == "diff" else 2 * j + u
                    if kind == "diff":
                        o, vc, vw = bank[:, j * P:(j + 1) * P], 2048 + j * P, P
                    elif kind == "moba":
                        o, vc, vw = bank[:, h * P:(h + 1) * P], 2560 + h * P, P
                    elif kind == "gqa":
                        o, vc, vw = bank[:, (h % 8) * 64:(h % 8 + 1) * 64], 1280 + (h // 4) * 64, 64
                    else:
                        o, vc, vw = bank[:, u * T:(u + 1) * T], h * T, T
                    for k in range(n):
                        c = u * w + k * P
                        ins = nc.tensor.matmul(o, pT[:, c:c + P], v[:, k, vc:vc + vw], start=(k == 0), stop=(k == n - 1))
                ins.then_inc(pv_done, 1)

            def attention(pairs, q0, v):
                n = ring(pairs[0][0])
                for k in range(n - 1):
                    scores(q0 + k, k, *pairs[k])
                for k, pair in enumerate(pairs):
                    a = k + n - 1
                    if a < len(pairs):
                        scores(q0 + a, a % n, *pairs[a])
                    probs_T(q0 + k, *pair)
                    if k:
                        values(q0 + k - 1, *pairs[k - 1], v)
                values(q0 + len(pairs) - 1, *pairs[-1], v)

            def x_at(name):
                return lambda t: x_count(name, t)

            def xn_at(name):
                return lambda t: xn_count(name, t)

            pe.wait_ge(pool_init, 2)
            stay_warm(14, 4)
            pe.wait_ge(con_loaded, 16)
            prep(X, x_loaded, lambda t: 16)
            stay_warm(14, 4)
            with pe.Fori(0, 3) as i:
                for c in range(2):
                    chunk_a(st["hy_in"], c, 2 * c, i, 2)
            pe.wait_ge(cw_loaded, 16 * 8)
            for l in range(2):
                for a in range(4):
                    c = (4 * l + a) * 2 * FT2
                    ins = nc.tensor.transpose(ps[7][:, c:c + 2 * FT2], cw_rows[:, l, a, :], con[0:2 * FT2, C_IDENT:C_IDENT + 2 * FT2])
            ins.then_inc(cw_T, 1)
            nat = ar(A_NAT, TT, 3072)
            pe.wait_ge(kz_ready, 1)
            pe.wait_ge(maskbf_ready, 2)
            pe.wait_ge(bank_free, st["hy_in"].f0 + 4 + 9)
            blocks(0, HY_FILLS, lambda b, t: nat[:, t, b * P:(b + 1) * P], rope_done, lambda f: 2 if f < 4 else 4, warm=6, warm_at=3)
            attention(HY_PAIRS, Q_HY, nat)
            project_out(st["hy_out"], xn, xn_ready, xn_at("hy_heads"))
            prep(X, x_ready, x_at("mix0"), warm=14)
            ffn("ffn0", 0)

            stay_warm(10, 0)
            prep(X, x_ready, x_at("ffn0"), warm=10)
            g = st["gla"]
            slab_up(g.s0, 2, tiles=(1,), stage=g)
            slab_up(g.s0 + 1, 3)
            pe.wait_ge(gla_small, 32)
            pe.wait_ge(pool_init, 3)
            pe.wait_ge(bank_free, g.f0 + 5)
            for t in range(TT):
                nc.tensor.matmul(ps[4 + t][:, :], one_row[:, :], bgate, start=True, stop=False)
                nc.tensor.matmul(ps[4 + t][:, :], hlow[:, t * P:(t + 1) * P], wup, start=False, stop=True).then_inc(z_ready, 1)
            slab_up(g.s0 + 2, 0)
            slab_up(g.s0 + 3, 1)
            for t in range(TT):
                pe.wait_ge(g_ready, t + 1)
                for h in range(4):
                    ins = nc.tensor.matmul(bank4(6 + t)[:, h, :], ar(GL_G, TT, CH)[:, t, h * P:(h + 1) * P], tri, start=True, stop=True)
                ins.then_inc(b_ready, 1)
            slab_up(g.s0 + 4, 2)

            def level(lv):
                z = ar(GL_Z, 2, 4, T)[:, lv % 2]
                if lv:
                    pe.wait_ge(zlev_ready, lv)
                if lv == 0:
                    pe.wait_ge(bank_free, g.f0 + 9)
                    pe.wait_ge(g_ready, TT)
                if lv == 1:
                    pe.wait_ge(b_copied, TT)
                for t in range(1 if lv == 8 else TT):
                    ts = slice(t * P, (t + 1) * P)
                    if lv >= 2:
                        pe.wait_ge(lv_done, 2 * (lv - 2) + t + 1)
                    for h in range(4):
                        o = bank4(4 + 2 * (lv % 2) + t)[:, h, :]
                        if lv == 0:
                            ins = nc.tensor.matmul(o, qk[:, 4 + h, ts], qk[:, h, ts], start=True, stop=True)
                        elif lv == 8:
                            ins = nc.tensor.matmul(o, z[:, h, 0:P], z[:, h, P:T], start=True, stop=True)
                        else:
                            ins = nc.tensor.matmul(o, z[:, h, ts], z[:, h, ts], start=True, stop=True)
                    ins.then_inc(lv_ready, 1)

            pe.wait_ge(bank_free, g.f0 + 8)
            for c in range(4):
                chunk_a(g, c, 5 + 2 * c, free=g.f0 + 5, between=lambda half: level(2 * c + half))
            level(8)
            vv = ar(A_NAT, TT, 2048)
            att = ar(GL_ATT, TT, 4, P)
            pe.wait_ge(bank_free, g.f0 + 4 + 5 + 8)
            pe.wait_ge(lv_done, 16)
            for t in range(TT):
                if t == 1:
                    pe.wait_ge(a01_done, 1)
                for h in range(4):
                    o = bank2(t + 2 * (h // 2))[:, h % 2, :]
                    if t == 1:
                        nc.tensor.matmul(o, ar(GL_A01, 4, P)[:, h, :], vv[:, 0, h * T:(h + 1) * T], start=True, stop=False)
                    ins = nc.tensor.matmul(o, att[:, t, h, :], vv[:, t, h * T:(h + 1) * T], start=(t == 0), stop=True)
                ins.then_inc(go_ready, 1)
            stay_warm(6, 4)
            project_out(st["gla_out"], xn, xn_ready, xn_at("gla_heads"))
            prep(X, x_ready, x_at("mix1"), warm=14)
            ffn("ffn1", SQ_GROUPS)

            def keys(l):
                prep(mem, mem_normed, lambda t: 2 * l + t + 1)
                g = st[f"mem{l}"]
                for j in range(4):
                    slab_up(g.s0 + j, j, stage=None if j else g)

            def mem_values(l, c, base):
                chunk_a(st[f"mem{l}"], c, 4 + 2 * c, free=st[f"mem{l}"].f0 + 4, base=base)

            keys(0)
            mem_values(0, 0, 0)
            prep(xn, xn_ready, xn_at("attn"), base=4)
            mem_values(0, 1, 0)

            pe.wait_ge(bank_free, st["mem0"].f0 + 10)
            stay_warm(6, 0)
            nat = ar(A_NAT, TT, 1536)

            def qk_blocks(fs, warm=0):
                blocks(8, QK_FILLS, lambda b, t: kd[:, t, b * P:(b + 1) * P] if b < 4 else nat[:, t, (b - 4) * P:(b - 3) * P],
                       rope_done, lambda f: 4 + 2 * (f // 2 + 1), warm=warm, warm_at=4, bank=0, fs=fs)

            for c in range(3):
                if c == 2:
                    qk_blocks(range(2))
                chunk_a(st["qkv"], c, 2 * c, base=4)
            pe.wait_ge(kz_ready, 2)
            qk_blocks(range(2, 6), warm=12)
            attention(QK_PAIRS, Q_QK, nat)
            project_out(st["wo"], xn, xn_ready, xn_at("qk_heads"))

            for l in range(2):
                g = st[f"xq{l}"]
                prep(xn, xn_ready, xn_at(f"xattn{l}"), warm=0 if l else 14)
                for j in range(4):
                    slab_up(g.s0 + j, j, stage=None if j else g)
                attention(XA_PAIRS, Q_XA[l], ar(XA_V, TT, D))
                project_out(st[f"xo{l}"], xn, xn_ready, xn_at(f"x_heads{l}"))
                prep(xn, xn_ready, xn_at(f"ffn{l}"), warm=14)
                conv(f"conv{l}", 2 * SQ_GROUPS + CV_GROUPS * l)
                if l == 0:
                    keys(1)
                    M = ar(PO_M, TT, 4 * T)
                    pe.wait_ge(pool_loaded, 32)
                    for t in range(TT):
                        pe.wait_ge(xn_ready, xn_count("pool", t))
                    for ct in range(KT):
                        for t in range(TT):
                            lo, hi = (0, P + POOL_REACH) if t == 0 else (P - POOL_REACH, T)
                            ins = nc.tensor.matmul(bank2(4 + ct // 2)[:, ct % 2, lo:hi], xn[:, t, ct * P:(ct + 1) * P],
                                                   M[:, t, (ct // 2) * T + lo:(ct // 2) * T + hi], start=(t == 0), stop=(t == 1),
                                                   skip_group_check=True)
                        if ct % 2:
                            ins.then_inc(pmix_ready, 1)
                    pe.wait_ge(bank_free, st["mem1"].f0 + 8)
                    pe.wait_ge(pmix_done, 4)
                    for t in range(TT):
                        for gr in range(4):
                            o = ps[2 * t + gr // 2][:, (gr % 2) * T:(gr % 2 + 1) * T]
                            for k in range(2):
                                ins = nc.tensor.matmul(o, mix[:, 2 * gr + k, t * P:(t + 1) * P], ar(PO_W, 8, T)[:, 2 * gr + k, :],
                                                       start=(k == 0), stop=(k == 1))
                            if gr % 2:
                                ins.then_inc(py_ready, 1)
                    for c in range(2):
                        mem_values(1, c, 4)


def constants():
    f = np.float32

    def rope(dim):
        inv = (f(1.0) / (f(10000.0) ** (np.arange(0, dim, 2, dtype=f) / f(dim)))).astype(f)
        ang = np.arange(T, dtype=f)[:, None] * inv[None, :]
        c, s = np.cos(ang), np.sin(ang)
        return np.concatenate([c, c], 1), np.concatenate([-s, s], 1)

    def axial():
        row = np.repeat(np.arange(T // 64, dtype=f), 64)
        col = np.tile(np.arange(64, dtype=f), T // 64)
        inv = f(10000.0) ** (-np.arange(16, dtype=f) / f(16))
        c, s = [], []
        for pos in (row, col):
            ang = pos[:, None] * inv
            c += [np.cos(ang), np.cos(ang)]
            s += [-np.sin(ang), np.sin(ang)]
        return np.concatenate(c, 1), np.concatenate(s, 1)

    def tiles(a):
        return a.reshape(TT, P, -1).transpose(1, 0, 2).reshape(P, -1)

    i = np.arange(P)
    parts = [np.eye(P), np.where(i[None, :] <= i[:, None], 0.0, NEG), np.where(i[:, None] <= i[None, :], 1.0 / 16, 0.0)]
    for c, s in (rope(64), rope(128), axial()):
        parts += [tiles(c), tiles(s)]
    table = np.concatenate([np.asarray(p, dtype=f) for p in parts], 1)
    j, q = i[:, None], i[None, :]
    levels = [j == q] + [(j // (2 * s) == q // (2 * s)) & (j % (2 * s) < s) & (q % (2 * s) >= s) for s in LEVELS]
    levels = np.concatenate(levels, 1).astype(f)
    pool = np.zeros((T, 4, T), f)
    for gr, w in enumerate(POOL_WINDOWS):
        for t in range(T):
            lo, hi = max(t - w // 2, 0), min(t + w - w // 2, T)
            pool[lo:hi, gr, t] = f(1.0) / f(hi - lo)
            pool[t, gr, t] -= f(1.0)
    return {"c_table": np.ascontiguousarray(table), "c_levels": np.ascontiguousarray(levels), "c_pool": pool.reshape(T, 4 * T)}


def kernel(**inputs):
    import concourse.bacc as bacc
    from concourse.bass_utils import run_bass_kernel_spmd

    a = {k: np.asarray(v) for k, v in inputs.items()}
    arrays = {"x": a["x"], "hy_w_in": a["hy_w_in"][0], "diff_lambda": a["diff_lambda"][0], "diff_subln": a["diff_subln"][0],
              "hy_w_out": a["hy_w_out"][0], "gla_w_in": a["gla_w_in"][0], "gla_w_gate_up": a["gla_w_gate_up"][0],
              "gla_b_gate": a["gla_b_gate"][0], "gla_norm": a["gla_norm"][0], "gla_w_out": a["gla_w_out"][0],
              "ffn_w1": a["ffn_w1"], "ffn_w2": a["ffn_w2"], "mem": a["mem_2"], "attn_norm": a["attn_norm_2"][0],
              "attn_w_qkv": a["attn_w_qkv_2"][0], "attn_q_gain": a["attn_q_gain_2"][0], "attn_k_gain": a["attn_k_gain_2"][0],
              "attn_w_o": a["attn_w_o_2"][0], "pool_norm": a["pool_norm_2"][0], "pool_w": a["pool_w_2"][0],
              "pool_scale": a["pool_scale_2"][0], "xattn_w_q": a["xattn_w_q_2"], "xattn_w_kv": a["xattn_w_kv_2"],
              "xattn_w_o": a["xattn_w_o_2"], "ffn_w_up": a["ffn_w_up_2"], "ffn_conv_w": a["ffn_conv_w_2"],
              "ffn_conv_b": a["ffn_conv_b_2"], "ffn_w_down": a["ffn_w_down_2"], "final_norm": a["final_norm_2"]}
    for l in range(DEPTH):
        for kind in ("mix", "ffn"):
            arrays[f"ln_{kind}_g{l}"] = a[f"ln_{kind}_g"][l]
            arrays[f"ln_{kind}_b{l}"] = a[f"ln_{kind}_b"][l]
        arrays[f"mem_norm{l}"] = a["mem_norm_2"][l]
        arrays[f"xattn_norm{l}"] = a["xattn_norm_2"][l]
        arrays[f"ffn_norm{l}"] = a["ffn_norm_2"][l]
    arrays.update(constants())
    arrays = {f"in_{k}": np.ascontiguousarray(v) for k, v in arrays.items()}
    nc = bacc.Bacc("TRN2", target_bir_lowering=False, num_devices=1)
    d = {k[3:]: nc.dram_tensor(k, v.shape, mybir.dt.from_np(v.dtype), kind="ExternalInput").ap() for k, v in arrays.items()}
    d["out"] = nc.dram_tensor("out", (1, T, D), F32, kind="ExternalOutput").ap()
    build(nc, d)
    r = run_bass_kernel_spmd(nc, [arrays], core_ids=[0])
    return r.results[0]["out"]
```
